# Optimizing a Trainium2 kernel written in Bass

```python
import math
import jax, jax.numpy as jnp
from jax import lax
import numpy as np
import jax
import jax.numpy as jnp

D_MODEL = 1024
BATCH = 1
SEQ = 1024
DEPTH = 2

GLA_HEADS = 4
GLA_DK = 64
GLA_DV = 128
GLA_GATE_RANK = 16
GLA_TAU = 16.0
GLA_CHUNK = 64
MLA_HEADS = 4
MLA_NOPE = 128
MLA_ROPE = 64
MLA_V = 128
MLA_Q_RANK = 256
MLA_KV_RANK = 128
ROPE_THETA = 10000.0
ATTN_BLOCK = 128
D_GLA = GLA_HEADS * GLA_DV
D_MLA = MLA_HEADS * MLA_V
D_MIX = D_GLA + D_MLA
D_FF = 4 * D_MODEL
N_MOD = 6
RMS_EPS = 1e-6
IN_SIZES = (GLA_HEADS * GLA_DK, GLA_HEADS * GLA_DK, D_GLA, D_GLA, GLA_GATE_RANK,
            MLA_Q_RANK, MLA_KV_RANK, MLA_ROPE)
D_IN = sum(IN_SIZES)


def split_cols(t, sizes):
    idx = []
    acc = 0
    for s in sizes[:-1]:
        acc += s
        idx.append(acc)
    return jnp.split(t, idx, axis=-1)

def rms_norm(x, gain=None):
    xf = x.astype(jnp.float32)
    y = xf * lax.rsqrt(jnp.mean(xf * xf, axis=-1, keepdims=True) + RMS_EPS)
    if gain is not None:
        y = y * gain.astype(jnp.float32)
    return y.astype(x.dtype)

def rope_tables(positions):
    inv_freq = ROPE_THETA ** (-jnp.arange(0, MLA_ROPE, 2, dtype=jnp.float32) / MLA_ROPE)
    ang = positions.astype(jnp.float32)[..., None] * inv_freq
    return jnp.cos(ang), jnp.sin(ang)

def apply_rope(t, cos, sin):
    t = t.astype(jnp.float32)
    half = t.shape[-1] // 2
    t1, t2 = t[..., :half], t[..., half:]
    return jnp.concatenate([t1 * cos - t2 * sin, t2 * cos + t1 * sin], axis=-1)

def gla_chunked(q, k, v, log_a):
    B, S, H, dk = q.shape
    dv = v.shape[-1]
    C = GLA_CHUNK
    N = S // C

    def to_chunks(t):
        return t.reshape(B, N, C, H, t.shape[-1]).transpose(1, 0, 3, 2, 4)

    causal = jnp.tril(jnp.ones((C, C), dtype=bool))

    def step(state, inp):
        qc, kc, vc, gc = inp
        b = jnp.cumsum(gc, axis=2)
        o_inter = jnp.einsum('bhcd,bhde->bhce', qc * jnp.exp(b), state)
        diff = b[:, :, :, None, :] - b[:, :, None, :, :]
        decay = jnp.exp(jnp.where(causal[:, :, None], diff, -jnp.inf))
        attn = jnp.sum(qc[:, :, :, None, :] * kc[:, :, None, :, :] * decay, axis=-1)
        o_intra = jnp.einsum('bhij,bhje->bhie', attn, vc)
        b_last = b[:, :, -1:, :]
        k_dec = kc * jnp.exp(b_last - b)
        state = jnp.exp(b_last[:, :, 0, :])[..., None] * state + jnp.einsum('bhcd,bhce->bhde', k_dec, vc)
        return state, o_inter + o_intra

    state0 = jnp.zeros((B, H, dk, dv), dtype=jnp.float32)
    _, o = lax.scan(step, state0, (to_chunks(q), to_chunks(k), to_chunks(v), to_chunks(log_a)))
    return o.transpose(1, 0, 3, 2, 4).reshape(B, S, H, dv)

def mla_attention(q_nope, q_pe, k_nope, k_pe, v):
    B, S, H, _ = q_nope.shape
    NB = S // ATTN_BLOCK
    scale = (MLA_NOPE + MLA_ROPE) ** -0.5
    key_idx = jnp.arange(S)

    def blocks(t):
        return t.reshape(B, NB, ATTN_BLOCK, *t.shape[2:]).swapaxes(0, 1)

    def one_block(args):
        qn, qp, blk = args
        s = (jnp.einsum('bqhd,bkhd->bhqk', qn, k_nope).astype(jnp.float32)
             + jnp.einsum('bqhr,bkr->bhqk', qp, k_pe).astype(jnp.float32)) * scale
        q_idx = blk * ATTN_BLOCK + jnp.arange(ATTN_BLOCK)
        mask = key_idx[None, :] <= q_idx[:, None]
        p = jax.nn.softmax(jnp.where(mask, s, -jnp.inf), axis=-1)
        return jnp.einsum('bhqk,bkhe->bqhe', p.astype(v.dtype), v)

    out = lax.map(one_block, (blocks(q_nope), blocks(q_pe), jnp.arange(NB)))
    return out.swapaxes(0, 1).reshape(B, S, H, v.shape[-1])

def hybrid_mixer(h, cos, sin, w_in, w_gate_up, b_gate, gla_out_norm, q_a_norm, w_q_up,
                 kv_a_norm, w_kv_up, q_norm_nope, k_norm_nope, q_norm_rope, k_norm_rope, w_out):
    B, S, _ = h.shape
    proj = h @ w_in
    g_q, g_k, g_v, g_o, g_a, m_q, m_kv, m_kpe = split_cols(proj, IN_SIZES)

    q = g_q.reshape(B, S, GLA_HEADS, GLA_DK).astype(jnp.float32) * (GLA_DK ** -0.5)
    k = g_k.reshape(B, S, GLA_HEADS, GLA_DK).astype(jnp.float32)
    v = g_v.reshape(B, S, GLA_HEADS, GLA_DV).astype(jnp.float32)
    log_a = jax.nn.log_sigmoid((g_a @ w_gate_up + b_gate).astype(jnp.float32)) / GLA_TAU
    log_a = log_a.reshape(B, S, GLA_HEADS, GLA_DK)
    o = gla_chunked(q, k, v, log_a)
    o = rms_norm(o, gla_out_norm) * jax.nn.silu(g_o.reshape(B, S, GLA_HEADS, GLA_DV).astype(jnp.float32))
    gla_out = o.reshape(B, S, D_GLA).astype(h.dtype)

    qh = (rms_norm(m_q, q_a_norm) @ w_q_up).reshape(B, S, MLA_HEADS, MLA_NOPE + MLA_ROPE)
    q_nope, q_pe = qh[..., :MLA_NOPE], qh[..., MLA_NOPE:]
    q_nope = rms_norm(q_nope, q_norm_nope)
    q_pe = apply_rope(rms_norm(q_pe, q_norm_rope), cos[:, :, None, :], sin[:, :, None, :])
    kv = (rms_norm(m_kv, kv_a_norm) @ w_kv_up).reshape(B, S, MLA_HEADS, MLA_NOPE + MLA_V)
    k_nope, mv = kv[..., :MLA_NOPE], kv[..., MLA_NOPE:]
    k_nope = rms_norm(k_nope, k_norm_nope)
    k_pe = apply_rope(rms_norm(m_kpe, k_norm_rope), cos, sin)
    mla_out = mla_attention(q_nope, q_pe, k_nope, k_pe, mv).reshape(B, S, D_MLA)

    mixed = jnp.concatenate([gla_out, mla_out.astype(gla_out.dtype)], axis=-1)
    return mixed @ w_out

def first_inputs(seed: int = 0) -> dict:
    key = jax.random.key(seed)
    ks = jax.random.split(key, 24)
    f32 = jnp.float32

    def w(k, shape, fan_in):
        return jax.random.normal(k, shape, f32) * (fan_in ** -0.5)

    def gain(k, shape):
        return 1.0 + 0.02 * jax.random.normal(k, shape, f32)

    x = jax.random.normal(ks[0], (BATCH, SEQ, D_MODEL), f32)
    c = jax.random.normal(ks[1], (BATCH, D_MODEL), f32)
    offsets = jax.random.randint(ks[2], (BATCH, 1), 0, 1024, dtype=jnp.int32)
    positions = (offsets + jnp.arange(SEQ, dtype=jnp.int32)[None, :]).astype(jnp.int32)
    return {
        'x': x,
        'c': c,
        'positions': positions,
        'w_ada': w(ks[3], (DEPTH, D_MODEL, N_MOD * D_MODEL), D_MODEL),
        'b_ada': 0.02 * jax.random.normal(ks[4], (DEPTH, N_MOD * D_MODEL), f32),
        'w_in': w(ks[5], (DEPTH, D_MODEL, D_IN), D_MODEL),
        'w_gate_up': w(ks[6], (DEPTH, GLA_GATE_RANK, GLA_HEADS * GLA_DK), GLA_GATE_RANK),
        'b_gate': 0.1 * jax.random.normal(ks[7], (DEPTH, GLA_HEADS * GLA_DK), f32),
        'gla_out_norm': gain(ks[8], (DEPTH, GLA_DV)),
        'q_a_norm': gain(ks[9], (DEPTH, MLA_Q_RANK)),
        'w_q_up': w(ks[10], (DEPTH, MLA_Q_RANK, MLA_HEADS * (MLA_NOPE + MLA_ROPE)), MLA_Q_RANK),
        'kv_a_norm': gain(ks[11], (DEPTH, MLA_KV_RANK)),
        'w_kv_up': w(ks[12], (DEPTH, MLA_KV_RANK, MLA_HEADS * (MLA_NOPE + MLA_V)), MLA_KV_RANK),
        'q_norm_nope': gain(ks[13], (DEPTH, MLA_NOPE)),
        'k_norm_nope': gain(ks[14], (DEPTH, MLA_NOPE)),
        'q_norm_rope': gain(ks[15], (DEPTH, MLA_ROPE)),
        'k_norm_rope': gain(ks[16], (DEPTH, MLA_ROPE)),
        'w_out': w(ks[17], (DEPTH, D_MIX, D_MODEL), D_MIX),
        'w_mlp_up': w(ks[18], (DEPTH, D_MODEL, D_FF), D_MODEL),
        'w_mlp_down': w(ks[19], (DEPTH, D_FF, D_MODEL), D_FF),
    }

def first_block(x, c, positions, w_ada, b_ada, w_in, w_gate_up, b_gate, gla_out_norm, q_a_norm,
              w_q_up, kv_a_norm, w_kv_up, q_norm_nope, k_norm_nope, q_norm_rope, k_norm_rope,
              w_out, w_mlp_up, w_mlp_down):
    cos, sin = rope_tables(positions)
    cond = jax.nn.silu(c)
    for l in range(DEPTH):
        mod = (cond @ w_ada[l] + b_ada[l])[:, None, :]
        shift_a, scale_a, gate_a, shift_f, scale_f, gate_f = jnp.split(mod, N_MOD, axis=-1)
        h = rms_norm(x) * (1.0 + scale_a) + shift_a
        mix = hybrid_mixer(h, cos, sin, w_in[l], w_gate_up[l], b_gate[l], gla_out_norm[l],
                           q_a_norm[l], w_q_up[l], kv_a_norm[l], w_kv_up[l], q_norm_nope[l],
                           k_norm_nope[l], q_norm_rope[l], k_norm_rope[l], w_out[l])
        x = x + gate_a * mix
        h = rms_norm(x) * (1.0 + scale_f) + shift_f
        x = x + gate_f * (jnp.square(jax.nn.relu(h @ w_mlp_up[l])) @ w_mlp_down[l])
    return x


DEPTH_2 = 1

CHUNK = 64
EPS = 1e-6
D_MIX_2 = D_MODEL
HEAD_DIM = 64

A_WIDTH = 3 * D_MIX_2 // 8
A_HEADS = A_WIDTH // HEAD_DIM
A_BLOCK = 128

B_WIDTH = 3 * D_MIX_2 // 8
B_HEADS = B_WIDTH // HEAD_DIM
CONV_WIDTH = 4
LRU_C = 8.0

C_WIDTH = D_MIX_2 - A_WIDTH - B_WIDTH
C_GROUP_DIM = 16
C_GROUPS = C_WIDTH // C_GROUP_DIM
C_STATE = 64

OFF_A_U = 0
OFF_A_V = OFF_A_U + A_WIDTH
OFF_B_X = OFF_A_V + A_WIDTH
OFF_B_G = OFF_B_X + B_WIDTH
OFF_C_X = OFF_B_G + B_WIDTH
IN_COLS = OFF_C_X + C_WIDTH

N_GROUPS = 4
EXPERTS_PER_GROUP = 4
N_EXPERTS = N_GROUPS * EXPERTS_PER_GROUP
TOP_K = 2
D_EXPERT = D_MODEL // 2
MOE_BLOCK = 256


def rms_norm_2(x, g):
    xf = x.astype(jnp.float32)
    y = xf * lax.rsqrt(jnp.mean(xf * xf, axis=-1, keepdims=True) + EPS)
    return (y * g.astype(jnp.float32)).astype(x.dtype)

def _linear_combine(left, right):
    a_l, b_l = left
    a_r, b_r = right
    return a_r * a_l, a_r * b_l + b_r

def linear_recurrence(a, b):
    _, h = lax.associative_scan(_linear_combine, (a, b), axis=1)
    return h

def causal_depthwise_conv(x, w, b):
    k_w = w.shape[0]
    seq = x.shape[1]
    xp = jnp.pad(x, ((0, 0), (k_w - 1, 0), (0, 0)))
    y = b + w[k_w - 1] * x
    for k in range(k_w - 1):
        y = y + w[k] * xp[:, k:k + seq]
    return y

def mixer_spatial_gating(u_raw, v_raw, v_norm_g, w_s, b_s):
    bsz, seq, _ = u_raw.shape
    u = jax.nn.gelu(u_raw)
    v = rms_norm_2(jax.nn.gelu(v_raw), v_norm_g)
    v = v.reshape(bsz, seq // A_BLOCK, A_BLOCK, A_HEADS, HEAD_DIM)
    chunk_id = jnp.arange(A_BLOCK) // CHUNK
    mask = chunk_id[None, :] <= chunk_id[:, None]
    w = jnp.where(mask[None], w_s, 0.0)
    sv = jnp.einsum("hij,bnjhd->bnihd", w, v) + b_s.T[:, :, None]
    return u * sv.reshape(bsz, seq, A_WIDTH)

def mixer_rglru(x_raw, g_raw, conv_w, conv_b, rg_w, rg_b, ig_w, ig_b, lam):
    bsz, seq, width = x_raw.shape
    xc = causal_depthwise_conv(x_raw, conv_w, conv_b)
    xh = xc.reshape(bsz, seq, B_HEADS, HEAD_DIM)
    r = jax.nn.sigmoid(jnp.einsum("bshi,hij->bshj", xh, rg_w).reshape(bsz, seq, width) + rg_b)
    i = jax.nn.sigmoid(jnp.einsum("bshi,hij->bshj", xh, ig_w).reshape(bsz, seq, width) + ig_b)
    log_a = -LRU_C * r.astype(jnp.float32) * jax.nn.softplus(-lam.astype(jnp.float32))
    a = jnp.exp(log_a)
    b = jnp.sqrt(-jnp.expm1(2.0 * log_a)) * (i * xc).astype(jnp.float32)
    h = linear_recurrence(a, b)
    return (h * jax.nn.gelu(g_raw.astype(jnp.float32))).astype(x_raw.dtype)

def mixer_s5(x_raw, a_re, a_im, log_dt, b_re, b_im, c_re, c_im, d, glu_w, glu_b):
    bsz, seq, width = x_raw.shape
    f32 = jnp.float32
    xf = x_raw.astype(f32)
    lam = lax.complex(a_re.astype(f32), a_im.astype(f32))
    dt = jnp.exp(log_dt.astype(f32))[:, None]
    lam_bar = jnp.exp(lam * dt)
    b_bar = ((lam_bar - 1.0) / lam)[:, :, None] * lax.complex(b_re.astype(f32), b_im.astype(f32))
    c_mat = lax.complex(c_re.astype(f32), c_im.astype(f32))
    xg = xf.reshape(bsz, seq, C_GROUPS, C_GROUP_DIM)
    bu = jnp.einsum("gpc,bsgc->bsgp", b_bar, xg.astype(jnp.complex64))
    state = linear_recurrence(jnp.broadcast_to(lam_bar, bu.shape), bu)
    y = jnp.einsum("gcp,bsgp->bsgc", c_mat, state).real.reshape(bsz, seq, width) + d.astype(f32) * xf
    y = jax.nn.gelu(y)
    y = y * jax.nn.sigmoid(y @ glu_w.astype(f32) + glu_b.astype(f32))
    return y.astype(x_raw.dtype)

def hybrid_mixer_2(h, norm_g, w_in, a_v_norm_g, a_spatial_w, a_spatial_b,
                 b_conv_w, b_conv_b, b_rg_w, b_rg_b, b_ig_w, b_ig_b, b_lambda,
                 c_a_re, c_a_im, c_log_dt, c_b_re, c_b_im, c_c_re, c_c_im, c_d, c_glu_w, c_glu_b,
                 mix_out_norm_g, w_out):
    z = rms_norm_2(h, norm_g) @ w_in
    y_a = mixer_spatial_gating(z[..., OFF_A_U:OFF_A_V], z[..., OFF_A_V:OFF_B_X],
                               a_v_norm_g, a_spatial_w, a_spatial_b)
    y_b = mixer_rglru(z[..., OFF_B_X:OFF_B_G], z[..., OFF_B_G:OFF_C_X],
                      b_conv_w, b_conv_b, b_rg_w, b_rg_b, b_ig_w, b_ig_b, b_lambda)
    y_c = mixer_s5(z[..., OFF_C_X:IN_COLS], c_a_re, c_a_im, c_log_dt, c_b_re, c_b_im,
                   c_c_re, c_c_im, c_d, c_glu_w, c_glu_b)
    y = jnp.concatenate([
        rms_norm_2(y_a, mix_out_norm_g[:A_WIDTH]),
        rms_norm_2(y_b, mix_out_norm_g[A_WIDTH:A_WIDTH + B_WIDTH]),
        rms_norm_2(y_c, mix_out_norm_g[A_WIDTH + B_WIDTH:]),
    ], axis=-1)
    return y @ w_out

def hierarchical_moe(hn, rg_w, rg_b, re_w, re_b, w_gate, w_up, w_down):
    bsz, seq, dm = hn.shape
    n_tok = bsz * seq
    xt = hn.reshape(n_tok, dm)
    f32 = jnp.float32
    g_logits = (xt @ rg_w).astype(f32) + rg_b.astype(f32)
    g_prob = jax.nn.softmax(g_logits, axis=-1)
    g_sel = jnp.argmax(g_logits, axis=-1).astype(jnp.int32)
    g_w = jnp.take_along_axis(g_prob, g_sel[:, None], axis=-1)[:, 0]
    e_all = jnp.einsum("td,gde->tge", xt, re_w).astype(f32) + re_b.astype(f32)
    e_logits = jnp.take_along_axis(e_all, g_sel[:, None, None], axis=1)[:, 0]
    e_top, e_idx = lax.top_k(e_logits, TOP_K)
    e_w = jax.nn.softmax(e_top, axis=-1)
    expert_id = g_sel[:, None] * EXPERTS_PER_GROUP + e_idx.astype(jnp.int32)
    gate = g_w[:, None] * e_w
    n_assign = n_tok * TOP_K
    flat_e = expert_id.reshape(n_assign)
    flat_tok = jnp.arange(n_assign, dtype=jnp.int32) // TOP_K
    flat_gate = gate.reshape(n_assign)
    order = jnp.argsort(flat_e)
    sorted_e = flat_e[order]
    counts = jnp.bincount(flat_e, length=N_EXPERTS)
    start = jnp.cumsum(counts) - counts
    padded = ((counts + MOE_BLOCK - 1) // MOE_BLOCK) * MOE_BLOCK
    pad_end = jnp.cumsum(padded)
    pad_start = pad_end - padded
    dest = pad_start[sorted_e] + (jnp.arange(n_assign, dtype=jnp.int32) - start[sorted_e])
    n_blocks = -(-n_assign // MOE_BLOCK) + N_EXPERTS
    n_rows = n_blocks * MOE_BLOCK
    row_tok = jnp.zeros((n_rows,), jnp.int32).at[dest].set(flat_tok[order])
    row_gate = jnp.zeros((n_rows,), f32).at[dest].set(flat_gate[order])
    block_e = jnp.minimum(
        jnp.searchsorted(pad_end, jnp.arange(n_blocks, dtype=pad_end.dtype) * MOE_BLOCK, side="right"),
        N_EXPERTS - 1).astype(jnp.int32)
    xs = jnp.take(xt, row_tok, axis=0).reshape(n_blocks, MOE_BLOCK, dm)

    def expert_block(args):
        xb, e = args
        return (jax.nn.silu(xb @ w_gate[e]) * (xb @ w_up[e])) @ w_down[e]

    ys = lax.map(expert_block, (xs, block_e)).reshape(n_rows, dm)
    ys = ys * row_gate[:, None].astype(ys.dtype)
    out = jnp.zeros((n_tok, dm), ys.dtype).at[row_tok].add(ys)
    return out.reshape(bsz, seq, dm)

def second_inputs(seed: int = 0) -> dict:
    key = jax.random.key(seed)
    ks = iter(jax.random.split(key, 48))
    f32 = jnp.float32
    L = DEPTH_2

    def nrm(shape, scale):
        return scale * jax.random.normal(next(ks), shape, f32)

    x = jax.random.normal(next(ks), (BATCH, SEQ, D_MODEL), f32)
    norm_mix_g = 1.0 + nrm((L, D_MODEL), 0.02)
    w_in = nrm((L, D_MODEL, IN_COLS), D_MODEL ** -0.5)
    a_v_norm_g = 1.0 + nrm((L, A_WIDTH), 0.02)
    a_spatial_w = nrm((L, A_HEADS, A_BLOCK, A_BLOCK), A_BLOCK ** -0.5)
    a_spatial_b = 1.0 + nrm((L, A_HEADS, A_BLOCK), 0.02)
    b_conv_w = nrm((L, CONV_WIDTH, B_WIDTH), CONV_WIDTH ** -0.5)
    b_conv_b = nrm((L, B_WIDTH), 0.02)
    b_rg_w = nrm((L, B_HEADS, HEAD_DIM, HEAD_DIM), HEAD_DIM ** -0.5)
    b_rg_b = nrm((L, B_WIDTH), 0.02)
    b_ig_w = nrm((L, B_HEADS, HEAD_DIM, HEAD_DIM), HEAD_DIM ** -0.5)
    b_ig_b = nrm((L, B_WIDTH), 0.02)
    a_pow = jax.random.uniform(next(ks), (L, B_WIDTH), f32, 0.9, 0.999)
    a0 = a_pow ** (1.0 / LRU_C)
    b_lambda = jnp.log(a0) - jnp.log1p(-a0)
    n_idx = jnp.arange(C_STATE, dtype=f32)
    c_a_re = -0.5 * jnp.exp(nrm((L, C_GROUPS, C_STATE), 0.05))
    c_a_im = math.pi * n_idx + nrm((L, C_GROUPS, C_STATE), 0.01)
    c_log_dt = jax.random.uniform(next(ks), (L, C_GROUPS), f32, math.log(1e-3), math.log(1e-1))
    c_b_re = nrm((L, C_GROUPS, C_STATE, C_GROUP_DIM), (2 * C_GROUP_DIM) ** -0.5)
    c_b_im = nrm((L, C_GROUPS, C_STATE, C_GROUP_DIM), (2 * C_GROUP_DIM) ** -0.5)
    c_c_re = nrm((L, C_GROUPS, C_GROUP_DIM, C_STATE), 0.5)
    c_c_im = nrm((L, C_GROUPS, C_GROUP_DIM, C_STATE), 0.5)
    c_d = nrm((L, C_WIDTH), 1.0)
    c_glu_w = nrm((L, C_WIDTH, C_WIDTH), C_WIDTH ** -0.5)
    c_glu_b = nrm((L, C_WIDTH), 0.02)
    mix_out_norm_g = 1.0 + nrm((L, D_MIX_2), 0.02)
    w_out = nrm((L, D_MIX_2, D_MODEL), D_MIX_2 ** -0.5)
    norm_ffn_g = 1.0 + nrm((L, D_MODEL), 0.02)
    router_group_w = nrm((L, D_MODEL, N_GROUPS), D_MODEL ** -0.5)
    router_group_b = nrm((L, N_GROUPS), 0.01)
    router_expert_w = nrm((L, N_GROUPS, D_MODEL, EXPERTS_PER_GROUP), D_MODEL ** -0.5)
    router_expert_b = nrm((L, N_GROUPS, EXPERTS_PER_GROUP), 0.01)
    expert_w_gate = nrm((L, N_EXPERTS, D_MODEL, D_EXPERT), D_MODEL ** -0.5)
    expert_w_up = nrm((L, N_EXPERTS, D_MODEL, D_EXPERT), D_MODEL ** -0.5)
    expert_w_down = nrm((L, N_EXPERTS, D_EXPERT, D_MODEL), D_EXPERT ** -0.5)
    final_norm_g = 1.0 + nrm((D_MODEL,), 0.02)
    return {
        "x": x, "norm_mix_g": norm_mix_g, "w_in": w_in,
        "a_v_norm_g": a_v_norm_g, "a_spatial_w": a_spatial_w, "a_spatial_b": a_spatial_b,
        "b_conv_w": b_conv_w, "b_conv_b": b_conv_b, "b_rg_w": b_rg_w, "b_rg_b": b_rg_b,
        "b_ig_w": b_ig_w, "b_ig_b": b_ig_b, "b_lambda": b_lambda,
        "c_a_re": c_a_re, "c_a_im": c_a_im, "c_log_dt": c_log_dt, "c_b_re": c_b_re, "c_b_im": c_b_im,
        "c_c_re": c_c_re, "c_c_im": c_c_im, "c_d": c_d, "c_glu_w": c_glu_w, "c_glu_b": c_glu_b,
        "mix_out_norm_g": mix_out_norm_g, "w_out": w_out, "norm_ffn_g": norm_ffn_g,
        "router_group_w": router_group_w, "router_group_b": router_group_b,
        "router_expert_w": router_expert_w, "router_expert_b": router_expert_b,
        "expert_w_gate": expert_w_gate, "expert_w_up": expert_w_up, "expert_w_down": expert_w_down,
        "final_norm_g": final_norm_g,
    }

def second_block(x, norm_mix_g, w_in, a_v_norm_g, a_spatial_w, a_spatial_b,
              b_conv_w, b_conv_b, b_rg_w, b_rg_b, b_ig_w, b_ig_b, b_lambda,
              c_a_re, c_a_im, c_log_dt, c_b_re, c_b_im, c_c_re, c_c_im, c_d, c_glu_w, c_glu_b,
              mix_out_norm_g, w_out, norm_ffn_g,
              router_group_w, router_group_b, router_expert_w, router_expert_b,
              expert_w_gate, expert_w_up, expert_w_down, final_norm_g):
    h = x
    for l in range(DEPTH_2):
        mix = hybrid_mixer_2(h, norm_mix_g[l], w_in[l], a_v_norm_g[l], a_spatial_w[l], a_spatial_b[l],
                           b_conv_w[l], b_conv_b[l], b_rg_w[l], b_rg_b[l], b_ig_w[l], b_ig_b[l], b_lambda[l],
                           c_a_re[l], c_a_im[l], c_log_dt[l], c_b_re[l], c_b_im[l], c_c_re[l], c_c_im[l],
                           c_d[l], c_glu_w[l], c_glu_b[l], mix_out_norm_g[l], w_out[l])
        h = h + mix.astype(h.dtype)
        ffn = hierarchical_moe(rms_norm_2(h, norm_ffn_g[l]), router_group_w[l], router_group_b[l],
                               router_expert_w[l], router_expert_b[l],
                               expert_w_gate[l], expert_w_up[l], expert_w_down[l])
        h = h + ffn.astype(h.dtype)
    return rms_norm_2(h, final_norm_g).astype(x.dtype)


def setup_inputs(seed=0):
    out = dict(first_inputs(seed))
    for name, value in second_inputs(seed + 1).items():
        if name != "x":
            out[name + "_2"] = value
    return out


def reference(
    x, c, positions, w_ada, b_ada, w_in, w_gate_up, b_gate, gla_out_norm, q_a_norm, w_q_up,
    kv_a_norm, w_kv_up, q_norm_nope, k_norm_nope, q_norm_rope, k_norm_rope, w_out, w_mlp_up,
    w_mlp_down, norm_mix_g_2, w_in_2, a_v_norm_g_2, a_spatial_w_2, a_spatial_b_2, b_conv_w_2,
    b_conv_b_2, b_rg_w_2, b_rg_b_2, b_ig_w_2, b_ig_b_2, b_lambda_2, c_a_re_2, c_a_im_2,
    c_log_dt_2, c_b_re_2, c_b_im_2, c_c_re_2, c_c_im_2, c_d_2, c_glu_w_2, c_glu_b_2,
    mix_out_norm_g_2, w_out_2, norm_ffn_g_2, router_group_w_2, router_group_b_2,
    router_expert_w_2, router_expert_b_2, expert_w_gate_2, expert_w_up_2, expert_w_down_2,
    final_norm_g_2,
):
    x = first_block(
        x, c, positions, w_ada, b_ada, w_in, w_gate_up, b_gate, gla_out_norm, q_a_norm, w_q_up,
        kv_a_norm, w_kv_up, q_norm_nope, k_norm_nope, q_norm_rope, k_norm_rope, w_out, w_mlp_up,
        w_mlp_down,
    )
    return second_block(
        x, norm_mix_g_2, w_in_2, a_v_norm_g_2, a_spatial_w_2, a_spatial_b_2, b_conv_w_2,
        b_conv_b_2, b_rg_w_2, b_rg_b_2, b_ig_w_2, b_ig_b_2, b_lambda_2, c_a_re_2, c_a_im_2,
        c_log_dt_2, c_b_re_2, c_b_im_2, c_c_re_2, c_c_im_2, c_d_2, c_glu_w_2, c_glu_b_2,
        mix_out_norm_g_2, w_out_2, norm_ffn_g_2, router_group_w_2, router_group_b_2,
        router_expert_w_2, router_expert_b_2, expert_w_gate_2, expert_w_up_2, expert_w_down_2,
        final_norm_g_2,
    )


_drawn_inputs = setup_inputs


def setup_inputs(seed=0):
    import zlib

    import numpy as np

    out = dict(_drawn_inputs(seed))
    spreads = {}
    factors = {'gla_out_norm': 5.075,
     'q_a_norm': 8.0,
     'kv_a_norm': 7.131,
     'q_norm_nope': 8.0,
     'k_norm_nope': 8.0,
     'q_norm_rope': 8.0,
     'k_norm_rope': 8.0,
     'norm_mix_g_2': 4.18,
     'a_v_norm_g_2': 8.0,
     'a_spatial_b_2': 8.0,
     'b_conv_b_2': 4.822,
     'b_rg_b_2': 8.0,
     'b_ig_b_2': 8.0,
     'c_a_re_2': 8.0,
     'c_glu_b_2': 8.0,
     'mix_out_norm_g_2': 5.119,
     'norm_ffn_g_2': 4.619,
     'router_group_b_2': 7.712,
     'router_expert_b_2': 23.343,
     'final_norm_g_2': 8.302}
    for name, (base, spread) in spreads.items():
        noise = np.random.default_rng([zlib.crc32(name.encode()), seed]).standard_normal(out[name].shape)
        drawn = base * np.exp(spread * noise) if base else spread * noise
        out[name] = jnp.asarray(drawn.astype(out[name].dtype))
    for name, factor in factors.items():
        out[name] = (out[name] * factor).astype(out[name].dtype)
    return out
```

```python
import numpy as np

import concourse.bass as bass
from concourse import mybir

ALU = mybir.AluOpType
ACT = mybir.ActivationFunctionType
AX = mybir.AxisListType
F32 = mybir.dt.float32
I32 = mybir.dt.int32
P = 128


class Loop:

    def __init__(self, name, reg, trips, per_trip):
        self.name, self.reg, self.trips, self.per_trip = name, reg, trips, per_trip


class Count:

    def __init__(self, owner, const, terms):
        self.owner, self.const, self.terms = owner, const, terms


class Counter:

    def __init__(self, prog, name):
        self.prog, self.name = prog, name
        self.sem = prog.nc.alloc_semaphore(name)
        self.const, self.terms, self.starts = 0, (), []
        prog.counters.append(self)

    def step(self, amount):
        self.const += amount
        return Count(self, self.const, self.terms)

    def now(self):
        return Count(self, self.const, self.terms)

    def enter(self, loop):
        per = self.prog.known.get((loop.name, self.name), 0)
        loop.per_trip[self.name] = per
        self.starts.append((self.const, self.terms))
        self.terms = self.terms + ((loop, per),)

    def leave(self, loop):
        const, terms = self.starts.pop()
        per = self.const - const
        self.prog.found[(loop.name, self.name)] = per
        self.const, self.terms = const + loop.trips * per, terms


class Engine:

    def __init__(self, prog, name, api):
        self.prog, self.api = prog, api
        self.count = Counter(prog, f"{name}_steps")
        self.last, self.seen, self.held = None, {}, False
        self.idle = prog.nc.alloc_semaphore(f"{name}_idle")

    def wait(self, *counts):
        for c in counts:
            if c is None:
                continue
            if isinstance(c, (list, tuple)):
                self.wait(*c)
                continue
            const, terms = self.prog.in_trip(c)
            key = (c.owner.name, tuple((l.name, p) for l, p in terms))
            if self.seen.get(key, -1) >= const:
                continue
            self.seen[key] = const
            if self.count.name == "sp_steps":
                self.settle()
            value = const
            for loop, per in terms:
                if per:
                    value, self.held = loop.reg * per + value, True
            self.api.wait_ge(c.owner.sem, value)

    def settle(self):
        if self.held:
            self.api.sem_inc(self.idle, 1)
        self.held = False

    def issue(self, instruction, *args, alone=False, **kw):
        if alone or any(type(a).__name__ == "AP" and a.regs_read for a in (*args, *kw.values())):
            self.settle()
        self.held = False
        return instruction(*args, **kw)

    def run(self, instruction, *args, after=(), **kw):
        self.wait(*after)
        self.issue(instruction, *args, **kw).then_inc(self.count.sem, 1)
        self.last = self.count.step(1)
        return self.last

    def then(self, instruction, *args, after=(), **kw):
        return self.run(instruction, *args, after=(self.last, *after), **kw)

    def quiet(self, instruction, *args, after=(), **kw):
        self.wait(*after)
        self.issue(instruction, *args, **kw)


class Channel:

    def __init__(self, prog, name):
        self.count = Counter(prog, name)

    def start(self, eng, out, in_, after=(), **kw):
        eng.wait(*after)
        if any(a.regs_read for a in (out, in_)):
            eng.settle()
        eng.held = False
        eng.api.dma_start(out, in_, **kw).then_inc(self.count.sem, 16)
        return self.count.step(16)

    def gather(self, eng, out, table, index, after=()):
        eng.wait(*after)
        eng.settle()
        eng.api.indirect_dma_start(out=out, out_offset=None, in_=table,
                                   in_offset=bass.IndirectOffsetOnAxis(ap=index, axis=0)).then_inc(self.count.sem, 16)
        return self.count.step(16)

    def scatter(self, eng, table, index, in_, after=()):
        eng.wait(*after)
        eng.settle()
        eng.api.indirect_dma_start(out=table, out_offset=bass.IndirectOffsetOnAxis(ap=index, axis=0), in_=in_,
                                   in_offset=None).then_inc(self.count.sem, 16)
        return self.count.step(16)


class Slot:

    def __init__(self, ring, n, ap, channel=None):
        self.ring, self.n, self.ap, self.channel = ring, n, ap, channel
        self.free, self.taken, self.held = [], False, False

    def release(self, *counts):
        self.free, self.held = list(counts), False


class Ring:

    def __init__(self, prog, name, aps, channels=None):
        self.prog, self.name, self.next = prog, name, 0
        self.slots = [Slot(self, n, ap, channels[n] if channels else None) for n, ap in enumerate(aps)]
        prog.rings.append(self)

    def take(self):
        slot = self.slots[self.next % len(self.slots)]
        self.next += 1
        assert not slot.held, f"{self.name}{slot.n} is taken before it is released"
        slot.taken = slot.held = True
        return slot

    def align(self, n):
        self.next = -(-self.next // n) * n


class Prog:
    def __init__(self, nc, known):
        self.nc, self.known, self.found = nc, known, {}
        self.counters, self.rings, self.loops = [], [], []
        self.pe = Engine(self, "pe", nc.tensor)
        self.act = Engine(self, "act", nc.scalar)
        self.dve = Engine(self, "dve", nc.vector)
        self.pool = Engine(self, "pool", nc.gpsimd)
        self.sp = Engine(self, "sp", nc.sync)
        self.engines = [self.pe, self.act, self.dve, self.pool, self.sp]

    def mark(self, name, *counts):
        self.found[("mark", name)] = [(c.owner.name, self.in_trip(c)[0]) for c in counts if c is not None]

    def in_trip(self, c):
        const, terms = c.const, []
        for loop, per in c.terms:
            if loop in self.loops:
                terms.append((loop, per))
            else:
                const += (loop.trips - 1) * self.found[(loop.name, c.owner.name)]
        return const, terms

    def before(self, name):
        out = []
        by_name = {c.name: c for c in self.counters}
        for owner, const in self.known.get(("mark", name), []):
            c = by_name[owner]
            loop = self.loops[-1]
            assert c.terms and c.terms[-1][0] is loop
            assert const - loop.per_trip[owner] > 0, (name, owner, const, loop.per_trip[owner])
            out.append(Count(c, const - loop.per_trip[owner], c.terms))
        return out

    def loop(self, name, trips):
        return _Body(self, name, trips)

    def join(self, *channels):
        engines = (self.pe, self.act, self.dve, self.pool)
        ends = [e.last for e in engines]
        for e in engines:
            e.wait(*ends, *[c.count.now() for c in channels])


class _Body:
    def __init__(self, prog, name, trips):
        self.prog, self.name, self.trips = prog, name, trips

    def __enter__(self):
        p = self.prog
        for ring in p.rings:
            writer = p.pe if ring.name == "psum" else p.sp
            for s in ring.slots:
                writer.wait(*s.free)
        for e in p.engines:
            e.settle()
        self.ctx = p.nc.Fori(0, self.trips)
        reg = self.ctx.__enter__()
        self.loop = Loop(self.name, reg, self.trips, {})
        for c in p.counters:
            c.enter(self.loop)
        p.loops.append(self.loop)
        self.saved = [dict(e.seen) for e in p.engines]
        for e in p.engines:
            e.seen = {}
            e.last = Count(e.count, e.count.const, e.count.terms)
        for r in p.rings:
            r.align(len(r.slots))
        self.outer = [[(s.free, s.taken) for s in r.slots] for r in p.rings]
        for ring in p.rings:
            for s in ring.slots:
                s.free, s.taken = p.before(f"{self.name}:{ring.name}{s.n}"), False
        return reg

    def __exit__(self, *exc):
        if exc[0] is not None:
            return False
        p = self.prog
        for ring, outer in zip(p.rings, self.outer):
            ring.align(len(ring.slots))
            for s, (free, taken) in zip(ring.slots, outer):
                if s.taken:
                    p.mark(f"{self.name}:{ring.name}{s.n}", *s.free)
                else:
                    s.free, s.taken = free, taken
        for e in p.engines:
            e.settle()
        p.loops.pop()
        self.ctx.__exit__(None, None, None)
        for c in p.counters:
            c.leave(self.loop)
        for e, seen in zip(p.engines, self.saved):
            e.seen = seen
            e.last = e.count.now()
        return False


AW, AH, HD = 384, 6, 64
BW, BC = 384, 3
CW, CG, CGD, CS = 256, 16, 16, 64
LRU_C = 8.0
NG, EPG = 4, 4
NE = NG * EPG
D_EXP = 512
TOP = 2
NB = 1024 * TOP // 128 + NE
NROWS = NB * 128
LOGITS = NG + NE
SCRATCH_2 = {"hn": (1024, 1024), "row_tok": (NROWS + 2 * 128, 1), "ys": (NROWS, 1024)}
INT_SCRATCH = ("row_tok",)
CHANNELS_2 = ("x2_in small2 small3 w_a_in b_in c_in lam_in w_out2_in hn_out tok_clear tok_out idx0_in idx1_in rows0_in rows1_in "
              "ys0_out ys1_out y1_in y2_in out0 w_route_in").split()


def second(k):
    spatial_gating(k)
    features_by_time(k)
    recurrence(k)
    state_space(k)
    output_and_route(k)
    placement(k)
    experts(k)
    combine(k)


def Areas2(k):
    A = Area(k.arena)
    k.yT = A.take(KC, S)
    k.hT2 = A.take(KC, S)
    return A


def spatial_gating(k):
    g, nc, d = k.g, k.g.nc, k.dram
    dve, act, pe, pool, v, s, gp = g.dve, g.act, g.pe, g.pool, nc.vector, nc.scalar, nc.gpsimd
    A = Areas2(k)
    w_a = A.take(KC, 2 * AW)
    xt, xn, hT = A.take(D), A.take(D), A.take(KC, P)
    wsT, ws = A.take(AH, P), A.take(AH, P)
    u, vv, junk, ya = A.take(AW), A.take(AW), A.take(AW), A.take(AW)
    vg = A.take(AW)
    rows = A.take(P)
    k.cols = k.small
    ch = k.channel("small2")
    C = k.cols

    def rows_to_cols(pieces):
        at = 0
        for src, n, col in pieces:
            got = ch.start(g.act, rows[at:at + n], src)
            at += n
        bank = k.bank()
        t = k.turn([(bank.ap[:, 0:at], rows[0:at])], after=[got])
        at = 0
        for src, n, col in pieces:
            e = dve.run(v.tensor_copy, C[:, col:col + n], bank.ap[:, at:at + n], after=[t])
            at += n
        bank.release(e)
        return e

    r = lambda name, n: d[name][0].rearrange("(k p) -> k p", p=P)
    cols = rows_to_cols([(r("norm_mix_g_2", 8), 8, 0), (r("mix_out_norm_g_2", 8), 8, 8), (d["a_spatial_b_2"][0], AH, 16),
                         (r("b_conv_b_2", 3), 3, 24), (r("b_rg_b_2", 3), 3, 27), (r("b_ig_b_2", 3), 3, 30),
                         (r("b_lambda_2", 3), 3, 33), (d["b_conv_w_2"][0].rearrange("w (k p) -> (w k) p", p=P), 12, 36),
                         (r("c_d_2", 2), 2, 48), (r("c_glu_b_2", 2), 2, 50)])
    ch = k.channel("small3")
    ch.start(g.act, vg, d["a_v_norm_g_2"][0].partition_broadcast(P))
    got = ch.start(g.act, ws, d["a_spatial_w_2"][0].rearrange("h i j -> i h j"))
    wi = d["w_in_2"][0].rearrange("(k p) n -> p k n", p=P)
    came_w = k.channel("w_a_in").start(g.act, w_a, wi[:, :, 0:2 * AW])
    for n in range(2):
        bank = k.bank()
        t = k.turn([(bank.ap[:, j * P:(j + 1) * P], ws[:, 3 * n + j, :]) for j in range(3)], after=[got])
        e = dve.run(v.tensor_copy, wsT[:, 3 * n:3 * n + 3, :].rearrange("p a n -> p (a n)"), bank.ap[:, 0:3 * P], after=[t])
        bank.release(e)
    hid = dve.then(v.memset, wsT[P // 2:P, :, 0:P // 2], 0.0)
    pe.wait(hid, came_w)
    act.wait(cols)
    stored = k.channel("x_out").count.now()
    st = k.stat
    with g.loop("tiles2", NT) as t:
        x_in = k.channel("x2_in").start(g.sp, xt, d["x_res"][bass.ds(t * P, P), :], after=[*g.before("x2_read"), stored])
        q = act.run(s.activation, xn, xt, ACT.Square, accum_out=st[:, 0:1], after=[x_in, *g.before("xn2_read")])
        r_ = k.rsqrt_mean(st[:, 1:2], st[:, 0:1], D, after=[q])
        n_ = dve.run(v.tensor_scalar, xn, xt, st[:, 1:2], None, ALU.mult, after=[r_])
        g.mark("x2_read", n_)
        for half in range(2):
            bank = k.bank()
            tt = k.turn([(bank.ap[:, j * P:(j + 1) * P], xn[:, (4 * half + j) * P:(4 * half + j + 1) * P]) for j in range(4)], after=[n_])
            e = dve.run(v.tensor_tensor, hT[:, 4 * half:4 * half + 4, :], bank.ap.rearrange("p (k n) -> p k n", k=4),
                        spread(C[:, 4 * half:4 * half + 4].unsqueeze(2), P, 4, P), ALU.mult, after=[tt, *g.before("hT2_read")])
            bank.release(e)
        g.mark("xn2_read", tt)
        cp = pool.run(gp.tensor_copy, k.hT2[:, :, bass.ds(t * P, P)], hT, after=[e])
        bu = k.bank()
        m = k.product(bu.ap[:, 0:AW], [(hT[:, c, :], w_a[:, c, 0:AW]) for c in range(KC)], after=[e])
        eu = act.run(s.activation, u, bu.ap[:, 0:AW], ACT.Gelu_apprx_tanh, after=[m, *g.before("u2_read")])
        bu.release(eu)
        bv = k.bank()
        m = k.product(bv.ap[:, 0:AW], [(hT[:, c, :], w_a[:, c, AW:]) for c in range(KC)])
        g.mark("hT2_read", m, cp)
        ev = act.run(s.activation, vv, bv.ap[:, 0:AW], ACT.Gelu_apprx_tanh, after=[m])
        bv.release(ev)
        q = act.then(s.activation, junk, vv, ACT.Square, accum_out=st[:, 2:3])
        r_ = k.rsqrt_mean(st[:, 3:4], st[:, 2:3], AW, after=[q])
        vn = dve.run(v.scalar_tensor_tensor, vv, vv, st[:, 3:4], vg, ALU.mult, ALU.mult, after=[r_])
        bs = k.bank()
        pe.wait(vn)
        for h in range(AH):
            m = k.product(bs.ap[:, h * HD:(h + 1) * HD], [(wsT[:, h, :], vv[:, h * HD:(h + 1) * HD])])
        y3 = ya.rearrange("p (h n) -> p h n", h=AH)
        sv = dve.run(v.tensor_tensor, y3, bs.ap[:, 0:AW].rearrange("p (h n) -> p h n", h=AH),
                     spread(C[:, 16:16 + AH].unsqueeze(2), P, AH, HD), ALU.add, after=[m, *g.before("ya_read")])
        bs.release(sv)
        y = dve.then(v.tensor_tensor, ya, ya, u, ALU.mult, after=[eu])
        g.mark("u2_read", y)
        q = act.run(s.activation, junk, ya, ACT.Square, accum_out=st[:, 4:5], after=[y])
        r_ = k.rsqrt_mean(st[:, 5:6], st[:, 4:5], AW, after=[q])
        y = dve.run(v.tensor_scalar, ya, ya, st[:, 5:6], None, ALU.mult, after=[r_])
        by = k.bank()
        tt = k.turn([(by.ap[:, j * P:(j + 1) * P], ya[:, j * P:(j + 1) * P]) for j in range(3)], after=[y])
        g.mark("ya_read", tt)
        e = act.run(s.activation, k.yT[:, 0:3, bass.ds(t * P, P)], by.ap[:, 0:3 * P].rearrange("p (a n) -> p a n", a=3), ACT.Copy,
                    after=[tt])
        by.release(e)
    g.join()


def features_by_time(k):
    g, nc, d = k.g, k.g.nc, k.dram
    dve, act, pe, v, s = g.dve, g.act, g.pe, nc.vector, nc.scalar
    A = Areas2(k)
    k.xc_in = A.take(2, S)
    k.xpad = A.take(BC, S + 3)
    k.gb = A.take(BC, S)
    k.area_b = A
    wi = d["w_in_2"][0].rearrange("(k p) n -> p k n", p=P)
    dve.run(v.memset, k.xpad[:, :, 0:3], 0.0)
    for piece in range(4):
        slot, view, came = k.load_weights(wi[:, :, 2 * AW + piece * 256:2 * AW + (piece + 1) * 256], (KC, 256))
        pe.wait(came)
        for blk in range(2):
            c = 2 * piece + blk
            for half in range(2):
                cols = slice(half * 512, (half + 1) * 512)
                bank = k.bank()
                m = k.product(bank.ap, [(view[:, kc, blk * P:(blk + 1) * P], k.hT2[:, kc, cols]) for kc in range(KC)])
                if c < BC:
                    e = dve.run(v.tensor_copy, k.xpad[:, c, 3 + half * 512:3 + (half + 1) * 512], bank.ap, after=[m])
                elif c < 2 * BC:
                    e = act.run(s.activation, k.gb[:, c - BC, cols], bank.ap, ACT.Gelu_apprx_tanh, after=[m])
                else:
                    e = dve.run(v.tensor_copy, k.xc_in[:, c - 2 * BC, cols], bank.ap, after=[m])
                bank.release(e)
        slot.release(m)
    g.join()


def recurrence(k):
    g, nc, d = k.g, k.g.nc, k.dram
    dve, act, pe, pool, v, s, gp = g.dve, g.act, g.pe, g.pool, nc.vector, nc.scalar, nc.gpsimd
    A = Area(k.arena)
    A.skip(KC * S)
    xc, r, = A.take(BC, S), A.take(BC, S)
    wr = A.take(2, BC, P)
    A2 = k.area_b
    i_ = A2.take(BC, S)
    h = A2.take(BC, S)
    C = k.cols
    neg = k.stat[:, 0:12]
    z = pool.run(gp.memset, wr, 0.0)
    for n, name in enumerate(("b_rg_w_2", "b_ig_w_2")):
        for a in range(2):
            got = k.channel("b_in").start(g.act, wr[64 * a:64 * a + 64, n, :, 64 * a:64 * a + 64],
                                          d[name][0].rearrange("(c a) i j -> a i c j", a=2)[a], after=[z])
    a1 = act.run(s.activation, neg[:, 6:9], C[:, 33:36], ACT.Abs)
    act.then(s.activation, neg[:, 6:9], neg[:, 6:9], ACT.Exp, scale=-1.0)
    a1 = act.then(s.activation, neg[:, 6:9], neg[:, 6:9], ACT.Ln, bias=1.0)
    dve.run(v.tensor_scalar, neg[:, 9:12], C[:, 33:36], -1.0, 0.0, ALU.mult, ALU.max)
    dve.then(v.tensor_tensor, neg[:, 6:9], neg[:, 6:9], neg[:, 9:12], ALU.add, after=[a1])
    ready = dve.then(v.tensor_scalar_mul, neg[:, 6:9], neg[:, 6:9], -LRU_C)
    for c in range(BC):
        dve.run(v.tensor_scalar, xc[:, c, :], k.xpad[:, c, 3:3 + S], C[:, 36 + 9 + c:37 + 9 + c], C[:, 24 + c:25 + c], ALU.mult, ALU.add)
        for w in range(3):
            x1 = dve.then(v.scalar_tensor_tensor, xc[:, c, :], k.xpad[:, c, w:w + S], C[:, 36 + 3 * w + c:37 + 3 * w + c], xc[:, c, :],
                          ALU.mult, ALU.add)
        pe.wait(x1, got)
        for n, out in enumerate((r, i_)):
            for half in range(2):
                cols = slice(half * 512, (half + 1) * 512)
                bank = k.bank()
                m = k.product(bank.ap, [(wr[:, n, c, :], xc[:, c, cols])])
                e = act.run(s.activation, out[:, c, cols], bank.ap, ACT.Sigmoid, bias=C[:, 27 + 3 * n + c:28 + 3 * n + c], after=[m])
                bank.release(e)
    ix = dve.run(v.tensor_tensor, i_, i_, xc, ALU.mult, after=[e])
    th = k.xpad[:, :, 0:S]
    for c in range(BC):
        act.run(s.activation, th[:, c, :], r[:, c, :], ACT.Tanh, scale=neg[:, 6 + c:7 + c], after=[ix, ready])
        act.then(s.activation, r[:, c, :], r[:, c, :], ACT.Exp, scale=neg[:, 6 + c:7 + c])
    act.then(s.activation, h, th, ACT.Ln, scale=-1.0, bias=1.0)
    e = act.then(s.activation, h, h, ACT.Exp, scale=-0.5)
    e2 = act.run(s.activation, th, th, ACT.Sqrt, scale=-2.0)
    dve.run(v.tensor_tensor, i_, i_, h, ALU.mult, after=[e])
    dve.then(v.tensor_tensor, i_, i_, th, ALU.mult, after=[e2])
    for c in range(BC):
        dve.then(v.tensor_tensor_scan, h[:, c, :], r[:, c, :], i_[:, c, :], 0.0, ALU.mult, ALU.add)
    dve.then(v.tensor_tensor, k.yT[:, 3:6, :], h, k.gb, ALU.mult)
    g.join()


def state_space(k):
    g, nc, d = k.g, k.g.nc, k.dram
    dve, act, pe, pool, v, s, gp = g.dve, g.act, g.pe, g.pool, nc.vector, nc.scalar, nc.gpsimd
    A = Area(k.arena)
    A.skip(KC * S)
    Bp, Cp = A.take(2, 4, P), A.take(2, 4, P)
    A.skip(KC * S - 2048)
    A.skip(2 * S)
    wide = A.take(2, S)
    gin = A.take(2, S)
    gs = A.take(2, S)
    pr = A.take(4, S)
    y = A.take(2, S)
    lam = A.take(24, 8)
    Bt, Ct = A.take(3, P), A.take(3, P)
    Bn = A.take(2, P)
    glu = A.take(2, CW)
    t1 = A.take(S)
    pw = A.take(2, 12)
    ar, ai, ldt, mag, th, cr, ci, nr, fr, fi, q1, q2 = (lam[:, n, :] for n in range(12))
    ch = k.channel("lam_in")
    for dst, name in ((ar, "c_a_re_2"), (ai, "c_a_im_2")):
        ch.start(g.act, dst, d[name][0].rearrange("(t a) p -> (a p) t", a=2), allow_slow_non_contiguous=True)
    for a in range(2):
        got = ch.start(g.act, ldt[64 * a:64 * a + 64],
                       d["c_log_dt_2"][0].rearrange("(t a) -> a t", a=2)[a].partition_broadcast(64), allow_slow_non_contiguous=True)
    got_glu = ch.start(g.act, glu, d["c_glu_w_2"][0].rearrange("(k p) n -> p k n", p=P))
    dt = act.run(s.activation, ldt, ldt, ACT.Exp, after=[got_glu])
    dve.run(v.tensor_tensor, mag, ar, ldt, ALU.mult, after=[dt])
    a0 = dve.run(v.tensor_tensor, th, ai, ldt, ALU.mult)
    a1 = act.run(s.activation, mag, mag, ACT.Exp, after=[a0])
    s1 = sine(k, ci, th, 0.0, (q1, q2), after=[a0, a1])
    s2 = sine(k, cr, th, np.pi / 2, (q1, q2), after=[s1])
    pr_, pi_ = A.take(11, 8), A.take(11, 8)
    dve.run(v.tensor_copy, pr_[:, 0, :], cr, after=[s2])
    dve.run(v.tensor_copy, pi_[:, 0, :], ci)
    for n in range(10):
        dve.then(v.tensor_tensor, q1, pr_[:, n, :], pr_[:, n, :], ALU.mult)
        dve.run(v.tensor_tensor, q2, pi_[:, n, :], pi_[:, n, :], ALU.mult)
        dve.run(v.scalar_tensor_tensor, pi_[:, n + 1, :], pr_[:, n, :], 2.0, pi_[:, n, :], ALU.mult, ALU.mult)
        dve.then(v.tensor_tensor, pr_[:, n + 1, :], q1, q2, ALU.subtract)
    dve.then(v.tensor_tensor, nr, mag, cr, ALU.mult)
    dve.then(v.tensor_scalar_add, nr, nr, -1.0)
    ni = dve.run(v.tensor_tensor, th, mag, ci, ALU.mult)
    dve.then(v.tensor_tensor, fr, nr, ar, ALU.mult)
    dve.run(v.tensor_tensor, q1, th, ai, ALU.mult)
    dve.then(v.tensor_tensor, fr, fr, q1, ALU.add)
    dve.run(v.tensor_tensor, fi, th, ar, ALU.mult)
    dve.run(v.tensor_tensor, q2, nr, ai, ALU.mult)
    dve.then(v.tensor_tensor, fi, fi, q2, ALU.subtract)
    dve.run(v.tensor_tensor, q1, ar, ar, ALU.mult)
    dve.then(v.tensor_tensor, q2, ai, ai, ALU.mult)
    dve.then(v.tensor_tensor, q1, q1, q2, ALU.add)
    dve.then(v.reciprocal, q1, q1)
    dve.then(v.tensor_tensor, fr, fr, q1, ALU.mult)
    dve.run(v.tensor_tensor, fi, fi, q1, ALU.mult)
    z = pool.run(gp.memset, Bp, 0.0)
    z = pool.run(gp.memset, Cp, 0.0)
    f3 = lambda x: x.rearrange("p (q s) -> p q s", q=2)
    bp_view = Bp.rearrange("p a s (c n) -> p a s c n", n=CGD)
    with g.loop("halves", 2) as q:
        after = [z, *g.before("pads_read")]
        for n, nm in enumerate(("re", "im")):
            bsrc = d[f"c_b_{nm}_2"][0].rearrange("(q s a) p c -> a q p s c", s=4, a=2)
            csrc = d[f"c_c_{nm}_2"][0].rearrange("(q s a) c p -> s a q c p", s=4, a=2)
            for a in range(2):
                for sg in range(4):
                    got = k.channel("c_in").start(g.act, Bp[64 * a:64 * a + 64, n, sg, CGD * (2 * sg + a):CGD * (2 * sg + a) + CGD],
                                                  bsrc[a][bass.ds(q, 1), :, sg, :].rearrange("o p c -> (o p) c"), after=after)
                    lo = CGD * (2 * sg + a)
                    got = k.channel("c_in").start(g.act, Cp[lo:lo + CGD, n, sg, 64 * a:64 * a + 64],
                                                  csrc[sg, a][bass.ds(q, 1)].rearrange("o c p -> (o c) p"))
        k.banks.align(8)
        y_banks = [k.bank(), k.bank()]
        for sg in range(4):
            col = lambda x: x[:, bass.ds(4 * q + sg, 1)]
            cfr, cfi = t1[:, 0:1], t1[:, 1:2]
            dve.then(v.tensor_copy, cfr, col(fr))
            dve.run(v.tensor_copy, cfi, col(fi))
            dve.run(v.tensor_copy, t1[:, 2:3], col(mag))
            dve.run(v.tensor_copy, t1[:, 4:15], pr_[:, :, bass.ds(4 * q + sg, 1)].rearrange("p a o -> p (a o)"))
            dve.run(v.tensor_copy, t1[:, 16:27], pi_[:, :, bass.ds(4 * q + sg, 1)].rearrange("p a o -> p (a o)"))
            dve.then(v.tensor_scalar, Bn[:, 0, :], Bp[:, 1, sg, :], cfi, None, ALU.mult, after=[got])
            dve.run(v.tensor_scalar, Bn[:, 1, :], Bp[:, 1, sg, :], cfr, None, ALU.mult)
            dve.then(v.scalar_tensor_tensor, Bn[:, 0, :], Bp[:, 0, sg, :], cfr, Bn[:, 0, :], ALU.mult, ALU.subtract)
            b_r = dve.run(v.scalar_tensor_tensor, Bn[:, 1, :], Bp[:, 0, sg, :], cfi, Bn[:, 1, :], ALU.mult, ALU.add)
            bank = k.bank()
            t = k.turn([(bank.ap[:, 0:P], Bn[:, 0, :]), (bank.ap[:, P:2 * P], Bn[:, 1, :]),
                        (bank.ap[:, 2 * P:3 * P], Cp[:, 0, sg, :]), (bank.ap[:, 3 * P:4 * P], Cp[:, 1, sg, :])], after=[b_r, got])
            act.run(s.activation, Bt[:, 0:2, :], bank.ap[:, 0:2 * P].rearrange("p (a n) -> p a n", a=2), ACT.Copy, after=[t])
            act.run(s.activation, Ct[:, 0, :], bank.ap[:, 2 * P:3 * P], ACT.Copy)
            act.run(s.activation, Ct[:, 1, :], bank.ap[:, 2 * P:3 * P], ACT.Copy, scale=-1.0)
            tb = act.run(s.activation, Ct[:, 2, :], bank.ap[:, 3 * P:4 * P], ACT.Copy, scale=-1.0)
            bank.release(tb)
            one = dve.run(v.memset, wide[:, 0, 0:1], 1.0)
            dve.run(v.memset, wide[:, 1, 0:1], 0.0)
            n = 1
            for lv in range(10):
                er, ei = wide[:, 0, 0:n], wide[:, 1, 0:n]
                wr_, wi_ = t1[:, 4 + lv:5 + lv], t1[:, 16 + lv:17 + lv]
                dve.then(v.tensor_scalar, wide[:, 0, n:2 * n], ei, wi_, None, ALU.mult)
                dve.run(v.tensor_scalar, wide[:, 1, n:2 * n], ei, wr_, None, ALU.mult)
                dve.then(v.scalar_tensor_tensor, wide[:, 0, n:2 * n], er, wr_, wide[:, 0, n:2 * n], ALU.mult, ALU.subtract)
                dve.run(v.scalar_tensor_tensor, wide[:, 1, n:2 * n], er, wi_, wide[:, 1, n:2 * n], ALU.mult, ALU.add)
                n *= 2
            for half in range(2):
                cols = slice(half * 512, (half + 1) * 512)
                bre, bim = k.bank_after(y_banks), k.bank_after(y_banks)
                x_ = k.xc_sel(q, cols)
                m = k.product(bre.ap, [(Bt[:, 0, :], x_)], after=[tb])
                m = k.product(bim.ap, [(Bt[:, 1, :], x_)])
                cs, sn = wide[:, 0, cols], wide[:, 1, cols]
                dve.then(v.tensor_tensor, gin[:, 0, cols], bre.ap, cs, ALU.mult, after=[m])
                dve.run(v.tensor_tensor, pr[:, 0, cols], bim.ap, sn, ALU.mult, after=[m])
                dve.run(v.tensor_tensor, gin[:, 1, cols], bim.ap, cs, ALU.mult)
                e = dve.run(v.tensor_tensor, pr[:, 1, cols], bre.ap, sn, ALU.mult)
                bre.release(e)
                bim.release(e)
            dve.then(v.tensor_tensor, gin[:, 0, :], gin[:, 0, :], pr[:, 0, :], ALU.add)
            dve.run(v.tensor_tensor, gin[:, 1, :], gin[:, 1, :], pr[:, 1, :], ALU.subtract)
            m_ = spread(t1[:, 2:3], P, S)
            dve.then(v.tensor_tensor_scan, gs[:, 0, :], m_, gin[:, 0, :], 0.0, ALU.mult, ALU.add)
            sc = dve.run(v.tensor_tensor_scan, gs[:, 1, :], m_, gin[:, 1, :], 0.0, ALU.mult, ALU.add)
            cs, sn = wide[:, 0, :], wide[:, 1, :]
            p1 = pool.run(gp.tensor_tensor, pr[:, 0, :], gs[:, 0, :], cs, ALU.mult, after=[sc])
            p1 = pool.run(gp.tensor_tensor, pr[:, 1, :], gs[:, 1, :], sn, ALU.mult)
            dve.then(v.tensor_tensor, pr[:, 2, :], gs[:, 0, :], sn, ALU.mult)
            p2 = dve.run(v.tensor_tensor, pr[:, 3, :], gs[:, 1, :], cs, ALU.mult)
            for half in range(2):
                cols = slice(half * 512, (half + 1) * 512)
                m = k.product(y_banks[half].ap, [(Ct[:, 0, :], pr[:, 0, cols]), (Ct[:, 1, :], pr[:, 1, cols]),
                                                 (Ct[:, 2, :], pr[:, 2, cols]), (Ct[:, 2, :], pr[:, 3, cols])],
                              after=[p1, p2], start=sg == 0, stop=sg == 3)
            act.wait(m)
            dve.wait(m)
        g.mark("pads_read", m, b_r)
        dcol = t1[:, 32:33]
        dve.then(v.tensor_copy, dcol, k.cols[:, bass.ds(48 + q, 1)])
        for half in range(2):
            cols = slice(half * 512, (half + 1) * 512)
            e = dve.then(v.scalar_tensor_tensor, y[:, bass.ds(q, 1), cols].rearrange("p o n -> p (o n)"), k.xc_sel(q, cols), dcol,
                         y_banks[half].ap, ALU.mult, ALU.add)
            y_banks[half].release(e)
    ge = act.run(s.activation, y, y, ACT.Gelu_apprx_tanh, after=[dve.last])
    for c in range(2):
        for half in range(2):
            cols = slice(half * 512, (half + 1) * 512)
            bank = k.bank()
            m = k.product(bank.ap, [(glu[:, kc, c * P:(c + 1) * P], y[:, kc, cols]) for kc in range(2)], after=[ge, got_glu])
            e = act.run(s.activation, gs[:, c, cols], bank.ap, ACT.Sigmoid, bias=k.cols[:, 50 + c:51 + c], after=[m])
            bank.release(e)
    dve.run(v.tensor_tensor, k.yT[:, 6:8, :], y, gs, ALU.mult, after=[e])
    g.join()


def output_and_route(k):
    g, nc, d = k.g, k.g.nc, k.dram
    dve, act, pe, pool, v, s, gp = g.dve, g.act, g.pe, g.pool, nc.vector, nc.scalar, nc.gpsimd
    A = Area(k.arena)
    A.skip(KC * S)
    x = A.take(NT, D)
    w = A.take(KC, D)
    yt, ysq = A.take(KC, P), A.take(5, P)
    hn, hnT, gain = A.take(D), A.take(KC, P), A.take(D)
    wr = A.take(KC, LOGITS)
    br = A.take(LOGITS)
    lg = A.take(NT, LOGITS)
    cnt = A.take(NE)
    k.x2 = x
    hot = k.small[:, 256:256 + NT * 2 * NE].rearrange("p (t a e) -> p t a e", t=NT, a=2)
    rank = k.small[:, 512:512 + 2 * NT].rearrange("p (t a) -> p t a", a=2)
    gate = k.small[:, 544:544 + 2 * NT].rearrange("p (t a) -> p t a", a=2)
    k.hot, k.rank, k.gates, k.cnt = hot, rank, gate, cnt
    came_w = k.channel("w_out2_in").start(g.act, w, d["w_out_2"][0].rearrange("(k p) n -> p k n", p=P))
    came_x = k.channel("x_all_in").start(g.act, x, d["x_res"][0:S].rearrange("(t p) n -> p t n", p=P))
    ch = k.channel("w_route_in")
    ch.start(g.act, gain, d["norm_ffn_g_2"][0].partition_broadcast(P))
    ch.start(g.act, wr[:, :, 0:NG], d["router_group_w_2"][0].rearrange("(k p) n -> p k n", p=P))
    for n in range(NG):
        ch.start(g.act, wr[:, :, NG + n * EPG:NG + (n + 1) * EPG], d["router_expert_w_2"][0, n].rearrange("(k p) n -> p k n", p=P))
    ch.start(g.act, br[:, 0:NG], d["router_group_b_2"][0].partition_broadcast(P))
    got = ch.start(g.act, br[:, NG:], d["router_expert_b_2"][0].rearrange("a b -> (a b)").partition_broadcast(P))
    z = dve.run(v.memset, cnt, 0.0)
    pe.wait(came_w, got)
    dve.wait(came_x, got, z)
    st = k.stat
    ones = k.c(K_ONE, 1)
    with g.loop("outs2", NT) as t:
        sl = bass.ds(t * P, P)
        sq = act.run(s.activation, ysq, k.yT[:, 3:8, sl], ACT.Square, after=g.before("ysq_read"))
        for c in range(KC):
            cp = act.run(s.activation, yt[:, c, :], k.yT[:, c, sl], ACT.Copy, scale=k.cols[:, 8 + c:9 + c], after=g.before("yt_read"))
        bn = k.bank()
        k.product(bn.ap[:, 0:1], [(ysq[:, c, :], ones) for c in range(0, 3)], after=[sq])
        m = k.product(bn.ap[:, 1:2], [(ysq[:, c, :], ones) for c in range(3, 5)])
        g.mark("ysq_read", m)
        c1 = dve.run(v.tensor_scalar, st[:, 0:1], bn.ap[:, 0:1], 1.0 / BW, EPS, ALU.mult, ALU.add, after=[m])
        c1 = dve.run(v.tensor_scalar, st[:, 1:2], bn.ap[:, 1:2], 1.0 / CW, EPS, ALU.mult, ALU.add)
        bn.release(c1)
        r_ = pool.run(gp.tensor_tensor, st[:, 0:2], st[:, 0:2], spread(k.c(K_MINUS_HALF, 1), P, 2), ALU.pow, after=[c1])
        xt = x[:, bass.ds(t, 1), :].rearrange("p a n -> p (a n)")
        pe.wait(cp)
        for half in range(2):
            cols = slice(half * 512, (half + 1) * 512)
            for seg, (lo, hi) in enumerate(((0, 3), (3, 6), (6, 8))):
                bank = k.bank()
                m = k.product(bank.ap, [(yt[:, c, :], w[:, c, cols]) for c in range(lo, hi)])
                if seg == 0:
                    e = dve.then(v.tensor_tensor, xt[:, cols], xt[:, cols], bank.ap, ALU.add, after=[m])
                else:
                    e = dve.then(v.scalar_tensor_tensor, xt[:, cols], bank.ap, st[:, seg - 1:seg], xt[:, cols], ALU.mult, ALU.add,
                                 after=[m, r_])
                bank.release(e)
        g.mark("yt_read", m)
        q = act.run(s.activation, hn, xt, ACT.Square, accum_out=st[:, 2:3], after=[e, *g.before("hn_read")])
        r_ = k.rsqrt_mean(st[:, 3:4], st[:, 2:3], D, after=[q])
        h_ = dve.run(v.scalar_tensor_tensor, hn, xt, st[:, 3:4], gain, ALU.mult, ALU.mult, after=[r_])
        sent = k.channel("hn_out").start(g.sp, d["hn"][sl, :], hn, after=[h_])
        for half in range(2):
            bank = k.bank()
            tt = k.turn([(bank.ap[:, j * P:(j + 1) * P], hn[:, (4 * half + j) * P:(4 * half + j + 1) * P]) for j in range(4)], after=[h_])
            e = act.run(s.activation, hnT[:, 4 * half:4 * half + 4, :].rearrange("p a n -> p (a n)"), bank.ap, ACT.Copy, after=[tt])
            bank.release(e)
        g.mark("hn_read", tt, sent)
        bl = k.bank()
        m = k.product(bl.ap[:, 0:LOGITS], [(hnT[:, c, :], wr[:, c, :]) for c in range(KC)], after=[e])
        e = dve.run(v.tensor_tensor, lg[:, bass.ds(t, 1), :].rearrange("p o n -> p (o n)"), bl.ap[:, 0:LOGITS], br, ALU.add, after=[m])
        bl.release(e)

    wide = lambda ap, n: spread(ap.unsqueeze(2), P, NT, n)
    iota4 = spread(k.c(K_IOTA, 4).unsqueeze(1), P, NT, 4)
    iota16 = spread(k.c(K_IOTA, NE).unsqueeze(1), P, NT, NE)
    gl = lg[:, :, 0:NG]
    ge = A.take(NT, NG, EPG)
    el, g_hot, e_hot, t4, t4b = (A.take(NT, 4) for _ in range(5))
    g_max, g_idx, g_sum, m1, m2, id1, id2, ex, den = (A.take(NT) for _ in range(9))

    def first_max(val, out_max, out_idx, out_hot, tmp):
        dve.then(v.tensor_reduce, out_max, val, AX.X, ALU.max)
        dve.then(v.tensor_tensor, tmp, val, wide(out_max, 4), ALU.is_equal)
        dve.then(v.scalar_tensor_tensor, tmp, tmp, -64.0, iota4, ALU.mult, ALU.add)
        dve.then(v.tensor_reduce, out_idx, tmp, AX.X, ALU.min)
        dve.then(v.tensor_scalar_add, out_idx, out_idx, 64.0)
        dve.then(v.tensor_tensor, out_hot, iota4, wide(out_idx, 4), ALU.is_equal)

    first_max(gl, g_max, g_idx, g_hot, t4)
    dve.then(v.tensor_tensor, t4, gl, wide(g_max, 4), ALU.subtract)
    x4 = act.run(s.activation, t4, t4, ACT.Exp, after=[dve.last])
    dve.then(v.tensor_reduce, g_sum, t4, AX.X, ALU.add, after=[x4])
    dve.then(v.tensor_tensor, ge, lg[:, :, NG:].rearrange("p t (g e) -> p t g e", g=NG),
             spread(g_hot.unsqueeze(3), P, NT, NG, EPG), ALU.mult)
    dve.then(v.tensor_tensor, t4, ge[:, :, 0, :], ge[:, :, 1, :], ALU.add)
    dve.then(v.tensor_tensor, t4b, ge[:, :, 2, :], ge[:, :, 3, :], ALU.add)
    dve.then(v.tensor_tensor, el, t4, t4b, ALU.add)
    first_max(el, m1, id1, e_hot, t4)
    dve.then(v.scalar_tensor_tensor, el, e_hot, -3.0e38, el, ALU.mult, ALU.add)
    first_max(el, m2, id2, e_hot, t4)
    dve.then(v.tensor_tensor, ex, m2, m1, ALU.subtract)
    x2 = act.run(s.activation, ex, ex, ACT.Exp, after=[dve.last])
    dve.then(v.tensor_scalar_add, den, ex, 1.0, after=[x2])
    dve.then(v.tensor_tensor, den, den, g_sum, ALU.mult)
    dve.then(v.reciprocal, den, den)
    dve.then(v.tensor_copy, gate[:, :, 0], den)
    dve.run(v.tensor_tensor, gate[:, :, 1], den, ex, ALU.mult)
    for n, ids in enumerate((id1, id2)):
        dve.then(v.scalar_tensor_tensor, ids, g_idx, float(EPG), ids, ALU.mult, ALU.add)
        dve.then(v.tensor_tensor, hot[:, :, n, :], iota16, wide(ids, NE), ALU.is_equal)
    multi, before_, after_ = A.take(NT, NE), A.take(NT, NE), A.take(2, NT, NE)
    both = dve.then(v.tensor_tensor, multi, hot[:, :, 0, :], hot[:, :, 1, :], ALU.add)
    bc = k.bank()
    flat = multi.rearrange("p t e -> p (t e)")
    k.product(bc.ap[:, 0:NT * NE], [(k.c(K_BEFORE), flat)], after=[both])
    m = k.product(bc.ap[:, NT * NE:2 * NT * NE], [(k.c(K_ONE), flat)])
    dve.then(v.tensor_copy, after_.rearrange("p a t e -> p (a t e)"), bc.ap[:, 0:2 * NT * NE], after=[m])
    bc.release(dve.last)
    for t in range(NT):
        dve.then(v.tensor_tensor, before_[:, t, :], after_[:, 0, t, :], cnt, ALU.add)
        dve.then(v.tensor_tensor, cnt, cnt, after_[:, 1, t, :], ALU.add)
    for n in range(2):
        dve.then(v.tensor_tensor, multi, hot[:, :, n, :], before_, ALU.mult)
        dve.then(v.tensor_reduce, rank[:, :, n], multi, AX.X, ALU.add)
    g.join(k.channel("hn_out"))


def placement(k):
    g, nc, d = k.g, k.g.nc, k.dram
    dve, act, pe, pool, v, s, gp = g.dve, g.act, g.pe, g.pool, nc.vector, nc.scalar, nc.gpsimd
    A = Area(k.arena)
    pad, end, start = A.take(NE), A.take(NE), A.take(NE)
    big = A.take(NT, 2, NE)
    blk = A.take(NB, NE)
    be = A.take(NB)
    dest = A.take(NT, 2)
    k.dest_i = nc.alloc_sbuf_tensor("dest_i", [P, NT, 2], I32)
    k.be_i = nc.alloc_sbuf_tensor("be_i", [P, NB], I32)
    tok_i = nc.alloc_sbuf_tensor("tok_i", [P, NT], I32)
    zero_i = nc.alloc_sbuf_tensor("zero_i", [P, NB + 2], I32)
    z = dve.run(v.memset, zero_i[:], 0)
    cleared = k.channel("tok_clear").start(g.sp, d["row_tok"].rearrange("(p n) o -> p (n o)", p=P), zero_i[:], after=[z])
    dve.then(v.tensor_scalar, pad, k.cnt, 1.0 / P, (P - 1) / P - 0.5 + 1.0 / 256, ALU.mult, ALU.add)
    dve.then(v.tensor_scalar_add, pad, pad, MAGIC)
    dve.then(v.tensor_scalar_add, pad, pad, -MAGIC)
    dve.then(v.tensor_scalar_mul, pad, pad, float(P))
    dve.then(v.tensor_tensor_scan, end, k.c(K_ONE, NE), pad, 0.0, ALU.mult, ALU.add)
    dve.then(v.tensor_tensor, start, end, pad, ALU.subtract)
    dve.then(v.tensor_tensor, big, k.hot, spread(start.unsqueeze(1).unsqueeze(1), P, NT, 2, NE), ALU.mult)
    dve.then(v.tensor_reduce, dest, big, AX.X, ALU.add)
    dve.then(v.tensor_tensor, dest, dest, k.rank, ALU.add)
    dve.then(v.tensor_copy, k.dest_i[:], dest)
    ti = dve.run(v.tensor_copy, tok_i[:], k.c(K_TOK, NT))
    dve.run(v.tensor_scalar_mul, be, k.c(K_IOTA, NB), float(P))
    dve.then(v.tensor_tensor, blk, spread(end.unsqueeze(1), P, NB, NE), spread(be.unsqueeze(2), P, NB, NE), ALU.is_le)
    dve.then(v.tensor_reduce, be, blk, AX.X, ALU.add)
    dve.then(v.tensor_scalar_min, be, be, float(NE - 1))
    b_ = dve.then(v.tensor_copy, k.be_i[:], be)
    for t in range(NT):
        for n in range(2):
            tab = k.channel("tok_out").scatter(pool, d["row_tok"], k.dest_i[:, t, n:n + 1], tok_i[:, t:t + 1],
                                               after=[cleared, b_, ti])
    k.table = tab
    g.sp.wait(b_)
    pool.wait(tab)
    g.sp.wait(tab)
    g.join()


def experts(k):
    g, nc, d = k.g, k.g.nc, k.dram
    dve, act, pe, pool, v, s, gp = g.dve, g.act, g.pe, g.pool, nc.vector, nc.scalar, nc.gpsimd
    A = Area(k.arena)
    big = A.take(3, 4096)
    A.skip(0)
    A2 = Area(k.arena)
    A2.skip(2 * KC * S)
    pieces = [k.arena[:, 0:4096], k.arena[:, 4096:8192], A2.take(4096)]
    ring = k.big_ring(pieces)
    xg = [A2.take(D) for _ in range(2)]
    xT = [A2.take(KC, P) for _ in range(2)]
    sg, su = A2.take(D_EXP), A2.take(D_EXP)
    hT = A2.take(4, P)
    ys = [A2.take(D) for _ in range(2)]
    idx = [nc.alloc_sbuf_tensor(f"idx{n}", [P, 1], I32) for n in range(2)]
    wg, wu, wd = (d[n][0] for n in ("expert_w_gate_2", "expert_w_up_2", "expert_w_down_2"))
    def rows_of(blk, n, after=()):
        ci = k.channel(f"idx{n}_in").start(pool, idx[n][:], d["row_tok"][bass.ds(blk * P, P), :], after=after)
        return k.channel(f"rows{n}_in").gather(pool, xg[n], d["hn"], idx[n][:], after=[ci])

    def turn_rows(n, rows):
        for half in range(2):
            bank = k.bank()
            tt = k.turn([(bank.ap[:, j * P:(j + 1) * P], xg[n][:, (4 * half + j) * P:(4 * half + j + 1) * P]) for j in range(4)],
                        after=rows)
            e_ = dve.run(v.tensor_copy, xT[n][:, 4 * half:4 * half + 4, :].rearrange("p a n -> p (a n)"), bank.ap, after=[tt])
            bank.release(e_)
        return tt, e_

    _, e_ = turn_rows(0, [rows_of(0, 0)])
    pe.wait(e_)
    rows_of(1, 1)
    pe.wait(k.channel("rows1_in").count.now())
    pool.wait(pe.last)
    with g.loop("blocks", NB // 2) as b:
        for n in range(2):
            blk = 2 * b + n
            g.sp.settle()
            e = nc.sync.value_load(k.be_i[0:1, bass.ds(blk, 1)], min_val=0, max_val=NE - 1)
            load = lambda src, shape: k.load_from(ring, src, shape)
            s_g, v_g, in_g = load(wg[bass.ds(e, 1)].rearrange("o (k p) n -> p (o k) n", p=P), (KC, D_EXP))
            s_u, v_u, in_u = load(wu[bass.ds(e, 1)].rearrange("o (k p) n -> p (o k) n", p=P), (KC, D_EXP))
            s_d, v_d, in_d = load(wd[bass.ds(e, 1)].rearrange("o (k p) n -> p (o k) n", p=P), (4, D))
            rows = rows_of(blk + 2, n, after=g.before("rows0_read") if n == 0 else [rows1_read])
            bg = k.bank()
            m = k.product(bg.ap, [(xT[n][:, c, :], v_g[:, c, :]) for c in range(KC)], after=[in_g, *g.before(f"turned{n}")])
            s_g.release(m)
            sx = act.run(s.activation, sg, bg.ap, ACT.Silu, after=[m])
            bg.release(sx)
            bu = k.bank()
            m = k.product(bu.ap, [(xT[n][:, c, :], v_u[:, c, :]) for c in range(KC)], after=[in_u])
            s_u.release(m)
            hx = dve.run(v.tensor_tensor, su, sg, bu.ap, ALU.mult, after=[m, sx])
            bu.release(hx)
            act.wait(hx)
            if n == 0:
                tt, e1 = turn_rows(1, g.before("rows1_ready"))
                pe.wait(e1)
            else:
                tt, e1 = turn_rows(0, [rows0])
                g.mark("turned0", e1)
                g.mark("rows1_ready", rows)
                g.mark("rows0_read", tt)
            if n == 0:
                rows1_read, rows0 = tt, rows
            bank = k.bank()
            tt = k.turn([(bank.ap[:, j * P:(j + 1) * P], su[:, j * P:(j + 1) * P]) for j in range(4)], after=[hx])
            e_ = dve.run(v.tensor_copy, hT.rearrange("p a n -> p (a n)"), bank.ap, after=[tt])
            bank.release(e_)
            for half in range(2):
                cols = slice(half * 512, (half + 1) * 512)
                bank = k.bank()
                m = k.product(bank.ap, [(hT[:, c, :], v_d[:, c, cols]) for c in range(4)], after=[e_, in_d])
                o = dve.run(v.tensor_copy, ys[n][:, cols], bank.ap, after=[m, *g.before(f"ys{n}_sent")])
                bank.release(o)
            s_d.release(m)
            k.channel(f"ys{n}_out").start(g.act, d["ys"][bass.ds(blk * P, P), :], ys[n], after=[o])
            g.mark(f"ys{n}_sent", k.channel(f"ys{n}_out").count.now())
    g.join(k.channel("ys0_out"), k.channel("ys1_out"))


def combine(k):
    g, nc, d = k.g, k.g.nc, k.dram
    dve, act, pe, pool, v, s, gp = g.dve, g.act, g.pe, g.pool, nc.vector, nc.scalar, nc.gpsimd
    A = Area(k.arena)
    y1, y2 = A.take(2, D), A.take(2, D)
    gain, junk = A.take(D), A.take(D)
    A2 = Area(k.arena)
    got = k.channel("small2").start(g.act, gain, d["final_norm_g_2"].partition_broadcast(P))
    st = k.stat
    dve.wait(got)
    for t in range(NT):
        n = t % 2
        xt = k.x2[:, t, :]
        if t >= 2:
            pool.wait(used[t - 2])
        r1 = k.channel("y1_in").gather(pool, y1[:, n, :], d["ys"], k.dest_i[:, t, 0:1])
        r2 = k.channel("y2_in").gather(pool, y2[:, n, :], d["ys"], k.dest_i[:, t, 1:2])
        if t == 0:
            used, queue = [], []
        dve.run(v.scalar_tensor_tensor, xt, y1[:, n, :], k.gates[:, t, 0:1], xt, ALU.mult, ALU.add, after=[r1])
        a = dve.then(v.scalar_tensor_tensor, xt, y2[:, n, :], k.gates[:, t, 1:2], xt, ALU.mult, ALU.add, after=[r2])
        used.append(a)
        q = act.run(s.activation, junk, xt, ACT.Square, accum_out=st[:, 2 * n:2 * n + 1], after=[a])
        r_ = k.rsqrt_mean(st[:, 2 * n + 1:2 * n + 2], st[:, 2 * n:2 * n + 1], D, after=[q])
        o = dve.run(v.scalar_tensor_tensor, xt, xt, st[:, 2 * n + 1:2 * n + 2], gain, ALU.mult, ALU.mult, after=[r_])
        k.channel("out").start(g.sp, d["out"][0, t * P:(t + 1) * P, :], xt, after=[o])
    g.sp.wait(k.channel("out").count.now())


S, D, DEPTH = 1024, 1024, 2
NT, KC = S // P, D // P
GH, DK, DV, GR = 4, 64, 128, 16
MH, NOPE, ROPE, MV, QR, KVR = 4, 128, 64, 128, 256, 128
HALF_ROPE = ROPE // 2
D_FF = 4 * D
D_IN = 2 * GH * DK + 2 * GH * DV + GR + QR + KVR + ROPE
C_Q, C_K = 0, GH * DK
C_V = 2 * GH * DK
C_O = C_V + GH * DV
C_A = C_O + GH * DV
C_M = C_A + GR
EPS = 1e-6
TAU = 16.0
LEVELS = P.bit_length() - 1
MASKED = -1e30
TWO_PI = 2 * np.pi
MAGIC = 1.5 * 2.0 ** 23

K_ID, K_ONE = 0, P
K_LEVEL = 2 * P
K_CAUSAL = K_LEVEL + LEVELS * P
K_BEFORE = K_CAUSAL + P
K_FREQ = K_BEFORE + P
K_IOTA = K_FREQ + HALF_ROPE
K_TOK = K_IOTA + 32
K_MINUS_HALF = K_TOK + NT
K_END = K_MINUS_HALF + 1


def constants():
    c = np.zeros((P, K_END), np.float32)
    p, f = np.arange(P)[:, None], np.arange(P)[None, :]
    c[:, K_ID:K_ID + P] = p == f
    c[:, K_ONE:K_ONE + P] = 1.0
    for v in range(LEVELS):
        half = 2 ** v
        same = p // (2 * half) == f // (2 * half)
        c[:, K_LEVEL + v * P:K_LEVEL + (v + 1) * P] = same & (p // half % 2 == 0) & (f // half % 2 == 1)
    c[:, K_CAUSAL:K_CAUSAL + P] = np.where(f <= p, 0.0, MASKED)
    c[:, K_BEFORE:K_BEFORE + P] = p < f
    c[:, K_FREQ:K_FREQ + HALF_ROPE] = np.float32(10000.0) ** (-np.arange(0, ROPE, 2, dtype=np.float32) / np.float32(ROPE))
    c[:, K_IOTA:K_IOTA + 32] = np.arange(32)
    c[:, K_TOK:K_TOK + NT] = np.arange(NT)[None, :] * P + p
    c[:, K_MINUS_HALF] = -0.5
    return c


ARENA = 38300
FF_BUF = 2 * 2 * S + 4 * 512
HEAD_START = 400
CHANNELS = ("setup_in x_copy bias_in gains_in w_in_in x_in q_out o_out q_in att_out0 att_out1 w_out_in x_all_in mixed_in "
            "x_out out").split() + CHANNELS_2


class Kit:

    def __init__(self, g, dram):
        self.g, self.dram = g, dram
        nc = g.nc
        self.psum = nc.alloc_psum_tensor("psum", [P, 8, 512], F32)
        self.banks = Ring(g, "psum", [self.psum[:, b, :] for b in range(8)])
        self.weights = nc.alloc_sbuf_tensor("weight_ring", [P, 4, 2048], F32)
        self.ring = Ring(g, "weights", [self.weights[:, n, :] for n in range(4)],
                         [Channel(g, f"weights{n}_in") for n in range(4)])
        self.const = nc.alloc_sbuf_tensor("const", [P, K_END], F32)
        self.arena = nc.alloc_sbuf_tensor("arena", [P, ARENA], F32)
        self.scratch = nc.alloc_sbuf_tensor("scratch", [P, 1024], F32)
        self.stat = nc.alloc_sbuf_tensor("stat", [P, 64], F32)
        self.expert_channels = [Channel(g, f"expert{n}_in") for n in range(3)]
        self.channels = {name: Channel(g, name) for name in CHANNELS}

    def channel(self, name):
        return self.channels[name]

    def c(self, at, n=P):
        return self.const[:, at:at + n]

    def ident(self, n=P):
        return self.const[0:n, K_ID:K_ID + n]

    def load_weights(self, src, shape, extra=()):
        slot = self.ring.take()
        n = int(np.prod(shape))
        view = slot.ap[:, 0:n]
        if len(shape) == 2:
            view = view.rearrange("p (a b) -> p a b", b=shape[1])
        sp = self.g.sp
        sp.wait(*slot.free)
        return slot, view, slot.channel.start(sp, view, src, after=extra)

    def load_wide(self, src, shape):
        self.ring.align(2)
        one, two = self.ring.take(), self.ring.take()
        view = self.weights[:, one.n:one.n + 2, :].rearrange("p a b -> p (a b)").rearrange("p (a b) -> p a b", b=shape[1])
        return (one, two), view, one.channel.start(self.g.sp, view, src, after=[*one.free, *two.free])

    def load_from(self, ring, src, shape):
        slot = ring.take()
        view = slot.ap.rearrange("p (a b) -> p a b", b=shape[1])
        return slot, view, slot.channel.start(self.g.sp, view, src, after=slot.free)

    def big_ring(self, pieces):
        return Ring(self.g, "expert_weights", pieces, self.expert_channels)

    def bank_after(self, held):
        while self.banks.slots[self.banks.next % 8] in held:
            self.banks.next += 1
        return self.bank()

    def xc_sel(self, q, cols):
        return self.xc_in[:, bass.ds(q, 1), cols].rearrange("p o n -> p (o n)")

    def bank(self):
        slot = self.banks.take()
        self.g.pe.wait(*slot.free)
        return slot

    def bank_pair(self):
        self.banks.align(2)
        pair = [self.bank(), self.bank()]
        return pair, self.psum[:, pair[0].n:pair[0].n + 2, :]

    def release(self, slots, *counts):
        for slot in slots:
            slot.release(*counts)

    def product(self, out, pairs, after=(), start=True, stop=True):
        pe, nc = self.g.pe, self.g.nc
        pe.wait(*after)
        for n, (lhs, rhs) in enumerate(pairs):
            last = n == len(pairs) - 1
            (pe.run if last else pe.quiet)(nc.tensor.matmul, out, lhs, rhs, start=start and n == 0, stop=stop and last)
        return pe.last

    def turn(self, outs_ins, after=()):
        pe, nc = self.g.pe, self.g.nc
        pe.wait(*after)
        for n, (out, in_) in enumerate(outs_ins):
            last = n == len(outs_ins) - 1
            (pe.run if last else pe.quiet)(nc.tensor.transpose, out, in_, self.ident(in_.shape[0]),
                                         alone=in_.shape[0] < P or in_.shape[1] < P)
        return pe.last

    def rsqrt_mean(self, out, total, width, after=()):
        pool, gp = self.g.pool, self.g.nc.gpsimd
        pool.run(gp.tensor_scalar, out, total, 1.0 / width, EPS, ALU.mult, ALU.add, after=after, alone=True)
        return pool.then(gp.tensor_tensor, out, out, spread(self.c(K_MINUS_HALF, 1), P, out.shape[1]), ALU.pow)

    def silu_factor(self, out, in_, after=(), scale=-1.0):
        act, dve, nc = self.g.act, self.g.dve, self.g.nc
        e = act.run(nc.scalar.activation, out, in_, ACT.Exp, scale=scale, after=after)
        dve.run(nc.vector.tensor_scalar_add, out, out, 1.0, after=[e])
        return dve.then(nc.vector.reciprocal, out, out)


def spread(ap, *shape):
    return ap.broadcast_to(list(shape))


def sine(k, out, angle, shift, tmp, after=()):
    dve, v = k.g.dve, k.g.nc.vector
    turns, rest = tmp
    c1 = 6.28125
    c2 = float(np.float32(TWO_PI - c1))
    c3 = float(TWO_PI - c1 - c2)
    dve.run(v.tensor_scalar, turns, angle, 1.0 / TWO_PI, shift / TWO_PI, ALU.mult, ALU.add, after=after)
    dve.then(v.tensor_scalar_add, turns, turns, MAGIC)
    dve.then(v.tensor_scalar_add, turns, turns, -MAGIC)
    dve.then(v.scalar_tensor_tensor, rest, turns, -c1, angle, ALU.mult, ALU.add)
    dve.then(v.scalar_tensor_tensor, rest, turns, -c2, rest, ALU.mult, ALU.add)
    dve.then(v.scalar_tensor_tensor, rest, turns, -c3, rest, ALU.mult, ALU.add)
    dve.then(v.tensor_scalar_add, rest, rest, shift)
    r = dve.then(v.tensor_scalar, rest, rest, 3.1415925, -3.1415925, ALU.min, ALU.max)
    return k.g.act.run(k.g.nc.scalar.activation, out, rest, ACT.Sin, after=[r])


def setup(k):
    g, nc, d = k.g, k.g.nc, k.dram
    load = k.channel("setup_in")
    for e in (g.pe, g.act, g.dve, g.pool):
        e.api.sem_inc(e.count.sem, HEAD_START)
        e.count.step(HEAD_START)
    for name in ("q_out", "o_out", "att_out0", "att_out1", "x_out", "hn_out", "ys0_out", "ys1_out"):
        c = k.channel(name).count
        g.act.api.sem_inc(c.sem, 16)
        c.step(16)
    k.channel("x_copy").start(g.pool, d["x_res"][0:S], d["x"][0])
    copied = k.channel("x_copy").start(g.pool, d["x_res"][S:S + P], d["x"][0, 0:P])
    k.pos_i = nc.alloc_sbuf_tensor("pos_i", [P, NT], I32)
    k.cond = nc.alloc_sbuf_tensor("cond", [P, KC], F32)
    k.cos = nc.alloc_sbuf_tensor("cos", [P, NT, HALF_ROPE], F32)
    k.sin = nc.alloc_sbuf_tensor("sin", [P, NT, HALF_ROPE], F32)
    load.start(g.sp, k.const[:], d["const"])
    load.start(g.sp, k.pos_i[:], d["positions"][0].rearrange("(t p) -> p t", p=P), allow_slow_non_contiguous=True)
    here = load.start(g.sp, k.cond[:], d["c"][0].rearrange("(k p) -> p k", p=P), allow_slow_non_contiguous=True)
    k.ready = here
    pos = k.arena[:, 0:NT]
    ang = k.arena[:, 1024:1024 + NT * HALF_ROPE]
    tmp = [k.arena[:, o:o + NT * HALF_ROPE] for o in (2048, 3072)]
    g.dve.run(nc.vector.tensor_copy, pos, k.pos_i[:], after=[here])
    a = g.dve.then(nc.vector.tensor_tensor, ang.rearrange("p (t f) -> p t f", t=NT),
                   spread(pos.unsqueeze(2), P, NT, HALF_ROPE), spread(k.c(K_FREQ, HALF_ROPE).unsqueeze(1), P, NT, HALF_ROPE), ALU.mult)
    s1 = sine(k, k.sin[:].rearrange("p t f -> p (t f)"), ang, 0.0, tmp, after=[a])
    sine(k, k.cos[:].rearrange("p t f -> p (t f)"), ang, np.pi / 2, tmp, after=[s1])
    f = k.silu_factor(k.scratch[:, 0:KC], k.cond[:], after=[here])
    c = g.dve.then(nc.vector.tensor_tensor, k.cond[:], k.cond[:], k.scratch[:, 0:KC], ALU.mult)
    k.x_stored = copied
    k.mod = nc.alloc_sbuf_tensor("mod", [P, 2, 2, KC], F32)
    k.gate = nc.alloc_sbuf_tensor("gate", [P, 2, D], F32)
    k.small = nc.alloc_sbuf_tensor("small", [P, 1024], F32)
    g.join()


def modulation(k, layer):
    g, nc, d = k.g, k.g.nc, k.dram
    bias_rows = k.arena[0:48, 0:P]
    bias_cols = k.arena[:, 128:128 + 48]
    gate_bias = k.arena[:, 1024:1024 + 2 * D].rearrange("p (a n) -> p a n", a=2)
    ch = k.channel("bias_in")
    ch.start(g.act, bias_rows, d["b_ada"][layer].rearrange("(c p) -> c p", p=P))
    for n in range(2):
        b = ch.start(g.act, gate_bias[:, n, :], d["b_ada"][layer][(3 * n + 2) * D:(3 * n + 3) * D].partition_broadcast(P))
    bank = k.bank()
    t = k.turn([(bank.ap[:, 0:48], bias_rows)], after=[b])
    bank.release(g.dve.run(nc.vector.tensor_copy, bias_cols, bank.ap[:, 0:48], after=[t]))
    g.dve.wait(g.dve.last)
    w = d["w_ada"][layer].rearrange("(k p) n -> p k n", p=P)
    part_sum = [k.arena[:, 5120 + n * 512:5632 + n * 512] for n in range(2)]
    rows = k.arena[:, 6144:6144 + 4 * D].rearrange("p (a n) -> p a n", a=2)
    summed = [None, None]
    for part in range(2):
        for piece in range(6):
            n = piece % 2
            lo = part * 3 * D + piece * 512
            slots, view, came = k.load_wide(w[:, :, lo:lo + 512], (KC, 512))
            acc = part_sum[n]
            g.dve.run(nc.vector.tensor_scalar, acc, view[:, 0, :], k.cond[:, 0:1], None, ALU.mult, after=[came, summed[n]])
            for c in range(1, KC):
                e = g.dve.then(nc.vector.scalar_tensor_tensor, acc, view[:, c, :], k.cond[:, c:c + 1], acc, ALU.mult, ALU.add)
            k.release(slots, e)
            bank = k.bank()
            m = summed[n] = k.product(bank.ap, [(k.c(K_ONE), acc)], after=[e])
            if piece < 4:
                e = g.act.run(nc.scalar.activation, rows[:, part, piece * 512:(piece + 1) * 512], bank.ap, ACT.Copy, after=[m])
            else:
                out = slice((piece - 4) * 512, (piece - 3) * 512)
                e = g.dve.run(nc.vector.tensor_tensor, k.gate[:, part, out], bank.ap, gate_bias[:, part, out], ALU.add, after=[m])
            bank.release(e)
    for part in range(2):
        mod = k.mod[:, part, :, :].rearrange("p a c -> p (a c)")
        for n in range(4):
            bank = k.bank()
            t = k.turn([(bank.ap[:, j * P:(j + 1) * P], rows[:, part, (4 * n + j) * P:(4 * n + j + 1) * P]) for j in range(4)],
                       after=[g.act.last])
            at = part * 24 + 4 * n
            e = g.dve.run(nc.vector.tensor_tensor, mod[:, 4 * n:4 * n + 4], bank.ap[:, 0:512:P], bias_cols[:, at:at + 4], ALU.add,
                          after=[t])
            bank.release(e)
        g.dve.then(nc.vector.tensor_scalar_add, k.mod[:, part, 1, :], k.mod[:, part, 1, :], 1.0)
    g.join()


def normed(k, x, xn, stat, after=()):
    g, nc = k.g, k.g.nc
    ss, rstd = stat[:, 0:1], stat[:, 1:2]
    q = g.act.run(nc.scalar.activation, xn, x, ACT.Square, accum_out=ss, after=after)
    r = k.rsqrt_mean(rstd, ss, D, after=[q])
    return g.dve.run(nc.vector.tensor_scalar, xn, x, rstd, None, ALU.mult, after=[r])


def turned_in(k, xn, out, part, after=(), free=()):
    g, nc = k.g, k.g.nc
    done = []
    for half in range(2):
        bank = k.bank()
        t = k.turn([(bank.ap[:, j * P:(j + 1) * P], xn[:, (4 * half + j) * P:(4 * half + j + 1) * P]) for j in range(4)], after=after)
        for j in range(4):
            c = 4 * half + j
            src, dst = bank.ap[:, j * P:(j + 1) * P], out(c)
            if half == 0:
                e = g.dve.run(nc.vector.tensor_scalar, dst, src, k.mod[:, part, 1, c:c + 1], k.mod[:, part, 0, c:c + 1],
                              ALU.mult, ALU.add, after=[t, *free])
            else:
                e = g.act.run(nc.scalar.activation, dst, src, ACT.Identity, scale=k.mod[:, part, 1, c:c + 1],
                              bias=k.mod[:, part, 0, c:c + 1], after=[t, *free])
        bank.release(e)
        done.append(e)
    return t, done


def mixer_tiles(k, layer):
    g, nc, d = k.g, k.g.nc, k.dram
    dve, act, pe, pool, v, s, gp = g.dve, g.act, g.pe, g.pool, nc.vector, nc.scalar, nc.gpsimd
    A = Area(k.arena)
    w_qk, w_am = A.take(KC, 512), A.take(KC, GR + 448)
    kT = A.take(MH, S)
    kpeT = A.take(S)
    val = A.take(NT, MH * MV)
    k.kT, k.kpeT, k.val = kT, kpeT, val
    wq_up = A.take(2, MH * (NOPE + ROPE))
    wkv_up = A.take(MH * (NOPE + MV))
    w_gate = A.take(GH * DK)
    xt, xn = A.take(D), A.take(D)
    hT = A.take(KC, P)
    qk = A.take(4, P)
    ga = A.take(P)
    z, la, b = A.take(2, P), A.take(2, P), A.take(2, P)
    decay = A.take(LEVELS, 2, P)
    ql, kl = A.take(LEVELS, 2, P), A.take(LEVELS, 2, P)
    attn = A.take(GH, P)
    vt, go = A.take(GH * DV), A.take(GH * DV)
    eb, ebl = A.take(2, P), A.take(2, P)
    qe, kd, kdn = A.take(2, P), A.take(2, P), A.take(2, P)
    state = A.take(2, 2 * DV)
    o, o_sq = A.take(GH * DV), A.take(GH * DV)
    m_q = A.take(QR + KVR)
    mT = A.take(3, P)
    qh, tmp = A.take(MH * (NOPE + ROPE)), k.scratch[:, 0:MH * (NOPE + ROPE)]
    kn = A.take(MH * NOPE)
    pe_in, pe_rot = A.take(MH + 1, ROPE), A.take(MH + 1, ROPE)
    rt = A.take(2, MH + 1, HALF_ROPE)
    q_out, qpe_out = A.take(MH, P), A.take(MH, P)
    st = k.stat
    S_ = k.small
    qa_g, kva_g, qn_g, kn_g, bg = S_[:, 0:2], S_[:, 2:3], S_[:, 3:4], S_[:, 4:5], S_[:, 5:7]
    out_g = S_[:, 8:8 + DV]
    pe_g = S_[:, 256:256 + (MH + 1) * ROPE].rearrange("p (h r) -> p h r", r=ROPE)
    ch = k.channel("gains_in")
    def col(dst, name, n):
        return ch.start(g.act, dst, d[name][layer].rearrange("(k p) -> p k", p=n), allow_slow_non_contiguous=True)
    col(qa_g, "q_a_norm", P), col(kva_g, "kv_a_norm", P), col(qn_g, "q_norm_nope", P), col(kn_g, "k_norm_nope", P)
    col(bg, "b_gate", P)
    ch.start(g.act, out_g, d["gla_out_norm"][layer].partition_broadcast(P))
    for h in range(MH + 1):
        ch.start(g.act, pe_g[:, h, :], d["q_norm_rope" if h < MH else "k_norm_rope"][layer].partition_broadcast(P))
    ch.start(g.act, wq_up, d["w_q_up"][layer].rearrange("(k p) n -> p k n", p=P))
    ch.start(g.act, wkv_up, d["w_kv_up"][layer])
    small = ch.start(g.act, w_gate[0:GR], d["w_gate_up"][layer])
    wi = d["w_in"][layer].rearrange("(k p) n -> p k n", p=P)
    k.channel("w_in_in").start(g.act, w_qk, wi[:, :, 0:512])
    came_w = k.channel("w_in_in").start(g.act, w_am, wi[:, :, C_A:])
    v_slots, w_v, came_v = k.load_wide(wi[:, :, C_V:C_V + 512], (KC, 512))
    o_slots, w_o, came_o = k.load_wide(wi[:, :, C_O:C_O + 512], (KC, 512))
    zero = pool.run(gp.memset, state, 0.0)
    g.pe.wait(small, came_w, came_v, came_o)
    g.dve.wait(small, zero)
    g.act.wait(small)
    g.pe.wait(zero)

    def norm_tile(i, after=(), turned=()):
        x_in = k.channel("x_in").start(g.sp, xt, d["x_res"][bass.ds(i * P, P), :], after=after)
        return normed(k, xt, xn, st, after=[x_in, *turned])

    n0 = norm_tile(0, after=k.x_ready)
    _, first = turned_in(k, xn, lambda c: hT[:, c, :], 0, after=[n0])
    pe.wait(*first)
    g.sp.wait(n0)
    act.wait(n0, pe.last)
    with g.loop("tiles", NT) as t:
        pe.wait(*g.before("h_ready"))
        b_ga = k.bank()
        m = k.product(b_ga.ap[0:GR, 0:P], [(w_am[:, c, 0:GR], hT[:, c, :]) for c in range(KC)])
        e_ga = act.run(s.activation, ga[0:GR], b_ga.ap[0:GR, 0:P], ACT.Copy, after=[m])
        b_ga.release(e_ga)
        b_qk = k.bank()
        for j in range(4):
            m = k.product(b_qk.ap[:, j * P:(j + 1) * P], [(w_qk[:, c, j * P:(j + 1) * P], hT[:, c, :]) for c in range(KC)])
        e_q = act.run(s.activation, qk[:, 0:2, :], b_qk.ap[:, 0:256].rearrange("p (a b) -> p a b", a=2), ACT.Copy,
                      scale=DK ** -0.5, after=[m, *g.before("qk_read")])
        e_k = act.run(s.activation, qk[:, 2:4, :], b_qk.ap[:, 256:512].rearrange("p (a b) -> p a b", a=2), ACT.Copy)
        b_qk.release(e_k)
        b_z = k.bank()
        for gi in range(2):
            m = k.product(b_z.ap[:, gi * P:(gi + 1) * P], [(w_gate[0:GR, gi * P:(gi + 1) * P], ga[0:GR])], after=[e_ga])
        for gi in range(2):
            dve.run(v.tensor_scalar_add, z[:, gi, :], b_z.ap[:, gi * P:(gi + 1) * P], bg[:, gi:gi + 1], after=[m])
        b_z.release(dve.last)
        az = act.run(s.activation, la, z, ACT.Abs, after=[dve.last])
        dve.then(v.tensor_scalar, z, z, 0.0, None, ALU.min, after=[az])
        act.then(s.activation, la, la, ACT.Exp, scale=-1.0)
        ln = act.then(s.activation, la, la, ACT.Ln, bias=1.0)
        dve.then(v.tensor_tensor, la, z, la, ALU.subtract, after=[ln])
        dve.then(v.tensor_scalar_mul, la, la, 1.0 / TAU)
        for gi in range(2):
            dve.then(v.tensor_tensor_scan, b[:, gi, :], k.c(K_ONE), la[:, gi, :], 0.0, ALU.mult, ALU.add)
        for lv in range(LEVELS):
            half = 2 ** lv
            bb = b.rearrange("p g n -> p (g n)").rearrange("p (n a h) -> p n a h", a=2, h=half)
            dd = decay[:, lv].rearrange("p g n -> p (g n)").rearrange("p (n a h) -> p n a h", a=2, h=half)
            mid = spread(bb[:, :, 0, half - 1:half], P, P // half, half)
            (dve.then if lv == 0 else dve.run)(v.tensor_tensor, dd[:, :, 1, :], bb[:, :, 1, :], mid, ALU.subtract)
            last = dve.run(v.tensor_tensor, dd[:, :, 0, :], mid, bb[:, :, 0, :], ALU.subtract)
        for gi in range(2):
            last = dve.run(v.tensor_scalar, ebl[:, gi, :], b[:, gi, :], b[:, gi, P - 1:P], -1.0, ALU.subtract, ALU.mult)
        e_dec = act.run(s.activation, decay, decay, ACT.Exp, after=[last])
        e_b = act.run(s.activation, eb, b, ACT.Exp)
        e_bl = act.run(s.activation, ebl, ebl, ACT.Exp)
        read = g.before("levels_read")
        late = LEVELS - 2
        wide = lambda ap, n: spread(ap.unsqueeze(1), P, n, 2, P)
        kx_late = pool.run(gp.tensor_tensor, kl[:, late:], wide(qk[:, 2:4, :], 2), decay[:, late:], ALU.mult,
                           after=[e_dec, e_k, *read])
        dve.run(v.tensor_tensor, kl[:, 0:late], wide(qk[:, 2:4, :], late), decay[:, 0:late], ALU.mult, after=[e_dec, e_q, e_k, *read])
        qx = dve.run(v.tensor_tensor, ql, wide(qk[:, 0:2, :], LEVELS), decay, ALU.mult)
        x1 = dve.run(v.tensor_tensor, kd, qk[:, 2:4, :], ebl, ALU.mult, after=[e_bl])
        x2 = dve.run(v.tensor_tensor, qe, qk[:, 0:2, :], eb, ALU.mult)
        g.mark("qk_read", x2, kx_late)
        b_v = k.bank()
        m_v = k.product(b_v.ap, [(hT[:, c, :], w_v[:, c, :]) for c in range(KC)])
        e_v = act.run(s.activation, vt, b_v.ap, ACT.Copy, after=[m_v])
        b_v.release(e_v)
        b_m = k.bank()
        m = k.product(b_m.ap[:, 0:448], [(hT[:, c, :], w_am[:, c, GR:GR + 448]) for c in range(KC)])
        sq = act.run(s.activation, tmp[:, 0:QR], b_m.ap[:, 0:QR], ACT.Square, accum_out=st[:, 4:5], after=[m])
        sq = act.run(s.activation, tmp[:, QR:QR + KVR], b_m.ap[:, QR:QR + KVR], ACT.Square, accum_out=st[:, 5:6])
        e_pe = act.run(s.activation, pe_in[:, MH, :], b_m.ap[:, QR + KVR:448], ACT.Copy, after=g.before("pe_read"))
        k.rsqrt_mean(st[:, 4:5], st[:, 4:5], QR, after=[sq])
        r = k.rsqrt_mean(st[:, 5:6], st[:, 5:6], KVR)
        dve.run(v.tensor_scalar, m_q[:, 0:QR], b_m.ap[:, 0:QR], st[:, 4:5], None, ALU.mult, after=[e_pe, r])
        mq = dve.run(v.tensor_scalar, m_q[:, QR:QR + KVR], b_m.ap[:, QR:QR + KVR], st[:, 5:6], None, ALU.mult)
        b_m.release(mq)
        b_go = k.bank()
        m_go = k.product(b_go.ap, [(hT[:, c, :], w_o[:, c, :]) for c in range(KC)])
        act.run(s.activation, go, b_go.ap, ACT.Abs, after=[m_go, *g.before("go_read")])
        act.then(s.activation, go, go, ACT.Exp, scale=-1.0)
        ln = act.then(s.activation, go, go, ACT.Ln, bias=1.0)
        ls = dve.run(v.scalar_tensor_tensor, go, b_go.ap, 0.0, go, ALU.min, ALU.subtract, after=[ln])
        ex = act.run(s.activation, go, go, ACT.Exp, after=[ls])
        silu = dve.run(v.tensor_tensor, go, go, b_go.ap, ALU.mult, after=[ex])
        b_go.release(silu)
        b_mt = k.bank()
        tt = k.turn([(b_mt.ap[:, j * P:(j + 1) * P], m_q[:, j * P:(j + 1) * P]) for j in range(3)], after=[mq])
        for j in range(3):
            gain = qa_g[:, j:j + 1] if j < 2 else kva_g
            e_mt = act.run(s.activation, mT[:, j, :], b_mt.ap[:, j * P:(j + 1) * P], ACT.Copy, scale=gain, after=[tt])
        b_mt.release(e_mt)
        norm = norm_tile(t + 1, after=g.before("xt_read"), turned=g.before("xn_read"))
        g.mark("xt_read", norm)
        pair, sc4 = k.bank_pair()
        for gi in range(2):
            for a in range(2):
                r = slice(64 * a, 64 * a + 64)
                m = k.product(sc4[:, a, gi * P:(gi + 1) * P], [(qk[r, 2 + gi, :], qk[r, gi, :])], after=[e_k])
        g.mark("qk_read", x2, kx_late, m)
        attn4 = attn.rearrange("p (a g) n -> p a g n", a=2)
        both = [P, 2, 2, P]
        dve.run(v.tensor_tensor, attn4, sc4[:, :, 0:256].rearrange("p a (g n) -> p a g n", g=2),
                spread(k.c(K_ID).unsqueeze(1).unsqueeze(1), *both), ALU.mult, after=[m, *g.before("attn_read")])
        k.release(pair, dve.last)
        for lv in range(LEVELS):
            pair, sc4 = k.bank_pair()
            for gi in range(2):
                for a in range(2):
                    r = slice(64 * a, 64 * a + 64)
                    m = k.product(sc4[:, a, gi * P:(gi + 1) * P], [(kl[r, lv, gi, :], ql[r, lv, gi, :])], after=[qx] if lv < late else [qx, kx_late])
            mask = spread(k.c(K_LEVEL + lv * P).unsqueeze(1).unsqueeze(1), *both).bitcast(I32)
            sc = dve.then(v.copy_predicated, attn4, mask, sc4[:, :, 0:256].rearrange("p a (g n) -> p a g n", g=2), after=[m],
                          alone=True)
            k.release(pair, sc)
        g.mark("levels_read", m)
        pe.wait(e_mt)
        banks = [k.bank() for _ in range(2)]
        for n in range(2):
            m = k.product(banks[n].ap[:, 0:384], [(mT[:, c, :], wq_up[:, c, n * 384:(n + 1) * 384]) for c in range(2)])
            e = act.run(s.activation, qh[:, n * 384:(n + 1) * 384], banks[n].ap[:, 0:384], ACT.Copy, after=[m, *g.before("qh_read")])
            banks[n].release(e)
        sq = act.then(s.activation, tmp, qh, ACT.Square)
        q3, t3 = (x_.rearrange("p (h n) -> p h n", h=MH) for x_ in (qh, tmp))
        dve.run(v.tensor_reduce, st[:, 8:12], t3[:, :, 0:NOPE], AX.X, ALU.add, after=[sq])
        r = dve.run(v.tensor_reduce, st[:, 12:16], t3[:, :, NOPE:], AX.X, ALU.add)
        bkv = [k.bank() for _ in range(2)]
        for n in range(2):
            m = k.product(bkv[n].ap, [(mT[:, 2, :], wkv_up[:, n * 512:(n + 1) * 512])])
            kv = bkv[n].ap.rearrange("p (h n) -> p h n", h=2)
            dst = val[:, bass.ds(t, 1), n * 256:(n + 1) * 256].rearrange("p a (h n) -> p (a h) n", h=2)
            act.run(s.activation, dst, kv[:, :, NOPE:], ACT.Copy, after=[m])
            e = act.run(s.activation, kn[:, n * 256:(n + 1) * 256].rearrange("p (h n) -> p h n", h=2), kv[:, :, 0:NOPE], ACT.Copy,
                        after=g.before("kn_read"))
            bkv[n].release(e)
        g.mark("mT_read", m)
        e_kn = e
        sq1 = act.then(s.activation, tmp[:, 0:512], kn, ACT.Square, after=[r])
        sq2 = act.run(s.activation, tmp[:, 512:576], pe_in[:, MH, :], ACT.Square, accum_out=st[:, 20:21])
        dve.run(v.tensor_reduce, st[:, 16:20], tmp[:, 0:512].rearrange("p (h n) -> p h n", h=MH), AX.X, ALU.add, after=[sq1, sq2])
        dve.then(v.tensor_scalar, st[:, 8:12], st[:, 8:12], 1.0 / NOPE, EPS, ALU.mult, ALU.add)
        dve.run(v.tensor_scalar, st[:, 16:20], st[:, 16:20], 1.0 / NOPE, EPS, ALU.mult, ALU.add)
        dve.run(v.tensor_scalar, st[:, 12:16], st[:, 12:16], 1.0 / ROPE, EPS, ALU.mult, ALU.add)
        dve.run(v.tensor_scalar, st[:, 20:21], st[:, 20:21], 1.0 / ROPE, EPS, ALU.mult, ALU.add)
        r = pool.run(gp.tensor_tensor, st[:, 8:21], st[:, 8:21], spread(k.c(K_MINUS_HALF, 1), P, 13), ALU.pow, after=[dve.last])
        dve.run(v.tensor_tensor, q3[:, :, 0:NOPE], q3[:, :, 0:NOPE], spread(st[:, 8:12].unsqueeze(2), P, MH, NOPE), ALU.mult, after=[r])
        qn_ready = dve.last
        kn3 = kn.rearrange("p (h n) -> p h n", h=MH)
        kn_ready = dve.run(v.tensor_tensor, kn3, kn3, spread(st[:, 16:20].unsqueeze(2), P, MH, NOPE), ALU.mult, after=[e_kn])
        dve.run(v.tensor_tensor, pe_in[:, 0:MH, :], q3[:, :, NOPE:], spread(st[:, 12:16].unsqueeze(2), P, MH, ROPE), ALU.mult)
        dve.run(v.tensor_scalar, pe_in[:, MH, :], pe_in[:, MH, :], st[:, 20:21], None, ALU.mult)
        dve.then(v.tensor_tensor, pe_in, pe_in, pe_g, ALU.mult)
        cos = spread(k.cos[:, bass.ds(t, 1), :], P, MH + 1, HALF_ROPE)
        sin = spread(k.sin[:, bass.ds(t, 1), :], P, MH + 1, HALF_ROPE)
        lo, hi = slice(0, HALF_ROPE), slice(HALF_ROPE, ROPE)
        dve.then(v.tensor_tensor, pe_rot[:, :, lo], pe_in[:, :, lo], cos, ALU.mult, after=g.before("rot_read"))
        dve.run(v.tensor_tensor, rt[:, 0], pe_in[:, :, hi], sin, ALU.mult)
        dve.run(v.tensor_tensor, pe_rot[:, :, hi], pe_in[:, :, hi], cos, ALU.mult)
        dve.run(v.tensor_tensor, rt[:, 1], pe_in[:, :, lo], sin, ALU.mult)
        g.mark("pe_read", dve.last)
        dve.then(v.tensor_tensor, pe_rot[:, :, lo], pe_rot[:, :, lo], rt[:, 0], ALU.subtract)
        rot = dve.run(v.tensor_tensor, pe_rot[:, :, hi], pe_rot[:, :, hi], rt[:, 1], ALU.add)
        b_kd = k.bank()
        m = k.turn([(b_kd.ap[:, gi * P:(gi + 1) * P], kd[:, gi, :]) for gi in range(2)], after=[x1])
        e_kd = act.run(s.activation, kdn.rearrange("p g n -> p (g n)"), b_kd.ap[:, 0:256], ACT.Copy, after=[m])
        b_kd.release(e_kd)
        b_o = k.bank()
        pe.wait(x2, e_v, sc, *g.before("state_new"))
        for gi in range(2):
            k.product(b_o.ap[:, gi * 256:(gi + 1) * 256], [(qe[:, gi, :], state[:, gi, :])], stop=False)
            st_read = pe.last
            for h in (2 * gi, 2 * gi + 1):
                m_o = k.product(b_o.ap[:, h * DV:(h + 1) * DV], [(attn[:, 2 * (h % 2) + gi, :], vt[:, h * DV:(h + 1) * DV])], start=False,
                                stop=h % 2 == 1)
        g.mark("attn_read", m_o)
        b_s = k.bank()
        for gi in range(2):
            m_s = k.product(b_s.ap[:, gi * 256:(gi + 1) * 256], [(kdn[:, gi, :], vt[:, gi * 256:(gi + 1) * 256])], after=[e_kd])
        for gi in range(2):
            for a in range(2):
                r, cc = slice(64 * a, 64 * a + 64), slice(DV * a, DV * a + DV)
                sn = dve.run(v.scalar_tensor_tensor, state[r, gi, cc], state[r, gi, cc], eb[r, gi, P - 1:P],
                             b_s.ap[r, gi * 256 + DV * a:gi * 256 + DV * a + DV], ALU.mult, ALU.add, after=[m_s, st_read, e_b])
        g.mark("state_new", sn)
        b_s.release(sn)
        sq = act.run(s.activation, o_sq, b_o.ap, ACT.Square, after=[m_o])
        dve.run(v.tensor_reduce, st[:, 24:28], o_sq.rearrange("p (h n) -> p h n", h=GH), AX.X, ALU.add, after=[sq])
        r = k.rsqrt_mean(st[:, 24:28], st[:, 24:28], DV, after=[dve.last])
        o3, go3 = (x_.rearrange("p (h n) -> p h n", h=GH) for x_ in (o, go))
        dve.then(v.tensor_tensor, o3, b_o.ap.rearrange("p (h n) -> p h n", h=GH), spread(st[:, 24:28].unsqueeze(2), P, GH, DV),
                 ALU.mult, after=[r, *g.before("o_sent")])
        b_o.release(dve.last)
        dve.then(v.tensor_tensor, o3, o3, spread(out_g.unsqueeze(1), P, GH, DV), ALU.mult)
        of = dve.then(v.tensor_tensor, o, o, go, ALU.mult, after=[silu])
        g.mark("go_read", of)
        k.channel("o_out").start(g.sp, d["mixed"][bass.ds(t * P, P), 0:512], o, after=[of])
        g.mark("o_sent", k.channel("o_out").count.now())
        turned, h_ready = turned_in(k, xn, lambda c: hT[:, c, :], 0, after=[norm], free=[m_go])
        g.mark("xn_read", turned)
        g.mark("h_ready", *h_ready)
        bt = k.bank()
        m = k.turn([(bt.ap[:, h * P:(h + 1) * P], q3[:, h, 0:NOPE]) for h in range(MH)], after=[qn_ready])
        g.mark("qh_read", m, rot)
        e1 = act.run(s.activation, q_out.rearrange("p h n -> p (h n)"), bt.ap, ACT.Copy, scale=qn_g, after=[m, *g.before("q_sent")])
        bt.release(e1)
        bt = k.bank()
        m = k.turn([(bt.ap[:, h * P:(h + 1) * P], kn3[:, h, :]) for h in range(MH)], after=[kn_ready])
        g.mark("kn_read", m)
        e = act.run(s.activation, kT[:, :, bass.ds(t * P, P)], bt.ap.rearrange("p (h n) -> p h n", h=MH), ACT.Copy,
                    scale=kn_g, after=[m])
        bt.release(e)
        bt = k.bank()
        m = k.turn([(bt.ap[0:ROPE, h * P:(h + 1) * P], pe_rot[:, h, :]) for h in range(MH)], after=[rot])
        e2 = act.run(s.activation, qpe_out[0:ROPE].rearrange("p h n -> p (h n)"), bt.ap[0:ROPE], ACT.Copy, after=[m])
        bt.release(e2)
        bt = k.bank()
        m = k.turn([(bt.ap[0:ROPE, 0:P], pe_rot[:, MH, :])])
        g.mark("rot_read", m)
        e = act.run(s.activation, kpeT[0:ROPE, bass.ds(t * P, P)], bt.ap[0:ROPE, 0:P], ACT.Copy, after=[m])
        bt.release(e)
        k.channel("q_out").start(g.sp, d["q_all"][:, :, bass.ds(t * P, P)].rearrange("h p n -> p h n"), q_out, after=[e1, e2])
        k.channel("q_out").start(g.sp, d["qpe_all"][:, :, bass.ds(t * P, P)].rearrange("h p n -> p h n"), qpe_out[0:ROPE])
        g.mark("q_sent", k.channel("q_out").count.now())
    for slot in (*v_slots, *o_slots):
        slot.release(pe.last)
    g.join(k.channel("o_out"), k.channel("q_out"))


def attention(k):
    g, nc, d = k.g, k.g.nc, k.dram
    dve, act, pe, v, s = g.dve, g.act, g.pe, nc.vector, nc.scalar
    A = Area(k.arena)
    A.skip(KC * (D_IN - 1024) + MH * S + S + NT * MH * MV)
    qT, qpeT = A.take(S), A.take(S)
    prob = [A.take(S) for _ in range(2)]
    probT = [A.take(NT, P) for _ in range(2)]
    out = [A.take(MV) for _ in range(2)]
    st = k.stat
    scale = float((NOPE + ROPE) ** -0.5)
    ch = k.channel("q_in")
    with g.loop("heads", MH) as h:
        after = [*g.before("q_read"), k.channel("q_out").count.now()]
        ch.start(g.sp, qT, d["q_all"][bass.ds(h, 1)].rearrange("a p n -> p (a n)"), after=after)
        q_in = ch.start(g.sp, qpeT[0:ROPE], d["qpe_all"][bass.ds(h, 1)].rearrange("a p n -> p (a n)"))
        pe.wait(q_in)
        sent = [[], []]
        for n in range(2):
            sent[n] = g.before(f"att_out{n}")
        pv_read = [g.before(f"probT_read{n}") for n in range(2)]
        exp_read = [g.before(f"prob_read{n}") for n in range(2)]

        def scores(qt):
            w = (qt + 1) * P
            pair, sc = k.bank_pair()
            sc = sc.rearrange("p a b -> p (a b)")
            for lo in range(0, w, 512):
                hi = min(lo + 512, w)
                kh = k.kT[:, bass.ds(h, 1), lo:hi].rearrange("p a n -> p (a n)")
                m = k.product(sc[:, lo:hi], [(qT[:, qt * P:(qt + 1) * P], kh)], stop=False)
                m = k.product(sc[:, lo:hi], [(qpeT[0:ROPE, qt * P:(qt + 1) * P], k.kpeT[0:ROPE, lo:hi])], start=False)
            return pair, sc, m

        ready = scores(0)
        for qt in range(NT):
            pair, sc, m = ready
            w, b = (qt + 1) * P, qt % 2
            mx, sm = st[:, 32 + 4 * b:33 + 4 * b], st[:, 33 + 4 * b:34 + 4 * b]
            dve.run(v.tensor_tensor, sc[:, w - P:w], sc[:, w - P:w], k.c(K_CAUSAL), ALU.add, after=[m])
            dve.then(v.tensor_reduce, mx, sc[:, 0:w], AX.X, ALU.max, after=exp_read[b])
            dve.then(v.tensor_scalar_mul, mx, mx, -scale)
            e = act.run(s.activation, prob[b][:, 0:w], sc[:, 0:w], ACT.Exp, bias=mx, scale=scale, accum_out=sm,
                        after=[dve.last, *exp_read[b]])
            for x_ in pair:
                x_.release(e)
            rc = dve.run(v.reciprocal, sm, sm, after=[e])
            if qt + 1 < NT:
                ready = scores(qt + 1)
            for lo in range(0, qt + 1, 4):
                hi = min(lo + 4, qt + 1)
                bank = k.bank()
                t = k.turn([(bank.ap[:, (j - lo) * P:(j - lo + 1) * P], prob[b][:, j * P:(j + 1) * P]) for j in range(lo, hi)], after=[e])
                dst = probT[b][:, lo:hi, :].rearrange("p a n -> p (a n)")
                if lo == 0:
                    c = dve.run(v.tensor_copy, dst, bank.ap[:, 0:(hi - lo) * P], after=[t, *pv_read[b]])
                else:
                    c = act.run(s.activation, dst, bank.ap[:, 0:(hi - lo) * P], ACT.Copy, after=[t, *pv_read[b]])
                bank.release(c)
                pe.wait(c)
            bank = k.bank()
            m = k.product(bank.ap[:, 0:MV], [(probT[b][:, j, :], k.val[:, j, bass.ds(h * MV, MV)]) for j in range(qt + 1)])
            ot = act.run(s.activation, out[b], bank.ap[:, 0:MV], ACT.Copy, scale=sm, after=[m, rc, *sent[b]])
            bank.release(ot)
            sent[b] = [k.channel(f"att_out{b}").start(g.sp, d["mixed"][qt * P:(qt + 1) * P, bass.ds(512 + h * MV, MV)], out[b],
                                                      after=[ot])]
            pv_read[b], exp_read[b] = [m], [t, ot, dve.last]
        g.mark("q_read", pe.last)
        for n in range(2):
            g.mark(f"att_out{n}", *sent[n])
            g.mark(f"probT_read{n}", *pv_read[n])
            g.mark(f"prob_read{n}", *exp_read[n])
    g.join(k.channel("att_out0"), k.channel("att_out1"))


def output_and_norm(k, layer):
    g, nc, d = k.g, k.g.nc, k.dram
    dve, act, pe, v, s = g.dve, g.act, g.pe, nc.vector, nc.scalar
    A = Area(k.arena)
    x, hT = A.take(NT, D), A.take(KC, S)
    A.skip(FF_BUF)
    w = A.take(KC, D)
    mixed = [A.take(D) for _ in range(2)]
    mT, xn, tmp = A.take(KC, P), A.take(D), A.take(D)
    k.x, k.hT = x, hT
    came_w = k.channel("w_out_in").start(g.act, w, d["w_out"][layer].rearrange("(k p) n -> p k n", p=P))
    came_x = k.channel("x_all_in").start(g.act, x, d["x_res"][0:S].rearrange("(t p) n -> p t n", p=P), after=k.x_ready)
    pe.wait(came_w)
    dve.wait(came_x)
    act.wait(came_x)
    made = [k.channel(n).count.now() for n in ("o_out", "att_out0", "att_out1")]
    mm = mixed[0]
    with g.loop("outs", NT) as t:
        mi = k.channel("mixed_in").start(g.sp, mm, d["mixed"][bass.ds(t * P, P), :], after=[*g.before("mixed_read"), *made])
        for half in range(2):
            bank = k.bank()
            tt = k.turn([(bank.ap[:, j * P:(j + 1) * P], mm[:, (4 * half + j) * P:(4 * half + j + 1) * P]) for j in range(4)], after=[mi])
            e = act.run(s.activation, mT[:, 4 * half:4 * half + 4, :].rearrange("p a b -> p (a b)"), bank.ap, ACT.Copy,
                        after=[tt, *g.before("mT_read2")])
            bank.release(e)
        g.mark("mixed_read", tt)
        xt = x[:, bass.ds(t, 1), :].rearrange("p a n -> p (a n)")
        for half in range(2):
            bank = k.bank()
            m = k.product(bank.ap, [(mT[:, c, :], w[:, c, half * 512:(half + 1) * 512]) for c in range(KC)], after=[e])
            cols = slice(half * 512, (half + 1) * 512)
            dve.run(v.tensor_tensor, tmp[:, cols], bank.ap, k.gate[:, 0, cols], ALU.mult, after=[m])
            bank.release(dve.last)
            xs = dve.then(v.tensor_tensor, xt[:, cols], xt[:, cols], tmp[:, cols], ALU.add)
        g.mark("mT_read2", m)
        n_ = normed(k, xt, xn, k.stat, after=[xs, *g.before("xn_read2")])
        tt, _ = turned_in(k, xn, lambda c: hT[:, c, bass.ds(t * P, P)], 1, after=[n_])
        g.mark("xn_read2", tt)
    g.join()


def feed_forward(k, layer):
    g, nc, d = k.g, k.g.nc, k.dram
    dve, act, pe, v, s = g.dve, g.act, g.pe, nc.vector, nc.scalar
    A = Area(k.arena)
    x, hT = A.take(NT, D), A.take(KC, S)
    u = [A.take(2, S) for _ in range(2)]
    tmp = [A.take(512) for _ in range(4)]
    wu = d["w_mlp_up"][layer].rearrange("(k p) n -> p k n", p=P)
    wd = d["w_mlp_down"][layer].rearrange("(c k p) n -> c p k n", p=P, k=2)
    with g.loop("ff", D_FF // 512) as j:
        tn = 0
        for half in range(2):
            up, upv, up_in = k.load_weights(wu[:, :, bass.ds(j * 512 + half * 256, 256)], (KC, 256))
            down, downv, down_in = k.load_weights(wd[bass.ds(2 * j + half, 1)].rearrange("a p k n -> p (a k) n"), (2, D))
            pe.wait(up_in)
            for blk in range(2):
                for tok in range(2):
                    bank = k.bank()
                    cols = slice(tok * 512, (tok + 1) * 512)
                    m = k.product(bank.ap, [(upv[:, c, blk * P:(blk + 1) * P], hT[:, c, cols]) for c in range(KC)])
                    r = act.run(s.activation, u[half][:, blk, cols], bank.ap, ACT.Relu, after=[m, *g.before(f"u_read{half}")])
                    bank.release(r)
                    act.then(s.activation, u[half][:, blk, cols], u[half][:, blk, cols], ACT.Square)
            up.release(m)
            pe.wait(act.last, down_in)
            for t in range(NT):
                for n in range(2):
                    bank = k.bank()
                    cols = slice(n * 512, (n + 1) * 512)
                    m = k.product(bank.ap, [(u[half][:, c, t * P:(t + 1) * P], downv[:, c, cols]) for c in range(2)])
                    dve.run(v.tensor_tensor, tmp[tn % 4], bank.ap, k.gate[:, 1, cols], ALU.mult, after=[m])
                    bank.release(dve.last)
                    dve.then(v.tensor_tensor, x[:, t, cols], x[:, t, cols], tmp[tn % 4], ALU.add)
                    tn += 1
            down.release(m)
            g.mark(f"u_read{half}", m)
    k.channel("x_out").start(g.act, d["x_res"][0:S].rearrange("(t p) n -> p t n", p=P), x, after=[dve.last])
    g.join(k.channel("x_out"))


class Area:

    def __init__(self, arena):
        self.arena, self.at = arena, 0

    def skip(self, n):
        self.at += n

    def take(self, *shape):
        n = int(np.prod(shape))
        view = self.arena[:, self.at:self.at + n]
        self.at += n
        assert self.at <= ARENA, self.at
        names = " ".join(f"d{i}" for i in range(len(shape)))
        if len(shape) > 1:
            view = view.rearrange(f"p ({names}) -> p {names}", **{f"d{i}": w for i, w in enumerate(shape) if i})
        return view


def program(nc, d, known):
    g = Prog(nc, known)
    k = Kit(g, d)
    setup(k)
    with g.loop("layers", DEPTH) as layer:
        k.x_ready = [k.x_stored, *g.before("x_stored")]
        modulation(k, layer)
        mixer_tiles(k, layer)
        attention(k)
        output_and_norm(k, layer)
        feed_forward(k, layer)
        g.mark("x_stored", k.channel("x_out").count.now())
    second(k)
    return g.found


_SCRATCH = {"x_res": (S + P, D), "q_all": (MH, P, S), "qpe_all": (MH, ROPE, S), "mixed": (S, D), **SCRATCH_2}


def _declare(nc, arrays, mybir_):
    d = {n: nc.dram_tensor(f"in_{n}", a.shape, mybir_.dt.from_np(a.dtype), kind="ExternalInput").ap() for n, a in arrays.items()}
    for n, shape in _SCRATCH.items():
        kind = I32 if n in INT_SCRATCH else F32
        d[n] = nc.dram_tensor(f"tmp_{n}", shape, kind, kind="Internal").ap()
    d["out"] = nc.dram_tensor("out", (1, S, D), F32, kind="ExternalOutput").ap()
    return d


def kernel(**inputs):
    import numpy as _np
    import concourse.bacc as _bacc
    from concourse import mybir as _mybir
    from concourse.bass_utils import run_bass_kernel_spmd as _run

    arrays = {n: _np.ascontiguousarray(a) for n, a in inputs.items()}
    arrays["const"] = constants()
    known = {}
    for _ in range(2):
        nc = _bacc.Bacc("TRN2", target_bir_lowering=False, num_devices=1)
        known = program(nc, _declare(nc, arrays, _mybir), known)
    r = _run(nc, [{f"in_{n}": a for n, a in arrays.items()}], core_ids=[0])
    return r.results[0]["out"]
```

```python
import numpy as np

import concourse.bass as bass
from concourse import mybir

ALU = mybir.AluOpType
ACT = mybir.ActivationFunctionType
AX = mybir.AxisListType
F32 = mybir.dt.float32
F32R = mybir.dt.float32r
I32 = mybir.dt.int32
P = 128


class Loop:

    def __init__(self, name, reg, trips, per_trip):
        self.name, self.reg, self.trips, self.per_trip = name, reg, trips, per_trip


class Count:

    def __init__(self, owner, const, terms):
        self.owner, self.const, self.terms = owner, const, terms


class Counter:

    def __init__(self, prog, name):
        self.prog, self.name = prog, name
        self.sem = prog.nc.alloc_semaphore(name)
        self.const, self.terms, self.starts = 0, (), []
        prog.counters.append(self)

    def step(self, amount):
        self.const += amount
        return Count(self, self.const, self.terms)

    def now(self):
        return Count(self, self.const, self.terms)

    def enter(self, loop):
        per = self.prog.known.get((loop.name, self.name), 0)
        loop.per_trip[self.name] = per
        self.starts.append((self.const, self.terms))
        self.terms = self.terms + ((loop, per),)

    def leave(self, loop):
        const, terms = self.starts.pop()
        per = self.const - const
        self.prog.found[(loop.name, self.name)] = per
        self.const, self.terms = const + loop.trips * per, terms


class Engine:

    def __init__(self, prog, name, api):
        self.prog, self.api = prog, api
        self.count = Counter(prog, f"{name}_steps")
        self.last, self.seen, self.held = None, {}, False
        self.idle = prog.nc.alloc_semaphore(f"{name}_idle")

    def wait(self, *counts):
        for c in counts:
            if c is None:
                continue
            if isinstance(c, (list, tuple)):
                self.wait(*c)
                continue
            const, terms = self.prog.in_trip(c)
            key = (c.owner.name, tuple((l.name, p) for l, p in terms))
            if self.seen.get(key, -1) >= const:
                continue
            self.seen[key] = const
            if self.count.name == "sp_steps":
                self.settle()
            value = const
            for loop, per in terms:
                if per:
                    value, self.held = loop.reg * per + value, True
            self.api.wait_ge(c.owner.sem, value)

    def settle(self):
        if self.held:
            self.api.sem_inc(self.idle, 1)
        self.held = False

    def issue(self, instruction, *args, alone=False, **kw):
        if alone or any(type(a).__name__ == "AP" and a.regs_read for a in (*args, *kw.values())):
            self.settle()
        self.held = False
        return instruction(*args, **kw)

    def run(self, instruction, *args, after=(), **kw):
        self.wait(*after)
        self.issue(instruction, *args, **kw).then_inc(self.count.sem, 1)
        self.last = self.count.step(1)
        return self.last

    def then(self, instruction, *args, after=(), **kw):
        return self.run(instruction, *args, after=(self.last, *after), **kw)

    def quiet(self, instruction, *args, after=(), **kw):
        self.wait(*after)
        self.issue(instruction, *args, **kw)


class Channel:

    def __init__(self, prog, name):
        self.count = Counter(prog, name)

    def start(self, eng, out, in_, after=(), **kw):
        eng.wait(*after)
        if any(a.regs_read for a in (out, in_)):
            eng.settle()
        eng.held = False
        eng.api.dma_start(out, in_, **kw).then_inc(self.count.sem, 16)
        return self.count.step(16)

    def gather(self, eng, out, table, index, after=()):
        eng.wait(*after)
        eng.settle()
        eng.api.indirect_dma_start(out=out, out_offset=None, in_=table,
                                   in_offset=bass.IndirectOffsetOnAxis(ap=index, axis=0)).then_inc(self.count.sem, 16)
        return self.count.step(16)

    def scatter(self, eng, table, index, in_, after=()):
        eng.wait(*after)
        eng.settle()
        eng.api.indirect_dma_start(out=table, out_offset=bass.IndirectOffsetOnAxis(ap=index, axis=0), in_=in_,
                                   in_offset=None).then_inc(self.count.sem, 16)
        return self.count.step(16)


class Slot:

    def __init__(self, ring, n, ap, channel=None):
        self.ring, self.n, self.ap, self.channel = ring, n, ap, channel
        self.free, self.taken, self.held = [], False, False

    def release(self, *counts):
        self.free, self.held = list(counts), False


class Ring:

    def __init__(self, prog, name, aps, channels=None):
        self.prog, self.name, self.next = prog, name, 0
        self.slots = [Slot(self, n, ap, channels[n] if channels else None) for n, ap in enumerate(aps)]
        prog.rings.append(self)

    def take(self):
        slot = self.slots[self.next % len(self.slots)]
        self.next += 1
        assert not slot.held, f"{self.name}{slot.n} is taken before it is released"
        slot.taken = slot.held = True
        return slot

    def align(self, n):
        self.next = -(-self.next // n) * n


class Prog:
    def __init__(self, nc, known):
        self.nc, self.known, self.found = nc, known, {}
        self.counters, self.rings, self.loops = [], [], []
        self.pe = Engine(self, "pe", nc.tensor)
        self.act = Engine(self, "act", nc.scalar)
        self.dve = Engine(self, "dve", nc.vector)
        self.pool = Engine(self, "pool", nc.gpsimd)
        self.sp = Engine(self, "sp", nc.sync)
        self.engines = [self.pe, self.act, self.dve, self.pool, self.sp]

    def mark(self, name, *counts):
        self.found[("mark", name)] = [(c.owner.name, self.in_trip(c)[0]) for c in counts if c is not None]

    def in_trip(self, c):
        const, terms = c.const, []
        for loop, per in c.terms:
            if loop in self.loops:
                terms.append((loop, per))
            else:
                const += (loop.trips - 1) * self.found[(loop.name, c.owner.name)]
        return const, terms

    def before(self, name):
        out = []
        by_name = {c.name: c for c in self.counters}
        for owner, const in self.known.get(("mark", name), []):
            c = by_name[owner]
            loop = self.loops[-1]
            assert c.terms and c.terms[-1][0] is loop
            assert const - loop.per_trip[owner] > 0, (name, owner, const, loop.per_trip[owner])
            out.append(Count(c, const - loop.per_trip[owner], c.terms))
        return out

    def loop(self, name, trips):
        return _Body(self, name, trips)

    def join(self, *channels):
        engines = (self.pe, self.act, self.dve, self.pool)
        ends = [e.last for e in engines]
        for e in engines:
            e.wait(*ends, *[c.count.now() for c in channels])


class _Body:
    def __init__(self, prog, name, trips):
        self.prog, self.name, self.trips = prog, name, trips

    def __enter__(self):
        p = self.prog
        for ring in p.rings:
            writer = p.pe if ring.name == "psum" else p.sp
            for s in ring.slots:
                writer.wait(*s.free)
        for e in p.engines:
            e.settle()
        self.ctx = p.nc.Fori(0, self.trips)
        reg = self.ctx.__enter__()
        self.loop = Loop(self.name, reg, self.trips, {})
        for c in p.counters:
            c.enter(self.loop)
        p.loops.append(self.loop)
        self.saved = [dict(e.seen) for e in p.engines]
        for e in p.engines:
            e.seen = {}
            e.last = Count(e.count, e.count.const, e.count.terms)
        for r in p.rings:
            r.align(len(r.slots))
        self.outer = [[(s.free, s.taken) for s in r.slots] for r in p.rings]
        for ring in p.rings:
            for s in ring.slots:
                s.free, s.taken = p.before(f"{self.name}:{ring.name}{s.n}"), False
        return reg

    def __exit__(self, *exc):
        if exc[0] is not None:
            return False
        p = self.prog
        for ring, outer in zip(p.rings, self.outer):
            ring.align(len(ring.slots))
            for s, (free, taken) in zip(ring.slots, outer):
                if s.taken:
                    p.mark(f"{self.name}:{ring.name}{s.n}", *s.free)
                else:
                    s.free, s.taken = free, taken
        for e in p.engines:
            e.settle()
        p.loops.pop()
        self.ctx.__exit__(None, None, None)
        for c in p.counters:
            c.leave(self.loop)
        for e, seen in zip(p.engines, self.saved):
            e.seen = seen
            e.last = e.count.now()
        return False


AW, AH, HD = 384, 6, 64
BW, BC = 384, 3
CW, CG, CGD, CS = 256, 16, 16, 64
LRU_C = 8.0
NG, EPG = 4, 4
NE = NG * EPG
D_EXP = 512
TOP = 2
NB = 1024 * TOP // 128 + NE
NROWS = NB * 128
LOGITS = NG + NE
SCRATCH_2 = {"hn": (1024, 1024), "row_tok": (NROWS + 2 * 128, 1), "ys": (NROWS, 1024)}
INT_SCRATCH = ("row_tok",)
CHANNELS_2 = ("x2_in small2 small3 w_a_in b_in c_in lam_in w_out2_in hn_out tok_clear tok_out rows0_in rows1_in "
              "ys0_out ys1_out y1_in y2_in out0 w_route_in").split()


def second(k):
    spatial_gating(k)
    features_by_time(k)
    recurrence(k)
    state_space(k)
    output_and_route(k)
    placement(k)
    experts(k)
    combine(k)


def Areas2(k):
    A = Area(k.arena)
    k.yT = A.take(KC, S)
    k.hT2 = A.take(KC, S)
    return A


def spatial_gating(k):
    g, nc, d = k.g, k.g.nc, k.dram
    dve, act, pe, pool, v, s, gp = g.dve, g.act, g.pe, g.pool, nc.vector, nc.scalar, nc.gpsimd
    A = Areas2(k)
    w_a = A.take(KC, 2 * AW)
    xt, xn, hT = A.take(D), A.take(D), A.take(KC, P)
    wsT, ws = A.take(AH, P), A.take(AH, P)
    u, vv, junk, ya = A.take(AW), A.take(AW), A.take(AW), A.take(AW)
    vg = A.take(AW)
    rows = A.take(P)
    k.cols = k.small
    ch = k.channel("small2")
    C = k.cols

    def rows_to_cols(pieces):
        at = 0
        for src, n, col in pieces:
            got = ch.start(g.act, rows[at:at + n], src)
            at += n
        bank = k.bank()
        t = k.turn([(bank.ap[:, 0:at], rows[0:at])], after=[got])
        at = 0
        for src, n, col in pieces:
            e = dve.run(v.tensor_copy, C[:, col:col + n], bank.ap[:, at:at + n], after=[t])
            at += n
        bank.release(e)
        return e

    r = lambda name, n: d[name][0].rearrange("(k p) -> k p", p=P)
    cols = rows_to_cols([(r("norm_mix_g_2", 8), 8, 0), (r("mix_out_norm_g_2", 8), 8, 8), (d["a_spatial_b_2"][0], AH, 16),
                         (r("b_conv_b_2", 3), 3, 24), (r("b_rg_b_2", 3), 3, 27), (r("b_ig_b_2", 3), 3, 30),
                         (r("b_lambda_2", 3), 3, 33), (d["b_conv_w_2"][0].rearrange("w (k p) -> (w k) p", p=P), 12, 36),
                         (r("c_d_2", 2), 2, 48), (r("c_glu_b_2", 2), 2, 50)])
    ch = k.channel("small3")
    ch.start(g.act, vg, d["a_v_norm_g_2"][0].partition_broadcast(P))
    got = ch.start(g.act, ws, d["a_spatial_w_2"][0].rearrange("h i j -> i h j"))
    wi = d["w_in_2"][0].rearrange("(k p) n -> p k n", p=P)
    came_w = k.channel("w_a_in").start(g.act, w_a, wi[:, :, 0:2 * AW])
    for n in range(2):
        bank = k.bank()
        t = k.turn([(bank.ap[:, j * P:(j + 1) * P], ws[:, 3 * n + j, :]) for j in range(3)], after=[got])
        e = dve.run(v.tensor_copy, wsT[:, 3 * n:3 * n + 3, :].rearrange("p a n -> p (a n)"), bank.ap[:, 0:3 * P], after=[t])
        bank.release(e)
    hid = dve.then(v.memset, wsT[P // 2:P, :, 0:P // 2], 0.0)
    pe.wait(hid, came_w)
    act.wait(cols)
    stored = k.channel("x_out").count.now()
    st = k.stat

    def load_x(i, after=()):
        return k.channel("x2_in").start(g.sp, xt, d["x_res"][at(i, P), :], after=[*after, stored])

    def norm(x_in, free=()):
        q = act.run(s.activation, xn, xt, ACT.Square, accum_out=st[:, 0:1], after=[x_in, *free])
        r_ = k.rsqrt_mean(st[:, 1:2], st[:, 0:1], D, after=[q])
        return dve.run(v.tensor_scalar, xn, xt, st[:, 1:2], None, ALU.mult, after=[r_])

    def turn_in(i, normed_, free=()):
        for half in range(2):
            bank = k.bank()
            tt = k.turn([(bank.ap[:, j * P:(j + 1) * P], xn[:, (4 * half + j) * P:(4 * half + j + 1) * P]) for j in range(4)], after=normed_)
            e = dve.run(v.tensor_tensor, hT[:, 4 * half:4 * half + 4, :], bank.ap.rearrange("p (k n) -> p k n", k=4),
                        spread(C[:, 4 * half:4 * half + 4].unsqueeze(2), P, 4, P), ALU.mult, after=[tt, *free])
            bank.release(e)
        return tt, e, pool.run(gp.tensor_copy, k.hT2[:, :, at(i, P)], hT, after=[e])

    def features(made, free=()):
        bu = k.bank()
        m = k.product(bu.ap[:, 0:AW], [(hT[:, c, :], w_a[:, c, 0:AW]) for c in range(KC)], after=made)
        eu = act.run(s.activation, u, bu.ap[:, 0:AW], ACT.Gelu_apprx_tanh, after=[m, *free])
        bu.release(eu)
        bv = k.bank()
        m = k.product(bv.ap[:, 0:AW], [(hT[:, c, :], w_a[:, c, AW:]) for c in range(KC)])
        ev = act.run(s.activation, vv, bv.ap[:, 0:AW], ACT.Gelu_apprx_tanh, after=[m])
        bv.release(ev)
        return m, ev

    def norm_v():
        q = act.then(s.activation, junk, vv, ACT.Square, accum_out=st[:, 2:3])
        r_ = k.rsqrt_mean(st[:, 3:4], st[:, 2:3], AW, after=[q])
        return dve.run(v.scalar_tensor_tensor, vv, vv, st[:, 3:4], vg, ALU.mult, ALU.mult, after=[r_])

    def gate(vn, free=()):
        bs = k.bank()
        pe.wait(*vn)
        for h in range(AH):
            m = k.product(bs.ap[:, h * HD:(h + 1) * HD], [(wsT[:, h, :], vv[:, h * HD:(h + 1) * HD])])
        y3 = ya.rearrange("p (h n) -> p h n", h=AH)
        sv = dve.run(v.tensor_tensor, y3, bs.ap[:, 0:AW].rearrange("p (h n) -> p h n", h=AH),
                     spread(C[:, 16:16 + AH].unsqueeze(2), P, AH, HD), ALU.add, after=[m, *free])
        bs.release(sv)
        y = dve.then(v.tensor_tensor, ya, ya, u, ALU.mult)
        q = act.run(s.activation, junk, ya, ACT.Square, accum_out=st[:, 4:5], after=[y])
        r_ = k.rsqrt_mean(st[:, 5:6], st[:, 4:5], AW, after=[q])
        return m, y, dve.run(v.tensor_scalar, ya, ya, st[:, 5:6], None, ALU.mult, after=[r_])

    def put(i, y):
        by = k.bank()
        tt = k.turn([(by.ap[:, j * P:(j + 1) * P], ya[:, j * P:(j + 1) * P]) for j in range(3)], after=y)
        e = act.run(s.activation, k.yT[:, 0:3, at(i, P)], by.ap[:, 0:3 * P].rearrange("p (a n) -> p a n", a=3), ACT.Copy, after=[tt])
        by.release(e)
        return tt

    made = norm(load_x(0))
    tt, e, cp = turn_in(0, [made])
    m, ev = features([e])
    act.wait(made)
    x_in = load_x(1, [made])
    made = norm(x_in, [tt])
    vn = norm_v()
    tt, e, cp = turn_in(1, [made], [m, cp])
    pe.wait(vn, e)
    dve.wait(ev)
    g.sp.wait(made)
    with g.loop("tiles2", NT - 2) as t:
        x_in = load_x(t + 2, g.before("x2_read"))
        m_g, y_u, y = gate(g.before("v_normed"), g.before("ya_read"))
        act.wait(m_g, y_u)
        m, ev = features(g.before("h_made"))
        n_ = norm(x_in, g.before("xn2_read"))
        g.mark("x2_read", n_)
        g.mark("v_normed", norm_v())
        g.mark("ya_read", put(t, [y]))
        tt, e, cp = turn_in(t + 2, [n_], [m, *g.before("h_copied")])
        g.mark("h_copied", cp)
        g.mark("xn2_read", tt)
        g.mark("h_made", e)
    m_g, y_u, y = gate([dve.last], [pe.last])
    act.wait(m_g, y_u)
    features([dve.last])
    vn = norm_v()
    tt = put(NT - 2, [y])
    m_g, y_u, y = gate([vn], [tt])
    put(NT - 1, [y])
    g.join()


def features_by_time(k):
    g, nc, d = k.g, k.g.nc, k.dram
    dve, act, pe, v, s = g.dve, g.act, g.pe, nc.vector, nc.scalar
    A = Areas2(k)
    k.xc_in = A.take(2, S)
    k.xpad = A.take(BC, S + 3)
    k.gb = A.take(BC, S)
    k.area_b = A
    wi = d["w_in_2"][0].rearrange("(k p) n -> p k n", p=P)
    dve.run(v.memset, k.xpad[:, :, 0:3], 0.0)
    for piece in range(4):
        slot, view, came = k.load_weights(wi[:, :, 2 * AW + piece * 256:2 * AW + (piece + 1) * 256], (KC, 256))
        pe.wait(came)
        for blk in range(2):
            c = 2 * piece + blk
            for half in range(2):
                cols = slice(half * 512, (half + 1) * 512)
                bank = k.bank()
                m = k.product(bank.ap, [(view[:, kc, blk * P:(blk + 1) * P], k.hT2[:, kc, cols]) for kc in range(KC)])
                if c < BC:
                    e = dve.run(v.tensor_copy, k.xpad[:, c, 3 + half * 512:3 + (half + 1) * 512], bank.ap, after=[m])
                elif c < 2 * BC:
                    e = act.run(s.activation, k.gb[:, c - BC, cols], bank.ap, ACT.Gelu_apprx_tanh, after=[m])
                else:
                    e = dve.run(v.tensor_copy, k.xc_in[:, c - 2 * BC, cols], bank.ap, after=[m])
                bank.release(e)
        slot.release(m)
    g.join()


def recurrence(k):
    g, nc, d = k.g, k.g.nc, k.dram
    dve, act, pe, pool, v, s, gp = g.dve, g.act, g.pe, g.pool, nc.vector, nc.scalar, nc.gpsimd
    A = Area(k.arena)
    A.skip(KC * S)
    xc, r, = A.take(BC, S), A.take(BC, S)
    wr = A.take(2, BC, P)
    A2 = k.area_b
    i_ = A2.take(BC, S)
    h = A2.take(BC, S)
    C = k.cols
    neg = k.stat[:, 0:12]
    z = pool.run(gp.memset, wr, 0.0)
    for n, name in enumerate(("b_rg_w_2", "b_ig_w_2")):
        for a in range(2):
            got = k.channel("b_in").start(g.act, wr[64 * a:64 * a + 64, n, :, 64 * a:64 * a + 64],
                                          d[name][0].rearrange("(c a) i j -> a i c j", a=2)[a], after=[z])
    a1 = act.run(s.activation, neg[:, 6:9], C[:, 33:36], ACT.Abs)
    act.then(s.activation, neg[:, 6:9], neg[:, 6:9], ACT.Exp, scale=-1.0)
    a1 = act.then(s.activation, neg[:, 6:9], neg[:, 6:9], ACT.Ln, bias=1.0)
    dve.run(v.tensor_scalar, neg[:, 9:12], C[:, 33:36], -1.0, 0.0, ALU.mult, ALU.max)
    dve.then(v.tensor_tensor, neg[:, 6:9], neg[:, 6:9], neg[:, 9:12], ALU.add, after=[a1])
    ready = dve.then(v.tensor_scalar_mul, neg[:, 6:9], neg[:, 6:9], -LRU_C)
    for c in range(BC):
        dve.run(v.tensor_scalar, xc[:, c, :], k.xpad[:, c, 3:3 + S], C[:, 36 + 9 + c:37 + 9 + c], C[:, 24 + c:25 + c], ALU.mult, ALU.add)
        for w in range(3):
            x1 = dve.then(v.scalar_tensor_tensor, xc[:, c, :], k.xpad[:, c, w:w + S], C[:, 36 + 3 * w + c:37 + 3 * w + c], xc[:, c, :],
                          ALU.mult, ALU.add)
        pe.wait(x1, got)
        for n, out in enumerate((r, i_)):
            for half in range(2):
                cols = slice(half * 512, (half + 1) * 512)
                bank = k.bank()
                m = k.product(bank.ap, [(wr[:, n, c, :], xc[:, c, cols])])
                e = act.run(s.activation, out[:, c, cols], bank.ap, ACT.Sigmoid, bias=C[:, 27 + 3 * n + c:28 + 3 * n + c], after=[m])
                bank.release(e)
    ix = dve.run(v.tensor_tensor, i_, i_, xc, ALU.mult, after=[e])
    th = k.xpad[:, :, 0:S]
    for c in range(BC):
        act.run(s.activation, th[:, c, :], r[:, c, :], ACT.Tanh, scale=neg[:, 6 + c:7 + c], after=[ix, ready])
        act.then(s.activation, r[:, c, :], r[:, c, :], ACT.Exp, scale=neg[:, 6 + c:7 + c])
    act.then(s.activation, h, th, ACT.Ln, scale=-1.0, bias=1.0)
    e = act.then(s.activation, h, h, ACT.Exp, scale=-0.5)
    e2 = act.run(s.activation, th, th, ACT.Sqrt, scale=-2.0)
    dve.run(v.tensor_tensor, i_, i_, h, ALU.mult, after=[e])
    dve.then(v.tensor_tensor, i_, i_, th, ALU.mult, after=[e2])
    for c in range(BC):
        dve.then(v.tensor_tensor_scan, h[:, c, :], r[:, c, :], i_[:, c, :], 0.0, ALU.mult, ALU.add)
    dve.then(v.tensor_tensor, k.yT[:, 3:6, :], h, k.gb, ALU.mult)
    g.join()


def state_space(k):
    g, nc, d = k.g, k.g.nc, k.dram
    dve, act, pe, pool, v, s, gp = g.dve, g.act, g.pe, g.pool, nc.vector, nc.scalar, nc.gpsimd
    A = Area(k.arena)
    A.skip(KC * S)
    Bp, Cp = A.take(2, 4, P), A.take(2, 4, P)
    A.skip(KC * S - 2048)
    A.skip(2 * S)
    wide = A.take(2, S)
    gin = A.take(2, S)
    gs = A.take(2, S)
    pr = A.take(4, S)
    y = A.take(2, S)
    lam = A.take(24, 8)
    Bt, Ct = A.take(3, P), A.take(3, P)
    Bn = A.take(2, P)
    glu = A.take(2, CW)
    t1 = A.take(S)
    pw = A.take(2, 12)
    ar, ai, ldt, mag, th, cr, ci, nr, fr, fi, q1, q2 = (lam[:, n, :] for n in range(12))
    ch = k.channel("lam_in")
    for dst, name in ((ar, "c_a_re_2"), (ai, "c_a_im_2")):
        ch.start(g.act, dst, d[name][0].rearrange("(t a) p -> (a p) t", a=2), allow_slow_non_contiguous=True)
    for a in range(2):
        got = ch.start(g.act, ldt[64 * a:64 * a + 64],
                       d["c_log_dt_2"][0].rearrange("(t a) -> a t", a=2)[a].partition_broadcast(64), allow_slow_non_contiguous=True)
    got_glu = ch.start(g.act, glu, d["c_glu_w_2"][0].rearrange("(k p) n -> p k n", p=P))
    dt = act.run(s.activation, ldt, ldt, ACT.Exp, after=[got_glu])
    dve.run(v.tensor_tensor, mag, ar, ldt, ALU.mult, after=[dt])
    a0 = dve.run(v.tensor_tensor, th, ai, ldt, ALU.mult)
    a1 = act.run(s.activation, mag, mag, ACT.Exp, after=[a0])
    s1 = sine(k, ci, th, 0.0, (q1, q2), after=[a0, a1])
    s2 = sine(k, cr, th, np.pi / 2, (q1, q2), after=[s1])
    pr_, pi_ = A.take(11, 8), A.take(11, 8)
    dve.run(v.tensor_copy, pr_[:, 0, :], cr, after=[s2])
    dve.run(v.tensor_copy, pi_[:, 0, :], ci)
    for n in range(10):
        dve.then(v.tensor_tensor, q1, pr_[:, n, :], pr_[:, n, :], ALU.mult)
        dve.run(v.tensor_tensor, q2, pi_[:, n, :], pi_[:, n, :], ALU.mult)
        dve.run(v.scalar_tensor_tensor, pi_[:, n + 1, :], pr_[:, n, :], 2.0, pi_[:, n, :], ALU.mult, ALU.mult)
        dve.then(v.tensor_tensor, pr_[:, n + 1, :], q1, q2, ALU.subtract)
    dve.then(v.tensor_tensor, nr, mag, cr, ALU.mult)
    dve.then(v.tensor_scalar_add, nr, nr, -1.0)
    dve.run(v.tensor_tensor, th, mag, ci, ALU.mult)
    dve.then(v.tensor_tensor, fr, nr, ar, ALU.mult)
    dve.run(v.tensor_tensor, q1, th, ai, ALU.mult)
    dve.then(v.tensor_tensor, fr, fr, q1, ALU.add)
    dve.run(v.tensor_tensor, fi, th, ar, ALU.mult)
    dve.run(v.tensor_tensor, q2, nr, ai, ALU.mult)
    dve.then(v.tensor_tensor, fi, fi, q2, ALU.subtract)
    dve.run(v.tensor_tensor, q1, ar, ar, ALU.mult)
    dve.then(v.tensor_tensor, q2, ai, ai, ALU.mult)
    dve.then(v.tensor_tensor, q1, q1, q2, ALU.add)
    dve.then(v.reciprocal, q1, q1)
    dve.then(v.tensor_tensor, fr, fr, q1, ALU.mult)
    dve.run(v.tensor_tensor, fi, fi, q1, ALU.mult)
    z = pool.run(gp.memset, Bp, 0.0)
    z = pool.run(gp.memset, Cp, 0.0)
    with g.loop("halves", 2) as q:
        after = [z, *g.before("pads_read")]
        for n, nm in enumerate(("re", "im")):
            bsrc = d[f"c_b_{nm}_2"][0].rearrange("(q s a) p c -> a q p s c", s=4, a=2)
            csrc = d[f"c_c_{nm}_2"][0].rearrange("(q s a) c p -> s a q c p", s=4, a=2)
            for a in range(2):
                for sg in range(4):
                    got = k.channel("c_in").start(g.act, Bp[64 * a:64 * a + 64, n, sg, CGD * (2 * sg + a):CGD * (2 * sg + a) + CGD],
                                                  bsrc[a][bass.ds(q, 1), :, sg, :].rearrange("o p c -> (o p) c"), after=after)
                    lo = CGD * (2 * sg + a)
                    got = k.channel("c_in").start(g.act, Cp[lo:lo + CGD, n, sg, 64 * a:64 * a + 64],
                                                  csrc[sg, a][bass.ds(q, 1)].rearrange("o c p -> (o c) p"))
        k.banks.align(8)
        y_banks = [k.bank(), k.bank()]
        p1 = tail = None
        for sg in range(4):
            dve.wait(p1)
            col = lambda x: x[:, bass.ds(4 * q + sg, 1)]
            cfr, cfi = t1[:, 0:1], t1[:, 1:2]
            dve.then(v.tensor_copy, cfr, col(fr))
            dve.run(v.tensor_copy, cfi, col(fi))
            dve.run(v.tensor_copy, t1[:, 2:3], col(mag))
            dve.run(v.tensor_copy, t1[:, 4:15], pr_[:, :, bass.ds(4 * q + sg, 1)].rearrange("p a o -> p (a o)"))
            dve.run(v.tensor_copy, t1[:, 16:27], pi_[:, :, bass.ds(4 * q + sg, 1)].rearrange("p a o -> p (a o)"))
            dve.then(v.tensor_scalar, Bn[:, 0, :], Bp[:, 1, sg, :], cfi, None, ALU.mult, after=[got])
            dve.run(v.tensor_scalar, Bn[:, 1, :], Bp[:, 1, sg, :], cfr, None, ALU.mult)
            dve.then(v.scalar_tensor_tensor, Bn[:, 0, :], Bp[:, 0, sg, :], cfr, Bn[:, 0, :], ALU.mult, ALU.subtract)
            b_r = dve.run(v.scalar_tensor_tensor, Bn[:, 1, :], Bp[:, 0, sg, :], cfi, Bn[:, 1, :], ALU.mult, ALU.add)
            bank = k.bank()
            t = k.turn([(bank.ap[:, 0:P], Bn[:, 0, :]), (bank.ap[:, P:2 * P], Bn[:, 1, :]),
                        (bank.ap[:, 2 * P:3 * P], Cp[:, 0, sg, :]), (bank.ap[:, 3 * P:4 * P], Cp[:, 1, sg, :])], after=[b_r, got])
            b_t = act.run(s.activation, Bt[:, 0:2, :], bank.ap[:, 0:2 * P].rearrange("p (a n) -> p a n", a=2), ACT.Copy, after=[t])
            act.run(s.activation, Ct[:, 0, :], bank.ap[:, 2 * P:3 * P], ACT.Copy, after=[tail])
            act.run(s.activation, Ct[:, 1, :], bank.ap[:, 2 * P:3 * P], ACT.Copy, scale=-1.0)
            tb = act.run(s.activation, Ct[:, 2, :], bank.ap[:, 3 * P:4 * P], ACT.Copy, scale=-1.0)
            bank.release(tb)
            dve.run(v.memset, wide[:, 0, 0:1], 1.0)
            dve.run(v.memset, wide[:, 1, 0:1], 0.0)
            n = 1
            for lv in range(10):
                er, ei = wide[:, 0, 0:n], wide[:, 1, 0:n]
                wr_, wi_ = t1[:, 4 + lv:5 + lv], t1[:, 16 + lv:17 + lv]
                dve.then(v.tensor_scalar, wide[:, 0, n:2 * n], ei, wi_, None, ALU.mult)
                dve.run(v.tensor_scalar, wide[:, 1, n:2 * n], ei, wr_, None, ALU.mult)
                dve.then(v.scalar_tensor_tensor, wide[:, 0, n:2 * n], er, wr_, wide[:, 0, n:2 * n], ALU.mult, ALU.subtract)
                dve.run(v.scalar_tensor_tensor, wide[:, 1, n:2 * n], er, wi_, wide[:, 1, n:2 * n], ALU.mult, ALU.add)
                n *= 2
            for half in range(2):
                cols = slice(half * 512, (half + 1) * 512)
                bre, bim = k.bank_after(y_banks), k.bank_after(y_banks)
                x_ = k.xc_sel(q, cols)
                m = k.product(bre.ap, [(Bt[:, 0, :], x_)], after=[b_t])
                m = k.product(bim.ap, [(Bt[:, 1, :], x_)])
                cs, sn = wide[:, 0, cols], wide[:, 1, cols]
                dve.then(v.tensor_tensor, gin[:, 0, cols], bre.ap, cs, ALU.mult, after=[m])
                dve.run(v.tensor_tensor, pr[:, 0, cols], bim.ap, sn, ALU.mult, after=[m])
                dve.run(v.tensor_tensor, gin[:, 1, cols], bim.ap, cs, ALU.mult)
                e = dve.run(v.tensor_tensor, pr[:, 1, cols], bre.ap, sn, ALU.mult)
                bre.release(e)
                bim.release(e)
            dve.then(v.tensor_tensor, gin[:, 0, :], gin[:, 0, :], pr[:, 0, :], ALU.add)
            dve.run(v.tensor_tensor, gin[:, 1, :], gin[:, 1, :], pr[:, 1, :], ALU.subtract)
            m_ = spread(t1[:, 2:3], P, S)
            dve.then(v.tensor_tensor_scan, gs[:, 0, :], m_, gin[:, 0, :], 0.0, ALU.mult, ALU.add)
            sc = dve.run(v.tensor_tensor_scan, gs[:, 1, :], m_, gin[:, 1, :], 0.0, ALU.mult, ALU.add)
            cs, sn = wide[:, 0, :], wide[:, 1, :]
            p1 = pool.run(gp.tensor_tensor, pr[:, 0, :], gs[:, 0, :], cs, ALU.mult, after=[sc])
            dve.run(v.tensor_tensor, pr[:, 1, :], gs[:, 1, :], sn, ALU.mult, after=[sc])
            dve.run(v.tensor_tensor, pr[:, 2, :], gs[:, 0, :], sn, ALU.mult)
            p2 = dve.run(v.tensor_tensor, pr[:, 3, :], gs[:, 1, :], cs, ALU.mult)
            for half in range(2):
                cols = slice(half * 512, (half + 1) * 512)
                m = k.product(y_banks[half].ap, [(Ct[:, 0, :], pr[:, 0, cols]), (Ct[:, 1, :], pr[:, 1, cols]),
                                                 (Ct[:, 2, :], pr[:, 2, cols]), (Ct[:, 2, :], pr[:, 3, cols])],
                              after=[p1, p2, tb], start=sg == 0, stop=sg == 3)
            tail = m
        act.wait(m)
        dve.wait(m)
        g.mark("pads_read", m, b_r)
        dcol = t1[:, 32:33]
        dve.then(v.tensor_copy, dcol, k.cols[:, bass.ds(48 + q, 1)])
        for half in range(2):
            cols = slice(half * 512, (half + 1) * 512)
            e = dve.then(v.scalar_tensor_tensor, y[:, bass.ds(q, 1), cols].rearrange("p o n -> p (o n)"), k.xc_sel(q, cols), dcol,
                         y_banks[half].ap, ALU.mult, ALU.add)
            y_banks[half].release(e)
    ge = act.run(s.activation, y, y, ACT.Gelu_apprx_tanh, after=[dve.last])
    for c in range(2):
        for half in range(2):
            cols = slice(half * 512, (half + 1) * 512)
            bank = k.bank()
            m = k.product(bank.ap, [(glu[:, kc, c * P:(c + 1) * P], y[:, kc, cols]) for kc in range(2)], after=[ge, got_glu])
            e = act.run(s.activation, gs[:, c, cols], bank.ap, ACT.Sigmoid, bias=k.cols[:, 50 + c:51 + c], after=[m])
            bank.release(e)
    dve.run(v.tensor_tensor, k.yT[:, 6:8, :], y, gs, ALU.mult, after=[e])
    g.join()


def output_and_route(k):
    g, nc, d = k.g, k.g.nc, k.dram
    dve, act, pe, pool, v, s, gp = g.dve, g.act, g.pe, g.pool, nc.vector, nc.scalar, nc.gpsimd
    A = Area(k.arena)
    A.skip(KC * S)
    x = A.take(NT, D)
    w = A.take(KC, D)
    yt, ysq = A.take(KC, P), A.take(5, P)
    hn, hnT, gain = A.take(D), A.take(KC, P), A.take(D)
    wr = A.take(KC, LOGITS)
    br = A.take(LOGITS)
    lg = A.take(NT, LOGITS)
    cnt = A.take(NE)
    k.x2 = x
    hot = k.small[:, 256:256 + NT * 2 * NE].rearrange("p (t a e) -> p t a e", t=NT, a=2)
    rank = k.small[:, 512:512 + 2 * NT].rearrange("p (t a) -> p t a", a=2)
    gate = k.small[:, 544:544 + 2 * NT].rearrange("p (t a) -> p t a", a=2)
    k.hot, k.rank, k.gates, k.cnt = hot, rank, gate, cnt
    came_w = k.channel("w_out2_in").start(g.act, w, d["w_out_2"][0].rearrange("(k p) n -> p k n", p=P))
    came_x = k.channel("x_all_in").start(g.act, x, d["x_res"][0:S].rearrange("(t p) n -> p t n", p=P))
    ch = k.channel("w_route_in")
    ch.start(g.act, gain, d["norm_ffn_g_2"][0].partition_broadcast(P))
    ch.start(g.act, wr[:, :, 0:NG], d["router_group_w_2"][0].rearrange("(k p) n -> p k n", p=P))
    for n in range(NG):
        ch.start(g.act, wr[:, :, NG + n * EPG:NG + (n + 1) * EPG], d["router_expert_w_2"][0, n].rearrange("(k p) n -> p k n", p=P))
    ch.start(g.act, br[:, 0:NG], d["router_group_b_2"][0].partition_broadcast(P))
    got = ch.start(g.act, br[:, NG:], d["router_expert_b_2"][0].rearrange("a b -> (a b)").partition_broadcast(P))
    z = dve.run(v.memset, cnt, 0.0)
    pe.wait(came_w, got)
    act.wait(came_x)
    dve.wait(came_x, got, z)
    st = k.stat
    ones = k.c(K_ONE, 1)
    for c in range(KC):
        scaled = dve.run(v.tensor_scalar, w[:, c, :], w[:, c, :], k.cols[:, 8 + c:9 + c], None, ALU.mult, after=[came_w])
    pe.wait(scaled)

    def gather_branches(i, after=()):
        cp = act.run(s.activation, yt, k.yT[:, :, at(i, P)], ACT.Copy, after=after)
        return cp, act.run(s.activation, ysq, k.yT[:, 3:8, at(i, P)], ACT.Square)

    def branch_norms(sq, after=()):
        bn = k.bank()
        m = k.product(bn.ap[:, 0:1], [(ysq[:, c, :], ones) for c in range(0, 3)], after=[sq])
        m = k.product(bn.ap[:, 1:2], [(ysq[:, c, :], ones) for c in range(3, 5)])
        c1 = dve.run(v.tensor_scalar, st[:, 0:1], bn.ap[:, 0:1], 1.0 / BW, EPS, ALU.mult, ALU.add, after=[m, *after])
        c1 = dve.run(v.tensor_scalar, st[:, 1:2], bn.ap[:, 1:2], 1.0 / CW, EPS, ALU.mult, ALU.add)
        bn.release(c1)
        return m, pool.run(gp.tensor_tensor, st[:, 0:2], st[:, 0:2], spread(k.c(K_MINUS_HALF, 1), P, 2), ALU.pow, after=[c1])

    def residual(i, copied, norms):
        xt = x[:, at(i), :].rearrange("p a n -> p (a n)")
        pe.wait(*copied)
        for half in range(2):
            cols = slice(half * 512, (half + 1) * 512)
            for seg, (lo, hi) in enumerate(((0, 3), (3, 6), (6, 8))):
                bank = k.bank()
                m = k.product(bank.ap, [(yt[:, c, :], w[:, c, cols]) for c in range(lo, hi)])
                if seg == 0:
                    e = dve.then(v.tensor_tensor, xt[:, cols], xt[:, cols], bank.ap, ALU.add, after=[m])
                else:
                    e = dve.then(v.scalar_tensor_tensor, xt[:, cols], bank.ap, st[:, seg - 1:seg], xt[:, cols], ALU.mult, ALU.add,
                                 after=[m, *norms])
                bank.release(e)
        return m, e

    def norm(i, summed, free=()):
        xt = x[:, at(i), :].rearrange("p a n -> p (a n)")
        q = act.run(s.activation, hn, xt, ACT.Square, accum_out=st[:, 2:3], after=[summed, *free])
        r_ = k.rsqrt_mean(st[:, 3:4], st[:, 2:3], D, after=[q])
        h_ = dve.run(v.scalar_tensor_tensor, hn, xt, st[:, 3:4], gain, ALU.mult, ALU.mult, after=[r_])
        return h_, k.channel("hn_out").start(g.sp, d["hn"][at(i, P), :], hn, after=[h_])

    def turn_norm(ready, free=()):
        for half in range(2):
            bank = k.bank()
            tt = k.turn([(bank.ap[:, j * P:(j + 1) * P], hn[:, (4 * half + j) * P:(4 * half + j + 1) * P]) for j in range(4)], after=ready)
            e = act.run(s.activation, hnT[:, 4 * half:4 * half + 4, :].rearrange("p a n -> p (a n)"), bank.ap, ACT.Copy,
                        after=[tt, *free])
            bank.release(e)
        return tt, e

    def logits(i, turned):
        bl = k.bank()
        m = k.product(bl.ap[:, 0:LOGITS], [(hnT[:, c, :], wr[:, c, :]) for c in range(KC)], after=[turned])
        e = dve.run(v.tensor_tensor, lg[:, at(i), :].rearrange("p o n -> p (o n)"), bl.ap[:, 0:LOGITS], br, ALU.add, after=[m])
        bl.release(e)
        return m

    cp, sq = gather_branches(0)
    _, roots = branch_norms(sq)
    m, e = residual(0, [cp], [roots])
    cp, sq = gather_branches(1, [m])
    _, roots = branch_norms(sq, [e])
    h_, _ = norm(0, e)
    pe.wait(cp, h_)
    dve.wait(roots)
    with g.loop("outs2", NT - 2) as t:
        m, e = residual(t + 1, g.before("copied"), g.before("roots"))
        cp, sq = gather_branches(t + 2, [m, *g.before("squares_read")])
        tt, turned = turn_norm(g.before("hn_ready"), g.before("hnT_read"))
        m, roots = branch_norms(sq, [e])
        g.mark("copied", cp)
        g.mark("roots", roots)
        g.mark("squares_read", m)
        g.mark("hnT_read", logits(t, turned))
        h_, sent = norm(t + 1, e, [tt, *g.before("hn_sent")])
        g.mark("hn_ready", h_)
        g.mark("hn_sent", sent)
    h_, sent = g.dve.last, k.channel("hn_out").count.now()
    m, e = residual(NT - 1, [act.last], [pool.last])
    tt, turned = turn_norm([h_], [pe.last])
    logits(NT - 2, turned)
    h_, _ = norm(NT - 1, e, [tt, sent])
    _, turned = turn_norm([h_], [pe.last])
    logits(NT - 1, turned)

    wide = lambda ap, n: spread(ap.unsqueeze(2), P, NT, n)
    iota4 = spread(k.c(K_IOTA, 4).unsqueeze(1), P, NT, 4)
    iota16 = spread(k.c(K_IOTA, NE).unsqueeze(1), P, NT, NE)
    gl = lg[:, :, 0:NG]
    ge = A.take(NT, NG, EPG)
    el, g_hot, e_hot, t4, t4b = (A.take(NT, 4) for _ in range(5))
    g_max, g_idx, g_sum, m1, m2, id1, id2, ex, den = (A.take(NT) for _ in range(9))

    def first_max(val, out_max, out_idx, out_hot, tmp):
        dve.then(v.tensor_reduce, out_max, val, AX.X, ALU.max)
        dve.then(v.tensor_tensor, tmp, val, wide(out_max, 4), ALU.is_equal)
        dve.then(v.scalar_tensor_tensor, tmp, tmp, -64.0, iota4, ALU.mult, ALU.add)
        dve.then(v.tensor_reduce, out_idx, tmp, AX.X, ALU.min)
        dve.then(v.tensor_scalar_add, out_idx, out_idx, 64.0)
        dve.then(v.tensor_tensor, out_hot, iota4, wide(out_idx, 4), ALU.is_equal)

    first_max(gl, g_max, g_idx, g_hot, t4)
    dve.then(v.tensor_tensor, t4, gl, wide(g_max, 4), ALU.subtract)
    x4 = act.run(s.activation, t4, t4, ACT.Exp, after=[dve.last])
    dve.then(v.tensor_reduce, g_sum, t4, AX.X, ALU.add, after=[x4])
    dve.then(v.tensor_tensor, ge, lg[:, :, NG:].rearrange("p t (g e) -> p t g e", g=NG),
             spread(g_hot.unsqueeze(3), P, NT, NG, EPG), ALU.mult)
    dve.then(v.tensor_tensor, t4, ge[:, :, 0, :], ge[:, :, 1, :], ALU.add)
    dve.then(v.tensor_tensor, t4b, ge[:, :, 2, :], ge[:, :, 3, :], ALU.add)
    dve.then(v.tensor_tensor, el, t4, t4b, ALU.add)
    first_max(el, m1, id1, e_hot, t4)
    dve.then(v.scalar_tensor_tensor, el, e_hot, -3.0e38, el, ALU.mult, ALU.add)
    first_max(el, m2, id2, e_hot, t4)
    dve.then(v.tensor_tensor, ex, m2, m1, ALU.subtract)
    x2 = act.run(s.activation, ex, ex, ACT.Exp, after=[dve.last])
    dve.then(v.tensor_scalar_add, den, ex, 1.0, after=[x2])
    dve.then(v.tensor_tensor, den, den, g_sum, ALU.mult)
    dve.then(v.reciprocal, den, den)
    dve.then(v.tensor_copy, gate[:, :, 0], den)
    dve.run(v.tensor_tensor, gate[:, :, 1], den, ex, ALU.mult)
    for n, ids in enumerate((id1, id2)):
        dve.then(v.scalar_tensor_tensor, ids, g_idx, float(EPG), ids, ALU.mult, ALU.add)
        dve.then(v.tensor_tensor, hot[:, :, n, :], iota16, wide(ids, NE), ALU.is_equal)
    multi, before_, after_ = A.take(NT, NE), A.take(NT, NE), A.take(2, NT, NE)
    both = dve.then(v.tensor_tensor, multi, hot[:, :, 0, :], hot[:, :, 1, :], ALU.add)
    bc = k.bank()
    flat = multi.rearrange("p t e -> p (t e)")
    k.product(bc.ap[:, 0:NT * NE], [(k.c(K_BEFORE), flat)], after=[both])
    m = k.product(bc.ap[:, NT * NE:2 * NT * NE], [(k.c(K_ONE), flat)])
    dve.then(v.tensor_copy, after_.rearrange("p a t e -> p (a t e)"), bc.ap[:, 0:2 * NT * NE], after=[m])
    bc.release(dve.last)
    for t in range(NT):
        dve.then(v.tensor_tensor, before_[:, t, :], after_[:, 0, t, :], cnt, ALU.add)
        dve.then(v.tensor_tensor, cnt, cnt, after_[:, 1, t, :], ALU.add)
    for n in range(2):
        dve.then(v.tensor_tensor, multi, hot[:, :, n, :], before_, ALU.mult)
        dve.then(v.tensor_reduce, rank[:, :, n], multi, AX.X, ALU.add)
    g.join(k.channel("hn_out"))


def placement(k):
    g, nc, d = k.g, k.g.nc, k.dram
    dve, act, pe, pool, v, s, gp = g.dve, g.act, g.pe, g.pool, nc.vector, nc.scalar, nc.gpsimd
    A = Area(k.arena)
    pad, end, start = A.take(NE), A.take(NE), A.take(NE)
    big = A.take(NT, 2, NE)
    blk = A.take(NB + 1, NE)
    be = A.take(NB + 1)
    dest = A.take(NT, 2)
    k.dest_i = nc.alloc_sbuf_tensor("dest_i", [P, NT, 2], I32)
    k.be_i = nc.alloc_sbuf_tensor("be_i", [P, NB + 1], I32)
    tok_i = nc.alloc_sbuf_tensor("tok_i", [P, NT], I32)
    zero_i = nc.alloc_sbuf_tensor("zero_i", [P, NB + 2], I32)
    z = dve.run(v.memset, zero_i[:], 0)
    cleared = k.channel("tok_clear").start(g.sp, d["row_tok"].rearrange("(p n) o -> p (n o)", p=P), zero_i[:], after=[z])
    dve.then(v.tensor_scalar, pad, k.cnt, 1.0 / P, (P - 1) / P - 0.5 + 1.0 / 256, ALU.mult, ALU.add)
    dve.then(v.tensor_scalar_add, pad, pad, MAGIC)
    dve.then(v.tensor_scalar_add, pad, pad, -MAGIC)
    dve.then(v.tensor_scalar_mul, pad, pad, float(P))
    dve.then(v.tensor_tensor_scan, end, k.c(K_ONE, NE), pad, 0.0, ALU.mult, ALU.add)
    dve.then(v.tensor_tensor, start, end, pad, ALU.subtract)
    dve.then(v.tensor_tensor, big, k.hot, spread(start.unsqueeze(1).unsqueeze(1), P, NT, 2, NE), ALU.mult)
    dve.then(v.tensor_reduce, dest, big, AX.X, ALU.add)
    dve.then(v.tensor_tensor, dest, dest, k.rank, ALU.add)
    dve.then(v.tensor_copy, k.dest_i[:], dest)
    ti = dve.run(v.tensor_copy, tok_i[:], k.c(K_TOK, NT))
    dve.run(v.tensor_scalar_mul, be, k.c(K_IOTA, NB + 1), float(P))
    dve.then(v.tensor_tensor, blk, spread(end.unsqueeze(1), P, NB + 1, NE), spread(be.unsqueeze(2), P, NB + 1, NE), ALU.is_le)
    dve.then(v.tensor_reduce, be, blk, AX.X, ALU.add)
    dve.then(v.tensor_scalar_min, be, be, float(NE - 1))
    b_ = dve.then(v.tensor_copy, k.be_i[:], be)
    for t in range(NT):
        for n in range(2):
            tab = k.channel("tok_out").scatter(pool, d["row_tok"], k.dest_i[:, t, n:n + 1], tok_i[:, t:t + 1],
                                               after=[cleared, b_, ti])
    k.table = tab
    g.sp.wait(b_)
    pool.wait(tab)
    g.sp.wait(tab)
    g.join()


def experts(k):
    g, nc, d = k.g, k.g.nc, k.dram
    dve, act, pe, pool, v, s, gp = g.dve, g.act, g.pe, g.pool, nc.vector, nc.scalar, nc.gpsimd
    A = Area(k.arena)
    A.skip(2 * KC * S)
    half_matrix = KC * D_EXP // 2
    pieces = [k.arena[:, n * half_matrix:(n + 1) * half_matrix] for n in range(4)] + [A.take(half_matrix) for _ in range(2)]
    ring = Ring(g, "expert_weights", pieces, k.expert_channels)
    high = Ring(g, "expert_high", [k.weights[:, n, :] for n in range(4)])
    xg = [A.take(D) for _ in range(2)]
    x_hi, x_lo = ([k.rounded(A.take(KC, P)) for _ in range(2)] for _ in range(2))
    sg, su = [A.take(D_EXP) for _ in range(2)], A.take(D_EXP)
    h_hi, h_lo = (k.rounded(A.take(4, P)) for _ in range(2))
    ys = [A.take(D) for _ in range(2)]
    idx = [nc.alloc_sbuf_tensor(f"idx{n}", [P, 1], I32) for n in range(2)]
    wg, wu, wd = (d[n][0] for n in ("expert_w_gate_2", "expert_w_up_2", "expert_w_down_2"))

    tok_row, tok_col = k.scratch.bitcast(I32)[0:NB + 2, 0:P], k.scratch.bitcast(I32)[:, 2 * P:2 * P + NB + 2]
    tok = k.scratch[0:NB + 2, P:2 * P]
    src, some = d["row_tok"].rearrange("(b p) o -> b (p o)", p=P), (NB + 2) // 2
    came = [k.channel(f"ys{n}_out").start(pool, tok_row[n * some:(n + 1) * some], src[n * some:(n + 1) * some]) for n in range(2)]
    e = dve.run(v.tensor_copy, tok, tok_row, after=came)
    bank = k.bank()
    e = k.turn([(bank.ap[:, 0:NB + 2], tok)], after=[e])
    have_tok = dve.run(v.tensor_copy, tok_col, bank.ap[:, 0:NB + 2], after=[e])
    bank.release(have_tok)

    def rows_of(blk, n, after=()):
        column = tok_col[:, bass.ds(blk, 1)] if not isinstance(blk, int) else tok_col[:, blk:blk + 1]
        c = dve.run(v.tensor_copy, idx[n][:], column, after=[have_tok, *after])
        return k.channel(f"rows{n}_in").gather(pool, xg[n], d["hn"], idx[n][:], after=[c])

    def turn_rows(n, rows):
        for half in range(2):
            bank = k.bank()
            tt = k.turn([(bank.ap[:, j * P:(j + 1) * P], xg[n][:, (4 * half + j) * P:(4 * half + j + 1) * P]) for j in range(4)],
                        after=rows)
            hi, lo = (x_[n][:, 4 * half:4 * half + 4, :].rearrange("p a n -> p (a n)") for x_ in (x_hi, x_lo))
            e = act.run(s.activation, hi, bank.ap, ACT.Copy, after=[tt])
            e = dve.run(v.tensor_tensor, lo, bank.ap, hi.bitcast(F32), ALU.subtract, after=[e])
            bank.release(e)
        return tt, e

    def halves(w, e, rows):
        src = w[bass.ds(e, 1)].rearrange("o (k p) n -> p (o k) n", p=P)
        n = rows // P // 2
        return [k.load_from(ring, src[:, i * n:(i + 1) * n], (n, half_matrix // n)) for i in range(2)]

    def high_part(piece):
        slot, w, came = piece
        hi = high.take()
        view = k.rounded(hi.ap.rearrange("p (a b) -> p a b", b=w.shape[2]))
        made = act.run(s.activation, view, w, ACT.Copy, after=[came, *hi.free])
        return hi, view, made

    def low_part(eng, api, piece, hi):
        w = piece[1]
        return k.rounded(w), eng.run(api.tensor_tensor, k.rounded(w), w, hi[1].bitcast(F32), ALU.subtract, after=[hi[2]])

    def products(banks, parts, piece, hi, lo, after=(), between=lambda: None):
        r_hi, r_lo = parts
        n = hi[0][1].shape[1]
        pe.wait(*after)
        for i in range(2):
            pe.wait(hi[i][2])
            for b_, bank in enumerate(banks):
                cols = slice(b_ * 512, (b_ + 1) * 512)
                m = k.product(bank.ap, [(r[:, i * n + c, :], hi[i][1][:, c, cols]) for c in range(n) for r in (r_hi, r_lo)],
                              start=i == 0, stop=False)
            hi[i][0].release(m, lo[i][1])
        between()
        for i in range(2):
            for b_, bank in enumerate(banks):
                cols = slice(b_ * 512, (b_ + 1) * 512)
                m = k.product(bank.ap, [(r_hi[:, i * n + c, :], lo[i][0][:, c, cols]) for c in range(n)], after=[lo[i][1]],
                              start=False, stop=i == 1)
            piece[i][0].release(m)
        return m

    def expert_of(blk):
        g.sp.settle()
        return nc.sync.value_load(k.be_i[0:1, bass.ds(blk, 1)], min_val=0, max_val=NE - 1)

    def load_gate(e):
        gate_in = halves(wg, e, D)
        gate_hi = [high_part(p) for p in gate_in]
        return gate_in, gate_hi, [low_part(pool, gp, gate_in[0], gate_hi[0]), low_part(dve, v, gate_in[1], gate_hi[1])]

    def gated(n, gate, after, between=lambda: None):
        bg = k.bank()
        m = products([bg], (x_hi[n], x_lo[n]), *gate, after=after, between=between)
        sx = act.run(s.activation, sg[n], bg.ap, ACT.Silu, after=[m])
        bg.release(sx)
        return sx

    _, turned = turn_rows(0, [rows_of(0, 0)])
    rows_of(1, 1)
    sx = gated(0, load_gate(expert_of(0)), [turned])
    dve.wait(sx)
    pe.wait(k.channel("rows1_in").count.now())
    pool.wait(pe.last)
    with g.loop("blocks", NB // 2) as b:
        gate_ready, rows_ready = g.before("gated0"), g.before("rows1_ready")
        for n in range(2):
            blk, other = 2 * b + n, 1 - n
            e, e_next = expert_of(blk), expert_of(blk + 1)
            up_in = halves(wu, e, D)
            up_hi = [high_part(p) for p in up_in]
            up_lo = [low_part(dve, v, *p) for p in zip(up_in, up_hi)]
            rows_next = [rows_of(blk + 2, n, after=g.before("rows0_read") if n == 0 else rows_read)]
            tt, turned = turn_rows(other, rows_ready)
            rows_read, rows_ready = [tt], rows_next
            bu = k.bank()
            m = products([bu], (x_hi[n], x_lo[n]), up_in, up_hi, up_lo)
            hx = dve.run(v.tensor_tensor, su, sg[n], bu.ap, ALU.mult, after=[m, *gate_ready])
            bu.release(hx)
            gate = load_gate(e_next)
            down_in = halves(wd, e, D_EXP)
            down_hi = [high_part(p) for p in down_in]
            down_lo = [low_part(pool, gp, down_in[0], down_hi[0])]
            made = []

            def hidden():
                bank = k.bank()
                tt = k.turn([(bank.ap[:, j * P:(j + 1) * P], su[:, j * P:(j + 1) * P]) for j in range(4)], after=[hx])
                hi, lo = (x_.rearrange("p a n -> p (a n)") for x_ in (h_hi, h_lo))
                e_ = act.run(s.activation, hi, bank.ap, ACT.Copy, after=[tt])
                made.append(dve.run(v.tensor_tensor, lo, bank.ap, hi.bitcast(F32), ALU.subtract, after=[e_]))
                bank.release(made[0])

            gate_ready = [gated(other, gate, [turned], hidden)]
            down_lo.append(low_part(dve, v, down_in[1], down_hi[1]))
            banks = [k.bank(), k.bank()]
            m = products(banks, (h_hi, h_lo), down_in, down_hi, down_lo, after=made)
            for half, bank in enumerate(banks):
                o = dve.run(v.tensor_copy, ys[n][:, half * 512:(half + 1) * 512], bank.ap, after=[m, *g.before(f"ys{n}_sent")])
                bank.release(o)
            k.channel(f"ys{n}_out").start(pool, d["ys"][bass.ds(blk * P, P), :], ys[n], after=[o])
            g.mark(f"ys{n}_sent", k.channel(f"ys{n}_out").count.now())
        g.mark("gated0", *gate_ready)
        g.mark("rows1_ready", *rows_ready)
        g.mark("rows0_read", *rows_read)
    g.join(k.channel("ys0_out"), k.channel("ys1_out"))


def combine(k):
    g, nc, d = k.g, k.g.nc, k.dram
    dve, act, pe, pool, v, s, gp = g.dve, g.act, g.pe, g.pool, nc.vector, nc.scalar, nc.gpsimd
    A = Area(k.arena)
    y1, y2 = A.take(2, D), A.take(2, D)
    gain, junk = A.take(D), A.take(D)
    got = k.channel("small2").start(g.act, gain, d["final_norm_g_2"].partition_broadcast(P))
    st = k.stat
    dve.wait(got)
    for t in range(NT):
        n = t % 2
        xt = k.x2[:, t, :]
        if t >= 2:
            pool.wait(used[t - 2])
        r1 = k.channel("y1_in").gather(pool, y1[:, n, :], d["ys"], k.dest_i[:, t, 0:1])
        r2 = k.channel("y2_in").gather(pool, y2[:, n, :], d["ys"], k.dest_i[:, t, 1:2])
        if t == 0:
            used, queue = [], []
        dve.run(v.scalar_tensor_tensor, xt, y1[:, n, :], k.gates[:, t, 0:1], xt, ALU.mult, ALU.add, after=[r1])
        a = dve.then(v.scalar_tensor_tensor, xt, y2[:, n, :], k.gates[:, t, 1:2], xt, ALU.mult, ALU.add, after=[r2])
        used.append(a)
        q = act.run(s.activation, junk, xt, ACT.Square, accum_out=st[:, 2 * n:2 * n + 1], after=[a])
        r_ = k.rsqrt_mean(st[:, 2 * n + 1:2 * n + 2], st[:, 2 * n:2 * n + 1], D, after=[q])
        o = dve.run(v.scalar_tensor_tensor, xt, xt, st[:, 2 * n + 1:2 * n + 2], gain, ALU.mult, ALU.mult, after=[r_])
        k.channel("out").start(g.sp, d["out"][0, t * P:(t + 1) * P, :], xt, after=[o])
    g.sp.wait(k.channel("out").count.now())


S, D, DEPTH = 1024, 1024, 2
NT, KC = S // P, D // P
GH, DK, DV, GR = 4, 64, 128, 16
MH, NOPE, ROPE, MV, QR, KVR = 4, 128, 64, 128, 256, 128
HALF_ROPE = ROPE // 2
D_FF = 4 * D
D_IN = 2 * GH * DK + 2 * GH * DV + GR + QR + KVR + ROPE
C_Q, C_K = 0, GH * DK
C_V = 2 * GH * DK
C_O = C_V + GH * DV
C_A = C_O + GH * DV
C_M = C_A + GR
EPS = 1e-6
TAU = 16.0
LEVELS = P.bit_length() - 1
MASKED = -1e30
TWO_PI = 2 * np.pi
MAGIC = 1.5 * 2.0 ** 23

K_ID, K_ONE = 0, P
K_LEVEL = 2 * P
K_CAUSAL = K_LEVEL + LEVELS * P
K_BEFORE = K_CAUSAL + P
K_FREQ = K_BEFORE + P
K_IOTA = K_FREQ + HALF_ROPE
K_TOK = K_IOTA + 40
K_MINUS_HALF = K_TOK + NT
K_END = K_MINUS_HALF + 1


def constants():
    c = np.zeros((P, K_END), np.float32)
    p, f = np.arange(P)[:, None], np.arange(P)[None, :]
    c[:, K_ID:K_ID + P] = p == f
    c[:, K_ONE:K_ONE + P] = 1.0
    for v in range(LEVELS):
        half = 2 ** v
        same = p // (2 * half) == f // (2 * half)
        c[:, K_LEVEL + v * P:K_LEVEL + (v + 1) * P] = same & (p // half % 2 == 0) & (f // half % 2 == 1)
    c[:, K_CAUSAL:K_CAUSAL + P] = np.where(f <= p, 0.0, MASKED)
    c[:, K_BEFORE:K_BEFORE + P] = p < f
    c[:, K_FREQ:K_FREQ + HALF_ROPE] = np.float32(10000.0) ** (-np.arange(0, ROPE, 2, dtype=np.float32) / np.float32(ROPE))
    c[:, K_IOTA:K_IOTA + 40] = np.arange(40)
    c[:, K_TOK:K_TOK + NT] = np.arange(NT)[None, :] * P + p
    c[:, K_MINUS_HALF] = -0.5
    return c


ARENA = 38300
HEAD_START = 400
CHANNELS = ("setup_in x_copy bias_in gains_in w_in_in x_in q_out o_out q_in att_out0 att_out1 w_out_in x_all_in mixed_in "
            "x_out out").split() + CHANNELS_2


class Kit:

    def __init__(self, g, dram):
        self.g, self.dram = g, dram
        nc = g.nc
        self.psum = nc.alloc_psum_tensor("psum", [P, 8, 512], F32)
        self.banks = Ring(g, "psum", [self.psum[:, b, :] for b in range(8)])
        self.starts, self.twins = {}, {}
        self.weights = self.memory("weight_ring", 4 * 2048)[:].rearrange("p (a b) -> p a b", b=2048)
        self.ring = Ring(g, "weights", [self.weights[:, n, :] for n in range(4)],
                         [Channel(g, f"weights{n}_in") for n in range(4)])
        self.const = nc.alloc_sbuf_tensor("const", [P, K_END], F32)
        self.arena = self.memory("arena", ARENA)
        self.scratch = nc.alloc_sbuf_tensor("scratch", [P, 1024], F32)
        self.stat = nc.alloc_sbuf_tensor("stat", [P, 64], F32)
        self.expert_channels = [Channel(g, f"expert{n}_in") for n in range(6)]
        self.channels = {name: Channel(g, name) for name in CHANNELS}

    def memory(self, name, words):
        self.starts[name] = -(-self.g.nc.sbuf_base // 32) * 32
        return self.g.nc.alloc_sbuf_tensor(name, [P, words], F32)

    def rounded(self, view):
        name, words = view.tensor.name, int(np.prod(view.shape[1:]))
        key = (name, view.offset, words)
        if key not in self.twins:
            self.twins[key] = self.g.nc.alloc_sbuf_tensor_at(f"{name}_r{len(self.twins)}", [P, words], F32R,
                                                             offset=self.starts[name] + 4 * view.offset)
        return bass.AP(self.twins[key], 0, ((words, P), *view.ap[1:]))

    def channel(self, name):
        return self.channels[name]

    def c(self, at, n=P):
        return self.const[:, at:at + n]

    def ident(self, n=P):
        return self.const[0:n, K_ID:K_ID + n]

    def load_weights(self, src, shape, extra=()):
        slot = self.ring.take()
        n = int(np.prod(shape))
        view = slot.ap[:, 0:n]
        if len(shape) == 2:
            view = view.rearrange("p (a b) -> p a b", b=shape[1])
        sp = self.g.sp
        sp.wait(*slot.free)
        return slot, view, slot.channel.start(sp, view, src, after=extra)

    def load_wide(self, src, shape):
        self.ring.align(2)
        one, two = self.ring.take(), self.ring.take()
        view = self.weights[:, one.n:one.n + 2, :].rearrange("p a b -> p (a b)").rearrange("p (a b) -> p a b", b=shape[1])
        return (one, two), view, one.channel.start(self.g.sp, view, src, after=[*one.free, *two.free])

    def load_from(self, ring, src, shape):
        slot = ring.take()
        view = slot.ap.rearrange("p (a b) -> p a b", b=shape[1])
        return slot, view, slot.channel.start(self.g.sp, view, src, after=slot.free)

    def bank_after(self, held):
        while self.banks.slots[self.banks.next % 8] in held:
            self.banks.next += 1
        return self.bank()

    def xc_sel(self, q, cols):
        return self.xc_in[:, bass.ds(q, 1), cols].rearrange("p o n -> p (o n)")

    def bank(self):
        slot = self.banks.take()
        self.g.pe.wait(*slot.free)
        return slot

    def bank_pair(self):
        self.banks.align(2)
        pair = [self.bank(), self.bank()]
        return pair, self.psum[:, pair[0].n:pair[0].n + 2, :]

    def release(self, slots, *counts):
        for slot in slots:
            slot.release(*counts)

    def product(self, out, pairs, after=(), start=True, stop=True):
        pe, nc = self.g.pe, self.g.nc
        pe.wait(*after)
        for n, (lhs, rhs) in enumerate(pairs):
            last = n == len(pairs) - 1
            (pe.run if last else pe.quiet)(nc.tensor.matmul, out, lhs, rhs, start=start and n == 0, stop=stop and last)
        return pe.last

    def split_product(self, out, quads, after=()):
        pairs = [p for lh, ll, rh, rl in quads for p in ((lh, rh), (lh, rl), (ll, rh))]
        return self.product(out, pairs, after=after)

    def turn(self, outs_ins, after=()):
        pe, nc = self.g.pe, self.g.nc
        pe.wait(*after)
        for n, (out, in_) in enumerate(outs_ins):
            last = n == len(outs_ins) - 1
            (pe.run if last else pe.quiet)(nc.tensor.transpose, out, in_, self.ident(in_.shape[0]),
                                         alone=in_.shape[0] < P or in_.shape[1] < P)
        return pe.last

    def rsqrt_mean(self, out, total, width, after=()):
        pool, gp = self.g.pool, self.g.nc.gpsimd
        pool.run(gp.tensor_scalar, out, total, 1.0 / width, EPS, ALU.mult, ALU.add, after=after, alone=True)
        return pool.then(gp.tensor_tensor, out, out, spread(self.c(K_MINUS_HALF, 1), P, out.shape[1]), ALU.pow)

    def silu_factor(self, out, in_, after=(), scale=-1.0):
        act, dve, nc = self.g.act, self.g.dve, self.g.nc
        e = act.run(nc.scalar.activation, out, in_, ACT.Exp, scale=scale, after=after)
        dve.run(nc.vector.tensor_scalar_add, out, out, 1.0, after=[e])
        return dve.then(nc.vector.reciprocal, out, out)


def spread(ap, *shape):
    return ap.broadcast_to(list(shape))


def sine(k, out, angle, shift, tmp, after=()):
    dve, v = k.g.dve, k.g.nc.vector
    turns, rest = tmp
    c1 = 6.28125
    c2 = float(np.float32(TWO_PI - c1))
    c3 = float(TWO_PI - c1 - c2)
    dve.run(v.tensor_scalar, turns, angle, 1.0 / TWO_PI, shift / TWO_PI, ALU.mult, ALU.add, after=after)
    dve.then(v.tensor_scalar_add, turns, turns, MAGIC)
    dve.then(v.tensor_scalar_add, turns, turns, -MAGIC)
    dve.then(v.scalar_tensor_tensor, rest, turns, -c1, angle, ALU.mult, ALU.add)
    dve.then(v.scalar_tensor_tensor, rest, turns, -c2, rest, ALU.mult, ALU.add)
    dve.then(v.scalar_tensor_tensor, rest, turns, -c3, rest, ALU.mult, ALU.add)
    dve.then(v.tensor_scalar_add, rest, rest, shift)
    r = dve.then(v.tensor_scalar, rest, rest, 3.1415925, -3.1415925, ALU.min, ALU.max)
    return k.g.act.run(k.g.nc.scalar.activation, out, rest, ACT.Sin, after=[r])


def setup(k):
    g, nc, d = k.g, k.g.nc, k.dram
    load = k.channel("setup_in")
    for e in (g.pe, g.act, g.dve, g.pool):
        e.api.sem_inc(e.count.sem, HEAD_START)
        e.count.step(HEAD_START)
    for name in ("q_out", "o_out", "att_out0", "att_out1", "x_out", "hn_out"):
        c = k.channel(name).count
        g.act.api.sem_inc(c.sem, 16)
        c.step(16)
    k.channel("x_copy").start(g.pool, d["x_res"][0:S], d["x"][0])
    copied = k.channel("x_copy").start(g.pool, d["x_res"][S:S + P], d["x"][0, 0:P])
    k.pos_i = nc.alloc_sbuf_tensor("pos_i", [P, NT], I32)
    k.cond = nc.alloc_sbuf_tensor("cond", [P, KC], F32)
    k.cos = nc.alloc_sbuf_tensor("cos", [P, NT, HALF_ROPE], F32)
    k.sin = nc.alloc_sbuf_tensor("sin", [P, NT, HALF_ROPE], F32)
    load.start(g.sp, k.const[:], d["const"])
    load.start(g.sp, k.pos_i[:], d["positions"][0].rearrange("(t p) -> p t", p=P), allow_slow_non_contiguous=True)
    here = load.start(g.sp, k.cond[:], d["c"][0].rearrange("(k p) -> p k", p=P), allow_slow_non_contiguous=True)
    k.ready = here
    pos = k.arena[:, 0:NT]
    ang = k.arena[:, 1024:1024 + NT * HALF_ROPE]
    tmp = [k.arena[:, o:o + NT * HALF_ROPE] for o in (2048, 3072)]
    g.dve.run(nc.vector.tensor_copy, pos, k.pos_i[:], after=[here])
    a = g.dve.then(nc.vector.tensor_tensor, ang.rearrange("p (t f) -> p t f", t=NT),
                   spread(pos.unsqueeze(2), P, NT, HALF_ROPE), spread(k.c(K_FREQ, HALF_ROPE).unsqueeze(1), P, NT, HALF_ROPE), ALU.mult)
    s1 = sine(k, k.sin[:].rearrange("p t f -> p (t f)"), ang, 0.0, tmp, after=[a])
    sine(k, k.cos[:].rearrange("p t f -> p (t f)"), ang, np.pi / 2, tmp, after=[s1])
    f = k.silu_factor(k.scratch[:, 0:KC], k.cond[:], after=[here])
    c = g.dve.then(nc.vector.tensor_tensor, k.cond[:], k.cond[:], k.scratch[:, 0:KC], ALU.mult)
    k.x_stored = copied
    k.mod = nc.alloc_sbuf_tensor("mod", [P, 2, 2, KC], F32)
    k.gate = nc.alloc_sbuf_tensor("gate", [P, 2, D], F32)
    k.small = nc.alloc_sbuf_tensor("small", [P, 1024], F32)
    g.join()


def modulation(k, layer):
    g, nc, d = k.g, k.g.nc, k.dram
    bias_rows = k.arena[0:48, 0:P]
    bias_cols = k.arena[:, 128:128 + 48]
    gate_bias = k.arena[:, 1024:1024 + 2 * D].rearrange("p (a n) -> p a n", a=2)
    ch = k.channel("bias_in")
    ch.start(g.act, bias_rows, d["b_ada"][layer].rearrange("(c p) -> c p", p=P))
    for n in range(2):
        b = ch.start(g.act, gate_bias[:, n, :], d["b_ada"][layer][(3 * n + 2) * D:(3 * n + 3) * D].partition_broadcast(P))
    bank = k.bank()
    t = k.turn([(bank.ap[:, 0:48], bias_rows)], after=[b])
    bank.release(g.dve.run(nc.vector.tensor_copy, bias_cols, bank.ap[:, 0:48], after=[t]))
    g.dve.wait(g.dve.last)
    w = d["w_ada"][layer].rearrange("(k p) n -> p k n", p=P)
    part_sum = [k.arena[:, 5120 + n * 512:5632 + n * 512] for n in range(2)]
    rows = k.arena[:, 6144:6144 + 4 * D].rearrange("p (a n) -> p a n", a=2)
    summed = [None, None]
    for part in range(2):
        for piece in range(6):
            n = piece % 2
            lo = part * 3 * D + piece * 512
            slots, view, came = k.load_wide(w[:, :, lo:lo + 512], (KC, 512))
            acc = part_sum[n]
            g.dve.run(nc.vector.tensor_scalar, acc, view[:, 0, :], k.cond[:, 0:1], None, ALU.mult, after=[came, summed[n]])
            for c in range(1, KC):
                e = g.dve.then(nc.vector.scalar_tensor_tensor, acc, view[:, c, :], k.cond[:, c:c + 1], acc, ALU.mult, ALU.add)
            k.release(slots, e)
            bank = k.bank()
            m = summed[n] = k.product(bank.ap, [(k.c(K_ONE), acc)], after=[e])
            if piece < 4:
                e = g.act.run(nc.scalar.activation, rows[:, part, piece * 512:(piece + 1) * 512], bank.ap, ACT.Copy, after=[m])
            else:
                out = slice((piece - 4) * 512, (piece - 3) * 512)
                e = g.dve.run(nc.vector.tensor_tensor, k.gate[:, part, out], bank.ap, gate_bias[:, part, out], ALU.add, after=[m])
            bank.release(e)
    for part in range(2):
        mod = k.mod[:, part, :, :].rearrange("p a c -> p (a c)")
        for n in range(4):
            bank = k.bank()
            t = k.turn([(bank.ap[:, j * P:(j + 1) * P], rows[:, part, (4 * n + j) * P:(4 * n + j + 1) * P]) for j in range(4)],
                       after=[g.act.last])
            at = part * 24 + 4 * n
            e = g.dve.run(nc.vector.tensor_tensor, mod[:, 4 * n:4 * n + 4], bank.ap[:, 0:512:P], bias_cols[:, at:at + 4], ALU.add,
                          after=[t])
            bank.release(e)
        g.dve.then(nc.vector.tensor_scalar_add, k.mod[:, part, 1, :], k.mod[:, part, 1, :], 1.0)
    g.join()


def normed(k, x, xn, stat, after=()):
    g, nc = k.g, k.g.nc
    ss, rstd = stat[:, 0:1], stat[:, 1:2]
    q = g.act.run(nc.scalar.activation, xn, x, ACT.Square, accum_out=ss, after=after)
    r = k.rsqrt_mean(rstd, ss, D, after=[q])
    return g.dve.run(nc.vector.tensor_scalar, xn, x, rstd, None, ALU.mult, after=[r])


def at(i, n=1):
    return slice(i * n, (i + 1) * n) if isinstance(i, int) else bass.ds(i * n, n)


def turned_in(k, xn, out, part, after=(), free=()):
    g, nc = k.g, k.g.nc
    done = []
    for half in range(2):
        bank = k.bank()
        t = k.turn([(bank.ap[:, j * P:(j + 1) * P], xn[:, (4 * half + j) * P:(4 * half + j + 1) * P]) for j in range(4)], after=after)
        for j in range(4):
            c = 4 * half + j
            src, dst = bank.ap[:, j * P:(j + 1) * P], out(c)
            if half == 0:
                e = g.dve.run(nc.vector.tensor_scalar, dst, src, k.mod[:, part, 1, c:c + 1], k.mod[:, part, 0, c:c + 1],
                              ALU.mult, ALU.add, after=[t, *free])
            else:
                e = g.act.run(nc.scalar.activation, dst, src, ACT.Identity, scale=k.mod[:, part, 1, c:c + 1],
                              bias=k.mod[:, part, 0, c:c + 1], after=[t, *free])
        bank.release(e)
        done.append(e)
    return t, done


def mixer_tiles(k, layer):
    g, nc, d = k.g, k.g.nc, k.dram
    dve, act, pe, pool, v, s, gp = g.dve, g.act, g.pe, g.pool, nc.vector, nc.scalar, nc.gpsimd
    A = Area(k.arena)
    w_qk, w_am = A.take(KC, 512), A.take(KC, GR + 448)
    kT = A.take(MH, S)
    kpeT = A.take(S)
    val = A.take(NT, MH * MV)
    k.kT, k.kpeT, k.val = kT, kpeT, val
    wq_up = A.take(2, MH * (NOPE + ROPE))
    wkv_up = A.take(MH * (NOPE + MV))
    w_gate = A.take(GH * DK)
    xt, xn = A.take(D), A.take(D)
    hT = A.take(KC, P)
    qk = A.take(4, P)
    ga = A.take(P)
    z, la, b = A.take(2, P), A.take(2, P), A.take(2, P)
    decay = A.take(LEVELS, 2, P)
    ql, kl = A.take(LEVELS, 2, P), A.take(LEVELS, 2, P)
    attn = A.take(GH, P)
    vt, go = A.take(GH * DV), A.take(GH * DV)
    eb, ebl = A.take(2, P), A.take(2, P)
    qe, kd, kdn = A.take(2, P), A.take(2, P), A.take(2, P)
    state = A.take(2, 2 * DV)
    o, o_sq = A.take(GH * DV), A.take(GH * DV)
    m_q = A.take(QR + KVR)
    mT = A.take(3, P)
    qh, tmp = A.take(MH * (NOPE + ROPE)), k.scratch[:, 0:MH * (NOPE + ROPE)]
    kn = A.take(MH * NOPE)
    pe_in, pe_rot = A.take(MH + 1, ROPE), A.take(MH + 1, ROPE)
    rt = A.take(2, MH + 1, HALF_ROPE)
    q_out, qpe_out = A.take(MH, P), A.take(MH, P)
    st = k.stat
    S_ = k.small
    qa_g, kva_g, qn_g, kn_g, bg = S_[:, 0:2], S_[:, 2:3], S_[:, 3:4], S_[:, 4:5], S_[:, 5:7]
    out_g = S_[:, 8:8 + DV]
    pe_g = S_[:, 256:256 + (MH + 1) * ROPE].rearrange("p (h r) -> p h r", r=ROPE)
    ch = k.channel("gains_in")
    def col(dst, name, n):
        return ch.start(g.act, dst, d[name][layer].rearrange("(k p) -> p k", p=n), allow_slow_non_contiguous=True)
    col(qa_g, "q_a_norm", P), col(kva_g, "kv_a_norm", P), col(qn_g, "q_norm_nope", P), col(kn_g, "k_norm_nope", P)
    col(bg, "b_gate", P)
    ch.start(g.act, out_g, d["gla_out_norm"][layer].partition_broadcast(P))
    for h in range(MH + 1):
        ch.start(g.act, pe_g[:, h, :], d["q_norm_rope" if h < MH else "k_norm_rope"][layer].partition_broadcast(P))
    ch.start(g.act, wq_up, d["w_q_up"][layer].rearrange("(k p) n -> p k n", p=P))
    ch.start(g.act, wkv_up, d["w_kv_up"][layer])
    small = ch.start(g.act, w_gate[0:GR], d["w_gate_up"][layer])
    wi = d["w_in"][layer].rearrange("(k p) n -> p k n", p=P)
    k.channel("w_in_in").start(g.act, w_qk, wi[:, :, 0:512])
    came_w = k.channel("w_in_in").start(g.act, w_am, wi[:, :, C_A:])
    v_slots, w_v, came_v = k.load_wide(wi[:, :, C_V:C_V + 512], (KC, 512))
    o_slots, w_o, came_o = k.load_wide(wi[:, :, C_O:C_O + 512], (KC, 512))
    zero = pool.run(gp.memset, state, 0.0)
    g.pe.wait(small, came_w, came_v, came_o)
    g.dve.wait(small, zero)
    g.act.wait(small)
    g.pe.wait(zero)

    def norm_tile(i, after=(), turned=()):
        x_in = k.channel("x_in").start(g.sp, xt, d["x_res"][bass.ds(i * P, P), :], after=after)
        return normed(k, xt, xn, st, after=[x_in, *turned])

    n0 = norm_tile(0, after=k.x_ready)
    _, first = turned_in(k, xn, lambda c: hT[:, c, :], 0, after=[n0])
    pe.wait(*first)
    g.sp.wait(n0)
    act.wait(n0, pe.last)
    with g.loop("tiles", NT) as t:
        pe.wait(*g.before("h_ready"))
        b_ga = k.bank()
        m = k.product(b_ga.ap[0:GR, 0:P], [(w_am[:, c, 0:GR], hT[:, c, :]) for c in range(KC)])
        e_ga = act.run(s.activation, ga[0:GR], b_ga.ap[0:GR, 0:P], ACT.Copy, after=[m])
        b_ga.release(e_ga)
        b_qk = k.bank()
        for j in range(4):
            m = k.product(b_qk.ap[:, j * P:(j + 1) * P], [(w_qk[:, c, j * P:(j + 1) * P], hT[:, c, :]) for c in range(KC)])
        e_q = act.run(s.activation, qk[:, 0:2, :], b_qk.ap[:, 0:256].rearrange("p (a b) -> p a b", a=2), ACT.Copy,
                      scale=DK ** -0.5, after=[m, *g.before("qk_read")])
        e_k = act.run(s.activation, qk[:, 2:4, :], b_qk.ap[:, 256:512].rearrange("p (a b) -> p a b", a=2), ACT.Copy)
        b_qk.release(e_k)
        b_z = k.bank()
        for gi in range(2):
            m = k.product(b_z.ap[:, gi * P:(gi + 1) * P], [(w_gate[0:GR, gi * P:(gi + 1) * P], ga[0:GR])], after=[e_ga])
        for gi in range(2):
            dve.run(v.tensor_scalar_add, z[:, gi, :], b_z.ap[:, gi * P:(gi + 1) * P], bg[:, gi:gi + 1], after=[m])
        b_z.release(dve.last)
        az = act.run(s.activation, la, z, ACT.Abs, after=[dve.last])
        dve.then(v.tensor_scalar, z, z, 0.0, None, ALU.min, after=[az])
        act.then(s.activation, la, la, ACT.Exp, scale=-1.0)
        ln = act.then(s.activation, la, la, ACT.Ln, bias=1.0)
        dve.then(v.tensor_tensor, la, z, la, ALU.subtract, after=[ln])
        dve.then(v.tensor_scalar_mul, la, la, 1.0 / TAU)
        for gi in range(2):
            dve.then(v.tensor_tensor_scan, b[:, gi, :], k.c(K_ONE), la[:, gi, :], 0.0, ALU.mult, ALU.add)
        for lv in range(LEVELS):
            half = 2 ** lv
            bb = b.rearrange("p g n -> p (g n)").rearrange("p (n a h) -> p n a h", a=2, h=half)
            dd = decay[:, lv].rearrange("p g n -> p (g n)").rearrange("p (n a h) -> p n a h", a=2, h=half)
            mid = spread(bb[:, :, 0, half - 1:half], P, P // half, half)
            (dve.then if lv == 0 else dve.run)(v.tensor_tensor, dd[:, :, 1, :], bb[:, :, 1, :], mid, ALU.subtract)
            last = dve.run(v.tensor_tensor, dd[:, :, 0, :], mid, bb[:, :, 0, :], ALU.subtract)
        for gi in range(2):
            last = dve.run(v.tensor_scalar, ebl[:, gi, :], b[:, gi, :], b[:, gi, P - 1:P], -1.0, ALU.subtract, ALU.mult)
        e_dec = act.run(s.activation, decay, decay, ACT.Exp, after=[last])
        e_b = act.run(s.activation, eb, b, ACT.Exp)
        e_bl = act.run(s.activation, ebl, ebl, ACT.Exp)
        read = g.before("levels_read")
        late = LEVELS - 2
        wide = lambda ap, n: spread(ap.unsqueeze(1), P, n, 2, P)
        kx_late = pool.run(gp.tensor_tensor, kl[:, late:], wide(qk[:, 2:4, :], 2), decay[:, late:], ALU.mult,
                           after=[e_dec, e_k, *read])
        dve.run(v.tensor_tensor, kl[:, 0:late], wide(qk[:, 2:4, :], late), decay[:, 0:late], ALU.mult, after=[e_dec, e_q, e_k, *read])
        qx = dve.run(v.tensor_tensor, ql, wide(qk[:, 0:2, :], LEVELS), decay, ALU.mult)
        x1 = dve.run(v.tensor_tensor, kd, qk[:, 2:4, :], ebl, ALU.mult, after=[e_bl])
        x2 = dve.run(v.tensor_tensor, qe, qk[:, 0:2, :], eb, ALU.mult)
        g.mark("qk_read", x2, kx_late)
        b_v = k.bank()
        m_v = k.product(b_v.ap, [(hT[:, c, :], w_v[:, c, :]) for c in range(KC)])
        e_v = act.run(s.activation, vt, b_v.ap, ACT.Copy, after=[m_v])
        b_v.release(e_v)
        b_m = k.bank()
        m = k.product(b_m.ap[:, 0:448], [(hT[:, c, :], w_am[:, c, GR:GR + 448]) for c in range(KC)])
        sq = act.run(s.activation, tmp[:, 0:QR], b_m.ap[:, 0:QR], ACT.Square, accum_out=st[:, 4:5], after=[m])
        sq = act.run(s.activation, tmp[:, QR:QR + KVR], b_m.ap[:, QR:QR + KVR], ACT.Square, accum_out=st[:, 5:6])
        e_pe = act.run(s.activation, pe_in[:, MH, :], b_m.ap[:, QR + KVR:448], ACT.Copy, after=g.before("pe_read"))
        k.rsqrt_mean(st[:, 4:5], st[:, 4:5], QR, after=[sq])
        r = k.rsqrt_mean(st[:, 5:6], st[:, 5:6], KVR)
        dve.run(v.tensor_scalar, m_q[:, 0:QR], b_m.ap[:, 0:QR], st[:, 4:5], None, ALU.mult, after=[e_pe, r])
        mq = dve.run(v.tensor_scalar, m_q[:, QR:QR + KVR], b_m.ap[:, QR:QR + KVR], st[:, 5:6], None, ALU.mult)
        b_m.release(mq)
        b_go = k.bank()
        m_go = k.product(b_go.ap, [(hT[:, c, :], w_o[:, c, :]) for c in range(KC)])
        k.silu_factor(go, b_go.ap, after=[m_go, *g.before("go_read")])
        silu = dve.then(v.tensor_tensor, go, go, b_go.ap, ALU.mult)
        b_go.release(silu)
        b_mt = k.bank()
        tt = k.turn([(b_mt.ap[:, j * P:(j + 1) * P], m_q[:, j * P:(j + 1) * P]) for j in range(3)], after=[mq])
        for j in range(3):
            gain = qa_g[:, j:j + 1] if j < 2 else kva_g
            e_mt = act.run(s.activation, mT[:, j, :], b_mt.ap[:, j * P:(j + 1) * P], ACT.Copy, scale=gain, after=[tt])
        b_mt.release(e_mt)
        norm = norm_tile(t + 1, after=g.before("xt_read"), turned=g.before("xn_read"))
        g.mark("xt_read", norm)
        pe.wait(e_mt)
        banks = [k.bank() for _ in range(2)]
        for n in range(2):
            m = k.product(banks[n].ap[:, 0:384], [(mT[:, c, :], wq_up[:, c, n * 384:(n + 1) * 384]) for c in range(2)])
            e = act.run(s.activation, qh[:, n * 384:(n + 1) * 384], banks[n].ap[:, 0:384], ACT.Copy, after=[m, *g.before("qh_read")])
            banks[n].release(e)
        sq = act.then(s.activation, tmp, qh, ACT.Square)
        q3, t3 = (x_.rearrange("p (h n) -> p h n", h=MH) for x_ in (qh, tmp))
        dve.run(v.tensor_reduce, st[:, 8:12], t3[:, :, 0:NOPE], AX.X, ALU.add, after=[sq])
        r = dve.run(v.tensor_reduce, st[:, 12:16], t3[:, :, NOPE:], AX.X, ALU.add)
        bkv = [k.bank() for _ in range(2)]
        for n in range(2):
            m = k.product(bkv[n].ap, [(mT[:, 2, :], wkv_up[:, n * 512:(n + 1) * 512])])
            kv = bkv[n].ap.rearrange("p (h n) -> p h n", h=2)
            dst = val[:, bass.ds(t, 1), n * 256:(n + 1) * 256].rearrange("p a (h n) -> p (a h) n", h=2)
            act.run(s.activation, dst, kv[:, :, NOPE:], ACT.Copy, after=[m])
            e = act.run(s.activation, kn[:, n * 256:(n + 1) * 256].rearrange("p (h n) -> p h n", h=2), kv[:, :, 0:NOPE], ACT.Copy,
                        after=g.before("kn_read"))
            bkv[n].release(e)
        g.mark("mT_read", m)
        e_kn = e
        sq1 = act.then(s.activation, tmp[:, 0:512], kn, ACT.Square, after=[r])
        sq2 = act.run(s.activation, tmp[:, 512:576], pe_in[:, MH, :], ACT.Square, accum_out=st[:, 20:21])
        dve.run(v.tensor_reduce, st[:, 16:20], tmp[:, 0:512].rearrange("p (h n) -> p h n", h=MH), AX.X, ALU.add, after=[sq1, sq2])
        dve.then(v.tensor_scalar, st[:, 8:12], st[:, 8:12], 1.0 / NOPE, EPS, ALU.mult, ALU.add)
        dve.run(v.tensor_scalar, st[:, 16:20], st[:, 16:20], 1.0 / NOPE, EPS, ALU.mult, ALU.add)
        dve.run(v.tensor_scalar, st[:, 12:16], st[:, 12:16], 1.0 / ROPE, EPS, ALU.mult, ALU.add)
        dve.run(v.tensor_scalar, st[:, 20:21], st[:, 20:21], 1.0 / ROPE, EPS, ALU.mult, ALU.add)
        r = pool.run(gp.tensor_tensor, st[:, 8:21], st[:, 8:21], spread(k.c(K_MINUS_HALF, 1), P, 13), ALU.pow, after=[dve.last])
        dve.run(v.tensor_tensor, q3[:, :, 0:NOPE], q3[:, :, 0:NOPE], spread(st[:, 8:12].unsqueeze(2), P, MH, NOPE), ALU.mult, after=[r])
        qn_ready = dve.last
        kn3 = kn.rearrange("p (h n) -> p h n", h=MH)
        kn_ready = dve.run(v.tensor_tensor, kn3, kn3, spread(st[:, 16:20].unsqueeze(2), P, MH, NOPE), ALU.mult, after=[e_kn])
        dve.run(v.tensor_tensor, pe_in[:, 0:MH, :], q3[:, :, NOPE:], spread(st[:, 12:16].unsqueeze(2), P, MH, ROPE), ALU.mult)
        dve.run(v.tensor_scalar, pe_in[:, MH, :], pe_in[:, MH, :], st[:, 20:21], None, ALU.mult)
        dve.then(v.tensor_tensor, pe_in, pe_in, pe_g, ALU.mult)
        cos = spread(k.cos[:, bass.ds(t, 1), :], P, MH + 1, HALF_ROPE)
        sin = spread(k.sin[:, bass.ds(t, 1), :], P, MH + 1, HALF_ROPE)
        lo, hi = slice(0, HALF_ROPE), slice(HALF_ROPE, ROPE)
        dve.then(v.tensor_tensor, pe_rot[:, :, lo], pe_in[:, :, lo], cos, ALU.mult, after=g.before("rot_read"))
        dve.run(v.tensor_tensor, rt[:, 0], pe_in[:, :, hi], sin, ALU.mult)
        dve.run(v.tensor_tensor, pe_rot[:, :, hi], pe_in[:, :, hi], cos, ALU.mult)
        dve.run(v.tensor_tensor, rt[:, 1], pe_in[:, :, lo], sin, ALU.mult)
        g.mark("pe_read", dve.last)
        dve.then(v.tensor_tensor, pe_rot[:, :, lo], pe_rot[:, :, lo], rt[:, 0], ALU.subtract)
        rot = dve.run(v.tensor_tensor, pe_rot[:, :, hi], pe_rot[:, :, hi], rt[:, 1], ALU.add)
        pair, sc4 = k.bank_pair()
        for gi in range(2):
            for a in range(2):
                r = slice(64 * a, 64 * a + 64)
                m = k.product(sc4[:, a, gi * P:(gi + 1) * P], [(qk[r, 2 + gi, :], qk[r, gi, :])], after=[e_k])
        g.mark("qk_read", x2, kx_late, m)
        attn4 = attn.rearrange("p (a g) n -> p a g n", a=2)
        both = [P, 2, 2, P]
        dve.run(v.tensor_tensor, attn4, sc4[:, :, 0:256].rearrange("p a (g n) -> p a g n", g=2),
                spread(k.c(K_ID).unsqueeze(1).unsqueeze(1), *both), ALU.mult, after=[m, *g.before("attn_read")])
        k.release(pair, dve.last)
        for lv in range(LEVELS):
            pair, sc4 = k.bank_pair()
            for gi in range(2):
                for a in range(2):
                    r = slice(64 * a, 64 * a + 64)
                    m = k.product(sc4[:, a, gi * P:(gi + 1) * P], [(kl[r, lv, gi, :], ql[r, lv, gi, :])], after=[qx] if lv < late else [qx, kx_late])
            mask = spread(k.c(K_LEVEL + lv * P).unsqueeze(1).unsqueeze(1), *both).bitcast(I32)
            sc = dve.then(v.copy_predicated, attn4, mask, sc4[:, :, 0:256].rearrange("p a (g n) -> p a g n", g=2), after=[m],
                          alone=True)
            k.release(pair, sc)
        g.mark("levels_read", m)
        turned, h_ready = turned_in(k, xn, lambda c: hT[:, c, :], 0, after=[norm], free=[m_go])
        g.mark("xn_read", turned)
        g.mark("h_ready", *h_ready)
        bt = k.bank()
        m = k.turn([(bt.ap[:, h * P:(h + 1) * P], q3[:, h, 0:NOPE]) for h in range(MH)], after=[qn_ready])
        g.mark("qh_read", m, rot)
        e1 = act.run(s.activation, q_out.rearrange("p h n -> p (h n)"), bt.ap, ACT.Copy, scale=qn_g, after=[m, *g.before("q_sent")])
        bt.release(e1)
        bt = k.bank()
        m = k.turn([(bt.ap[:, h * P:(h + 1) * P], kn3[:, h, :]) for h in range(MH)], after=[kn_ready])
        g.mark("kn_read", m)
        e = act.run(s.activation, kT[:, :, bass.ds(t * P, P)], bt.ap.rearrange("p (h n) -> p h n", h=MH), ACT.Copy,
                    scale=kn_g, after=[m])
        bt.release(e)
        bt = k.bank()
        m = k.turn([(bt.ap[0:ROPE, h * P:(h + 1) * P], pe_rot[:, h, :]) for h in range(MH)], after=[rot])
        e2 = act.run(s.activation, qpe_out[0:ROPE].rearrange("p h n -> p (h n)"), bt.ap[0:ROPE], ACT.Copy, after=[m])
        bt.release(e2)
        bt = k.bank()
        m = k.turn([(bt.ap[0:ROPE, 0:P], pe_rot[:, MH, :])])
        g.mark("rot_read", m)
        e = act.run(s.activation, kpeT[0:ROPE, bass.ds(t * P, P)], bt.ap[0:ROPE, 0:P], ACT.Copy, after=[m])
        bt.release(e)
        k.channel("q_out").start(g.sp, d["q_all"][:, :, bass.ds(t * P, P)].rearrange("h p n -> p h n"), q_out, after=[e1, e2])
        k.channel("q_out").start(g.sp, d["qpe_all"][:, :, bass.ds(t * P, P)].rearrange("h p n -> p h n"), qpe_out[0:ROPE])
        g.mark("q_sent", k.channel("q_out").count.now())
        b_kd = k.bank()
        m = k.turn([(b_kd.ap[:, gi * P:(gi + 1) * P], kd[:, gi, :]) for gi in range(2)], after=[x1])
        e_kd = act.run(s.activation, kdn.rearrange("p g n -> p (g n)"), b_kd.ap[:, 0:256], ACT.Copy, after=[m])
        b_kd.release(e_kd)
        b_o = k.bank()
        pe.wait(x2, e_v, sc, *g.before("state_new"))
        for gi in range(2):
            k.product(b_o.ap[:, gi * 256:(gi + 1) * 256], [(qe[:, gi, :], state[:, gi, :])], stop=False)
            st_read = pe.last
            for h in (2 * gi, 2 * gi + 1):
                m_o = k.product(b_o.ap[:, h * DV:(h + 1) * DV], [(attn[:, 2 * (h % 2) + gi, :], vt[:, h * DV:(h + 1) * DV])], start=False,
                                stop=h % 2 == 1)
        g.mark("attn_read", m_o)
        b_s = k.bank()
        for gi in range(2):
            m_s = k.product(b_s.ap[:, gi * 256:(gi + 1) * 256], [(kdn[:, gi, :], vt[:, gi * 256:(gi + 1) * 256])], after=[e_kd])
        for gi in range(2):
            for a in range(2):
                r, cc = slice(64 * a, 64 * a + 64), slice(DV * a, DV * a + DV)
                sn = dve.run(v.scalar_tensor_tensor, state[r, gi, cc], state[r, gi, cc], eb[r, gi, P - 1:P],
                             b_s.ap[r, gi * 256 + DV * a:gi * 256 + DV * a + DV], ALU.mult, ALU.add, after=[m_s, st_read, e_b])
        g.mark("state_new", sn)
        b_s.release(sn)
        sq = act.run(s.activation, o_sq, b_o.ap, ACT.Square, after=[m_o])
        dve.run(v.tensor_reduce, st[:, 24:28], o_sq.rearrange("p (h n) -> p h n", h=GH), AX.X, ALU.add, after=[sq])
        r = k.rsqrt_mean(st[:, 24:28], st[:, 24:28], DV, after=[dve.last])
        o3, go3 = (x_.rearrange("p (h n) -> p h n", h=GH) for x_ in (o, go))
        dve.then(v.tensor_tensor, o3, b_o.ap.rearrange("p (h n) -> p h n", h=GH), spread(st[:, 24:28].unsqueeze(2), P, GH, DV),
                 ALU.mult, after=[r, *g.before("o_sent")])
        b_o.release(dve.last)
        dve.then(v.tensor_tensor, o3, o3, spread(out_g.unsqueeze(1), P, GH, DV), ALU.mult)
        of = dve.then(v.tensor_tensor, o, o, go, ALU.mult, after=[silu])
        g.mark("go_read", of)
        k.channel("o_out").start(g.sp, d["mixed"][bass.ds(t * P, P), 0:512], o, after=[of])
        g.mark("o_sent", k.channel("o_out").count.now())
    for slot in (*v_slots, *o_slots):
        slot.release(pe.last)
    g.join(k.channel("o_out"), k.channel("q_out"))


def attention(k):
    g, nc, d = k.g, k.g.nc, k.dram
    dve, act, pe, v, s = g.dve, g.act, g.pe, nc.vector, nc.scalar
    A = Area(k.arena)
    A.skip(KC * (D_IN - 1024) + MH * S + S + NT * MH * MV)
    qT, qpeT = A.take(S), A.take(S)
    prob = [A.take(S) for _ in range(2)]
    probT = [A.take(NT, P) for _ in range(2)]
    out = [A.take(MV) for _ in range(2)]
    st = k.stat
    scale = float((NOPE + ROPE) ** -0.5)
    ch = k.channel("q_in")
    with g.loop("heads", MH) as h:
        after = [*g.before("q_read"), k.channel("q_out").count.now()]
        ch.start(g.sp, qT, d["q_all"][bass.ds(h, 1)].rearrange("a p n -> p (a n)"), after=after)
        q_in = ch.start(g.sp, qpeT[0:ROPE], d["qpe_all"][bass.ds(h, 1)].rearrange("a p n -> p (a n)"))
        pe.wait(q_in)
        sent = [[], []]
        for n in range(2):
            sent[n] = g.before(f"att_out{n}")
        pv_read = [g.before(f"probT_read{n}") for n in range(2)]
        exp_read = [g.before(f"prob_read{n}") for n in range(2)]

        def scores(qt):
            w = (qt + 1) * P
            pair, sc = k.bank_pair()
            sc = sc.rearrange("p a b -> p (a b)")
            for lo in range(0, w, 512):
                hi = min(lo + 512, w)
                kh = k.kT[:, bass.ds(h, 1), lo:hi].rearrange("p a n -> p (a n)")
                m = k.product(sc[:, lo:hi], [(qT[:, qt * P:(qt + 1) * P], kh)], stop=False)
                m = k.product(sc[:, lo:hi], [(qpeT[0:ROPE, qt * P:(qt + 1) * P], k.kpeT[0:ROPE, lo:hi])], start=False)
            return pair, sc, m

        ready = scores(0)
        for qt in range(NT):
            pair, sc, m = ready
            w, b = (qt + 1) * P, qt % 2
            mx, sm = st[:, 32 + 4 * b:33 + 4 * b], st[:, 33 + 4 * b:34 + 4 * b]
            dve.run(v.tensor_tensor, sc[:, w - P:w], sc[:, w - P:w], k.c(K_CAUSAL), ALU.add, after=[m])
            dve.then(v.tensor_reduce, mx, sc[:, 0:w], AX.X, ALU.max, after=exp_read[b])
            dve.then(v.tensor_scalar_mul, mx, mx, -scale)
            e = act.run(s.activation, prob[b][:, 0:w], sc[:, 0:w], ACT.Exp, bias=mx, scale=scale, accum_out=sm,
                        after=[dve.last, *exp_read[b]])
            for x_ in pair:
                x_.release(e)
            rc = dve.run(v.reciprocal, sm, sm, after=[e])
            if qt + 1 < NT:
                ready = scores(qt + 1)
            for lo in range(0, qt + 1, 4):
                hi = min(lo + 4, qt + 1)
                bank = k.bank()
                t = k.turn([(bank.ap[:, (j - lo) * P:(j - lo + 1) * P], prob[b][:, j * P:(j + 1) * P]) for j in range(lo, hi)], after=[e])
                dst = probT[b][:, lo:hi, :].rearrange("p a n -> p (a n)")
                if lo == 0:
                    c = dve.run(v.tensor_copy, dst, bank.ap[:, 0:(hi - lo) * P], after=[t, *pv_read[b]])
                else:
                    c = act.run(s.activation, dst, bank.ap[:, 0:(hi - lo) * P], ACT.Copy, after=[t, *pv_read[b]])
                bank.release(c)
                pe.wait(c)
            bank = k.bank()
            m = k.product(bank.ap[:, 0:MV], [(probT[b][:, j, :], k.val[:, j, bass.ds(h * MV, MV)]) for j in range(qt + 1)])
            ot = act.run(s.activation, out[b], bank.ap[:, 0:MV], ACT.Copy, scale=sm, after=[m, rc, *sent[b]])
            bank.release(ot)
            sent[b] = [k.channel(f"att_out{b}").start(g.sp, d["mixed"][qt * P:(qt + 1) * P, bass.ds(512 + h * MV, MV)], out[b],
                                                      after=[ot])]
            pv_read[b], exp_read[b] = [m], [t, ot, dve.last]
        g.mark("q_read", pe.last)
        for n in range(2):
            g.mark(f"att_out{n}", *sent[n])
            g.mark(f"probT_read{n}", *pv_read[n])
            g.mark(f"prob_read{n}", *exp_read[n])
    g.join(k.channel("att_out0"), k.channel("att_out1"))


def output_and_norm(k, layer):
    g, nc, d = k.g, k.g.nc, k.dram
    dve, act, pe, v, s = g.dve, g.act, g.pe, nc.vector, nc.scalar
    A = Area(k.arena)
    x, hT, h_hi = A.take(NT, D), A.take(KC, S), k.rounded(A.take(KC, S))
    h_lo = k.rounded(hT)
    w = A.take(KC, D)
    mixed, mT, xn, tmp = A.take(D), A.take(KC, P), A.take(D), A.take(D)
    came_w = k.channel("w_out_in").start(g.act, w, d["w_out"][layer].rearrange("(k p) n -> p k n", p=P))
    came_x = k.channel("x_all_in").start(g.act, x, d["x_res"][0:S].rearrange("(t p) n -> p t n", p=P), after=k.x_ready)
    pe.wait(came_w)
    dve.wait(came_x)
    act.wait(came_x)
    made = [k.channel(n).count.now() for n in ("o_out", "att_out0", "att_out1")]
    sp = g.sp

    def load(i, after):
        return k.channel("mixed_in").start(sp, mixed, d["mixed"][at(i, P), :], after=after)

    def turn_mixed(loaded, after=()):
        for half in range(2):
            bank = k.bank()
            tt = k.turn([(bank.ap[:, j * P:(j + 1) * P], mixed[:, (4 * half + j) * P:(4 * half + j + 1) * P]) for j in range(4)],
                        after=[loaded])
            e = act.run(s.activation, mT[:, 4 * half:4 * half + 4, :].rearrange("p a b -> p (a b)"), bank.ap, ACT.Copy,
                        after=[tt, *after])
            bank.release(e)
        return tt, e

    def residual(i, after=()):
        xt = x[:, at(i), :].rearrange("p a n -> p (a n)")
        for half in range(2):
            bank = k.bank()
            m = k.product(bank.ap, [(mT[:, c, :], w[:, c, half * 512:(half + 1) * 512]) for c in range(KC)], after=after)
            cols = slice(half * 512, (half + 1) * 512)
            dve.run(v.tensor_tensor, tmp[:, cols], bank.ap, k.gate[:, 0, cols], ALU.mult, after=[m])
            bank.release(dve.last)
            xs = dve.then(v.tensor_tensor, xt[:, cols], xt[:, cols], tmp[:, cols], ALU.add)
        return m, xs

    def norm(i, xs, after=()):
        return normed(k, x[:, at(i), :].rearrange("p a n -> p (a n)"), xn, k.stat, after=[xs, *after])

    def store(i, n_):
        tt, made = turned_in(k, xn, lambda c: hT[:, c, at(i, P)], 1, after=[n_] if n_ else g.before("normed"))
        here = (slice(None), slice(None), at(i, P))
        hi = act.run(s.activation, h_hi[here], hT[here], ACT.Copy, after=made)
        dve.run(v.tensor_tensor, h_lo[here], hT[here], h_hi[here].bitcast(F32), ALU.subtract, after=[hi])
        return tt

    tt, mT_made = turn_mixed(load(0, made))
    loaded = load(1, [tt])
    m, xs = residual(0, [mT_made])
    n_ = norm(0, xs)
    tt, mT_made = turn_mixed(loaded, [m])
    pe.wait(mT_made, n_)
    sp.wait(tt)
    with g.loop("outs", NT - 2) as t:
        loaded = load(t + 2, g.before("mixed_read"))
        m, xs = residual(t + 1, g.before("mT_made"))
        tt, mT_made = turn_mixed(loaded, [m])
        g.mark("mixed_read", tt)
        g.mark("mT_made", mT_made)
        tt = store(t, None)
        g.mark("normed", norm(t + 1, xs, [tt]))
    n_ = dve.last
    m, xs = residual(NT - 1, [act.last])
    tt = store(NT - 2, n_)
    store(NT - 1, norm(NT - 1, xs, [tt]))
    g.join()


def feed_forward(k, layer):
    g, nc, d = k.g, k.g.nc, k.dram
    dve, act, pe, pool, v, s, gp = g.dve, g.act, g.pe, g.pool, nc.vector, nc.scalar, nc.gpsimd
    A = Area(k.arena)
    x, h_lo, h_hi = A.take(NT, D), A.take(KC, S), A.take(KC, S)
    h_lo, h_hi = k.rounded(h_lo), k.rounded(h_hi)
    u, u_hi = [A.take(2, S) for _ in range(2)], [k.rounded(A.take(2, S)) for _ in range(2)]
    u_lo = [k.rounded(b) for b in u]
    up_hi, down_hi = k.rounded(A.take(KC, 256)), k.rounded(A.take(2, D))
    wu = d["w_mlp_up"][layer].rearrange("(k p) n -> p k n", p=P)
    wd = d["w_mlp_down"][layer].rearrange("(c k p) n -> c p k n", p=P, k=2)
    chunks = D_FF // 256
    u_made, u_read = [[], []], [[], []]
    up_read, down_read = [], []

    def load_up(n):
        slot, w, came = k.load_weights(wu[:, :, n * 256:n * 256 + 256] if isinstance(n, int) else wu[:, :, bass.ds(n * 256, 256)],
                                       (KC, 256))
        hi = act.run(s.activation, up_hi, w, ACT.Copy, after=[came, *up_read])
        lo = pool.run(gp.tensor_tensor, k.rounded(w), w, up_hi.bitcast(F32), ALU.subtract, after=[hi])
        return slot, k.rounded(w), lo

    def load_down(n):
        src = wd[n] if isinstance(n, int) else wd[bass.ds(n, 1)].rearrange("a p k n -> p (a k) n")
        slot, w, came = k.load_weights(src, (2, D))
        e = dve.run(v.tensor_tensor, w, w, spread(k.gate[:, 1:2, :], P, 2, D), ALU.mult, after=[came])
        hi = act.run(s.activation, down_hi, w, ACT.Copy, after=[e, *down_read])
        lo = dve.run(v.tensor_tensor, k.rounded(w), w, down_hi.bitcast(F32), ALU.subtract, after=[hi])
        return slot, k.rounded(w), lo

    def up(b, slot, lo_w, ready):
        pe.wait(ready)
        for blk in range(2):
            for tok in range(2):
                bank = k.bank()
                cols, wc = slice(tok * 512, (tok + 1) * 512), slice(blk * P, (blk + 1) * P)
                m = k.split_product(bank.ap, [(up_hi[:, c, wc], lo_w[:, c, wc], h_hi[:, c, cols], h_lo[:, c, cols]) for c in range(KC)])
                whole, lo, hi = u[b][:, blk, cols], u_lo[b][:, blk, cols], u_hi[b][:, blk, cols]
                r = act.run(s.activation, whole, bank.ap, ACT.Relu, after=[m, *u_read[b]])
                bank.release(r)
                act.then(s.activation, whole, whole, ACT.Square)
                e = act.then(s.activation, hi, whole, ACT.Copy)
                made = dve.run(v.tensor_tensor, lo, whole, hi.bitcast(F32), ALU.subtract, after=[e])
        slot.release(m)
        up_read[:] = [m]
        u_made[b] = [made]

    def down(b, slot, lo_w, ready):
        pe.wait(ready, *u_made[b])
        for t in range(NT):
            for n in range(2):
                bank = k.bank()
                cols, tok = slice(n * 512, (n + 1) * 512), slice(t * P, (t + 1) * P)
                m = k.split_product(bank.ap, [(u_hi[b][:, c, tok], u_lo[b][:, c, tok], down_hi[:, c, cols], lo_w[:, c, cols])
                                              for c in range(2)])
                dve.run(v.tensor_tensor, x[:, t, cols], x[:, t, cols], bank.ap, ALU.add, after=[m])
                bank.release(dve.last)
        slot.release(m)
        down_read[:] = [m]
        u_read[b] = [m]

    def step(n, b):
        w_up, w_down = load_up(n), load_down(n - 1)
        up(b, *w_up)
        down(1 - b, *w_down)

    up(0, *load_up(0))
    pe.wait(*u_made[0])
    act.wait(*up_read)
    with g.loop("ff", chunks // 2 - 1) as j:
        up_read[:], down_read[:] = g.before("up_read"), g.before("down_read")
        u_made[0], u_read[1] = g.before("u_made0"), g.before("u_read1")
        step(2 * j + 1, 1)
        step(2 * j + 2, 0)
        g.mark("up_read", *up_read)
        g.mark("down_read", *down_read)
        g.mark("u_made0", *u_made[0])
        g.mark("u_read1", *u_read[1])
    step(chunks - 1, 1)
    down(1, *load_down(chunks - 1))
    k.channel("x_out").start(g.act, d["x_res"][0:S].rearrange("(t p) n -> p t n", p=P), x, after=[dve.last])
    g.join(k.channel("x_out"))


class Area:

    def __init__(self, arena):
        self.arena, self.at = arena, 0

    def skip(self, n):
        self.at += n

    def take(self, *shape):
        n = int(np.prod(shape))
        view = self.arena[:, self.at:self.at + n]
        self.at += n
        assert self.at <= ARENA, self.at
        names = " ".join(f"d{i}" for i in range(len(shape)))
        if len(shape) > 1:
            view = view.rearrange(f"p ({names}) -> p {names}", **{f"d{i}": w for i, w in enumerate(shape) if i})
        return view


def program(nc, d, known):
    g = Prog(nc, known)
    k = Kit(g, d)
    setup(k)
    with g.loop("layers", DEPTH) as layer:
        k.x_ready = [k.x_stored, *g.before("x_stored")]
        modulation(k, layer)
        mixer_tiles(k, layer)
        attention(k)
        output_and_norm(k, layer)
        feed_forward(k, layer)
        g.mark("x_stored", k.channel("x_out").count.now())
    second(k)
    return g.found


_SCRATCH = {"x_res": (S + P, D), "q_all": (MH, P, S), "qpe_all": (MH, ROPE, S), "mixed": (S, D), **SCRATCH_2}


def _declare(nc, arrays, mybir_):
    d = {n: nc.dram_tensor(f"in_{n}", a.shape, mybir_.dt.from_np(a.dtype), kind="ExternalInput").ap() for n, a in arrays.items()}
    for n, shape in _SCRATCH.items():
        kind = I32 if n in INT_SCRATCH else F32
        d[n] = nc.dram_tensor(f"tmp_{n}", shape, kind, kind="Internal").ap()
    d["out"] = nc.dram_tensor("out", (1, S, D), F32, kind="ExternalOutput").ap()
    return d


def kernel(**inputs):
    import numpy as _np
    import concourse.bacc as _bacc
    from concourse import mybir as _mybir
    from concourse.bass_utils import run_bass_kernel_spmd as _run

    arrays = {n: _np.ascontiguousarray(a) for n, a in inputs.items()}
    arrays["const"] = constants()
    known = {}
    for _ in range(2):
        nc = _bacc.Bacc("TRN2", target_bir_lowering=False, num_devices=1)
        known = program(nc, _declare(nc, arrays, _mybir), known)
    r = _run(nc, [{f"in_{n}": a for n, a in arrays.items()}], core_ids=[0])
    return r.results[0]["out"]
```
